# Optimizing a Trainium2 kernel written in Bass

```python
import jax, jax.numpy as jnp
from jax import lax
import numpy as np
import math

D_MODEL = 1024
BATCH = 1
SEQ = 512
DEPTH = 2

GRID_W = 64
CTX_LEN = 256
N_EVEN = (DEPTH + 1) // 2
N_ODD = DEPTH // 2

MLA_HEADS = 8
MLA_Q_RANK = 384
MLA_KV_RANK = 256
MLA_NOPE = 64
MLA_ROPE = 32
MLA_V = 64
MLA_QK = MLA_NOPE + MLA_ROPE
GQA_HEADS = 8
GQA_KV_HEADS = 2
GQA_DIM = 64
EVEN_SPLITS = (MLA_Q_RANK, MLA_KV_RANK, MLA_ROPE, GQA_HEADS * GQA_DIM,
               GQA_KV_HEADS * GQA_DIM, GQA_KV_HEADS * GQA_DIM)
EVEN_IN = sum(EVEN_SPLITS)
EVEN_MIX = MLA_HEADS * MLA_V + GQA_HEADS * GQA_DIM
MLSTM_HEADS = 8
MLSTM_QK = 64
MLSTM_V = 128
MLSTM_CONV = 3
MLSTM_CHUNK = 64
ODD_SPLITS = (2 * MLSTM_HEADS * MLSTM_QK, MLSTM_HEADS * MLSTM_V, MLSTM_HEADS * MLSTM_V, 4 * MLSTM_HEADS)
ODD_IN = sum(ODD_SPLITS)
D_FF = 2816
FFN_CONV = 3

Q_BLOCK = 128
ROPE_THETA = 10000.0
EPS = 1e-6


def rmsnorm(x, g):
    xf = x.astype(jnp.float32)
    y = xf * lax.rsqrt(jnp.mean(xf * xf, axis=-1, keepdims=True) + EPS)
    return (y * g.astype(jnp.float32)).astype(x.dtype)

def modulate(h, shift, scale):
    return h * (1 + scale) + shift

def split_cols(p, sizes):
    return jnp.split(p, np.cumsum(sizes)[:-1].tolist(), axis=-1)

def dwconv(x, w, b):
    width, T = w.shape[0], x.shape[1]
    left = (width - 1) // 2
    xp = jnp.pad(x, ((0, 0), (left, width - 1 - left), (0, 0)))
    return sum(xp[:, j:j + T] * w[j] for j in range(width)) + b

def axial_rope_tables(n_tokens, rot_dim):
    rows = n_tokens // GRID_W
    row = jnp.repeat(jnp.arange(rows), GRID_W).astype(jnp.float32)
    col = jnp.tile(jnp.arange(GRID_W), rows).astype(jnp.float32)
    n_freq = rot_dim // 4
    inv = ROPE_THETA ** (-jnp.arange(n_freq, dtype=jnp.float32) / n_freq)
    a_r, a_c = row[:, None] * inv, col[:, None] * inv
    ang = jnp.concatenate([a_r, a_r, a_c, a_c], axis=-1)
    return jnp.cos(ang), jnp.sin(ang)

def apply_rope(x, cos, sin):
    a1, a2, b1, b2 = jnp.split(x, 4, axis=-1)
    rot = jnp.concatenate([-a2, a1, -b2, b1], axis=-1)
    shape = (1, x.shape[1]) + (1,) * (x.ndim - 3) + (x.shape[-1],)
    return x * cos.reshape(shape).astype(x.dtype) + rot * sin.reshape(shape).astype(x.dtype)

def attend(q, k, v):
    B, T, G, R, dk = q.shape
    nb = T // Q_BLOCK
    scale = dk ** -0.5
    qb = jnp.moveaxis(q.reshape(B, nb, Q_BLOCK, G, R, dk), 1, 0)

    def block(qi):
        s = jnp.einsum('bqgrd,bsgd->bgrqs', qi, k).astype(jnp.float32) * scale
        p = jax.nn.softmax(s, axis=-1).astype(v.dtype)
        return jnp.einsum('bgrqs,bsgd->bqgrd', p, v)

    out = lax.map(block, qb)
    return jnp.moveaxis(out, 0, 1).reshape(B, T, G, R, v.shape[-1])

def mla_q(cq, g_qa, w_qb, g_q, rope):
    B, T, _ = cq.shape
    q = jnp.dot(rmsnorm(cq, g_qa), w_qb).reshape(B, T, MLA_HEADS, MLA_QK)
    q = rmsnorm(q, g_q)
    if rope is not None:
        q = jnp.concatenate([q[..., :MLA_NOPE], apply_rope(q[..., MLA_NOPE:], *rope)], axis=-1)
    return q[:, :, :, None, :]

def mla_kv(ckv, k_rope, g_kva, w_kvb, g_k, rope):
    B, T, _ = ckv.shape
    kv = jnp.dot(rmsnorm(ckv, g_kva), w_kvb).reshape(B, T, MLA_HEADS, MLA_NOPE + MLA_V)
    k_nope, v = kv[..., :MLA_NOPE], kv[..., MLA_NOPE:]
    k_pe = jnp.broadcast_to(k_rope[:, :, None, :], (B, T, MLA_HEADS, MLA_ROPE))
    k = rmsnorm(jnp.concatenate([k_nope, k_pe], axis=-1), g_k)
    if rope is not None:
        k = jnp.concatenate([k[..., :MLA_NOPE], apply_rope(k[..., MLA_NOPE:], *rope)], axis=-1)
    return k, v

def gqa_q(q, g_q, rope):
    B, T, _ = q.shape
    q = rmsnorm(q.reshape(B, T, GQA_HEADS, GQA_DIM), g_q)
    if rope is not None:
        q = apply_rope(q, *rope)
    return q.reshape(B, T, GQA_KV_HEADS, GQA_HEADS // GQA_KV_HEADS, GQA_DIM)

def gqa_kv(k, v, g_k, rope):
    B, T, _ = k.shape
    k = rmsnorm(k.reshape(B, T, GQA_KV_HEADS, GQA_DIM), g_k)
    if rope is not None:
        k = apply_rope(k, *rope)
    return k, v.reshape(B, T, GQA_KV_HEADS, GQA_DIM)

def even_mixer(h_lat, h_ctx, w_in, g_qa, w_qb, g_kva, w_kvb, g_mq, g_mk, g_gq, g_gk, w_out,
               rope_mla, rope_gqa, need_ctx_out):
    cq_l, ckv_l, kr_l, gq_l, gk_l, gv_l = split_cols(jnp.dot(h_lat, w_in), EVEN_SPLITS)
    cq_c, ckv_c, kr_c, gq_c, gk_c, gv_c = split_cols(jnp.dot(h_ctx, w_in), EVEN_SPLITS)
    ka_c, va_c = mla_kv(ckv_c, kr_c, g_kva, w_kvb, g_mk, None)
    ka_l, va_l = mla_kv(ckv_l, kr_l, g_kva, w_kvb, g_mk, rope_mla)
    kb_c, vb_c = gqa_kv(gk_c, gv_c, g_gk, None)
    kb_l, vb_l = gqa_kv(gk_l, gv_l, g_gk, rope_gqa)
    ka, va = jnp.concatenate([ka_c, ka_l], axis=1), jnp.concatenate([va_c, va_l], axis=1)
    kb, vb = jnp.concatenate([kb_c, kb_l], axis=1), jnp.concatenate([vb_c, vb_l], axis=1)

    def merge(o_a, o_b):
        B, T = o_a.shape[:2]
        return jnp.dot(jnp.concatenate([o_a.reshape(B, T, -1), o_b.reshape(B, T, -1)], axis=-1), w_out)

    out_lat = merge(attend(mla_q(cq_l, g_qa, w_qb, g_mq, rope_mla), ka, va),
                    attend(gqa_q(gq_l, g_gq, rope_gqa), kb, vb))
    out_ctx = None
    if need_ctx_out:
        out_ctx = merge(attend(mla_q(cq_c, g_qa, w_qb, g_mq, None), ka_c, va_c),
                        attend(gqa_q(gq_c, g_gq, None), kb_c, vb_c))
    return out_lat, out_ctx

def mlstm_inputs(h, w_in, conv_w, conv_b, gate_b):
    B, T, _ = h.shape
    qk, v, o, g = split_cols(jnp.dot(h, w_in), ODD_SPLITS)
    q, k = jnp.split(jax.nn.silu(dwconv(qk, conv_w, conv_b)), 2, axis=-1)

    def heads(t, d):
        return jnp.swapaxes(t.reshape(B, T, MLSTM_HEADS, d), 1, 2).astype(jnp.float32)

    g = (g + gate_b).astype(jnp.float32).reshape(B, T, 4, MLSTM_HEADS)
    g = jnp.transpose(g, (2, 0, 3, 1))
    gates = (g[0], jax.nn.log_sigmoid(g[1]), g[2], jax.nn.log_sigmoid(g[3]))
    return heads(q, MLSTM_QK), heads(k, MLSTM_QK) * MLSTM_QK ** -0.5, heads(v, MLSTM_V), o, gates

def mlstm_state_update(state, k, v, log_i, b):
    C, n, m = state
    b_last = b[..., -1]
    a = b_last[..., None] - b + log_i
    m_new = jnp.maximum(b_last + m, jnp.max(a, axis=-1))
    decay = jnp.exp(b_last + m - m_new)
    w = jnp.exp(a - m_new[..., None])
    C_new = decay[..., None, None] * C + jnp.einsum('bhs,bhsv,bhsd->bhvd', w, v, k)
    n_new = decay[..., None] * n + jnp.einsum('bhs,bhsd->bhd', w, k)
    return (C_new, n_new, m_new)

def mlstm_chunkwise(q, k, v, log_i, log_f, state0):
    B, H, T, dk = q.shape
    dv = v.shape[-1]
    L = MLSTM_CHUNK
    nc = T // L
    lower = jnp.tril(jnp.ones((L, L), dtype=bool))

    def chunks(t):
        return jnp.moveaxis(t.reshape((B, H, nc, L) + t.shape[3:]), 2, 0)

    def step(state, inp):
        C, n, m = state
        qc, kc, vc, ic, fc = inp
        b = jnp.cumsum(fc, axis=-1)
        logw = jnp.where(lower, b[..., :, None] - b[..., None, :] + ic[..., None, :], -jnp.inf)
        log_inter = b + m[..., None]
        m_t = jnp.maximum(log_inter, jnp.max(logw, axis=-1))
        w_inter = jnp.exp(log_inter - m_t)
        s = jnp.einsum('bhtd,bhsd->bhts', qc, kc) * jnp.exp(logw - m_t[..., None])
        num = w_inter[..., None] * jnp.einsum('bhvd,bhtd->bhtv', C, qc) + jnp.einsum('bhts,bhsv->bhtv', s, vc)
        den = w_inter * jnp.einsum('bhd,bhtd->bht', n, qc) + jnp.sum(s, axis=-1)
        h = num / jnp.maximum(jnp.abs(den), jnp.exp(-m_t))[..., None]
        return mlstm_state_update(state, kc, vc, ic, b), h

    state, h = lax.scan(step, state0, (chunks(q), chunks(k), chunks(v), chunks(log_i), chunks(log_f)))
    return jnp.moveaxis(h, 0, 2).reshape(B, H, T, dv), state

def mlstm_direction(q_l, k_l, v_l, li_l, lf_l, q_c, k_c, v_c, li_c, lf_c, need_ctx_out):
    B, H = q_l.shape[:2]
    state0 = (jnp.zeros((B, H, MLSTM_V, MLSTM_QK), jnp.float32),
              jnp.zeros((B, H, MLSTM_QK), jnp.float32),
              jnp.zeros((B, H), jnp.float32))
    if need_ctx_out:
        h_c, state_c = mlstm_chunkwise(q_c, k_c, v_c, li_c, lf_c, state0)
    else:
        h_c = None
        state_c = mlstm_state_update(state0, k_c, v_c, li_c, jnp.cumsum(lf_c, axis=-1))
    h_l, _ = mlstm_chunkwise(q_l, k_l, v_l, li_l, lf_l, state_c)
    return h_l, h_c

def odd_mixer(h_lat, h_ctx, w_in, conv_w, conv_b, gate_b, out_g, w_out, need_ctx_out):
    q_l, k_l, v_l, o_l, g_l = mlstm_inputs(h_lat, w_in, conv_w, conv_b, gate_b)
    q_c, k_c, v_c, o_c, g_c = mlstm_inputs(h_ctx, w_in, conv_w, conv_b, gate_b)

    def rev(t):
        return jnp.flip(t, axis=2)

    hf_l, hf_c = mlstm_direction(q_l, k_l, v_l, g_l[0], g_l[1], q_c, k_c, v_c, g_c[0], g_c[1], need_ctx_out)
    hb_l, hb_c = mlstm_direction(rev(q_l), rev(k_l), rev(v_l), rev(g_l[2]), rev(g_l[3]),
                                 rev(q_c), rev(k_c), rev(v_c), rev(g_c[2]), rev(g_c[3]), need_ctx_out)

    def readout(hf, hb, o):
        h = jnp.swapaxes(hf + rev(hb), 1, 2)
        B, T = h.shape[:2]
        h = rmsnorm(h, out_g).reshape(B, T, -1).astype(o.dtype)
        return jnp.dot(h * jax.nn.sigmoid(o), w_out)

    out_lat = readout(hf_l, hb_l, o_l)
    out_ctx = readout(hf_c, hb_c, o_c) if need_ctx_out else None
    return out_lat, out_ctx

def conv_ffn(h, w_up, conv_w, conv_b, w_down):
    gate, val = jnp.split(jnp.dot(h, w_up), 2, axis=-1)
    return jnp.dot(jax.nn.silu(dwconv(gate, conv_w, conv_b)) * val, w_down)

def first_inputs(seed: int = 0) -> dict:
    key = jax.random.key(seed)
    keys = jax.random.split(key, 40)
    counter = iter(range(40))
    D = D_MODEL

    def nrm(shape, scale):
        return jax.random.normal(keys[next(counter)], shape, jnp.float32) * scale

    def gain(shape):
        return 1.0 + nrm(shape, 0.05)

    H = MLSTM_HEADS
    i_bias = nrm((N_ODD, 2, 1, H), 0.1)
    f_bias = jnp.linspace(3.0, 6.0, H, dtype=jnp.float32) + nrm((N_ODD, 2, 1, H), 0.1)
    ml_gate_b = jnp.concatenate([i_bias, f_bias], axis=2).reshape(N_ODD, 4 * H)
    return {
        'x': nrm((BATCH, SEQ, D), 1.0),
        'c': nrm((BATCH, D), 1.0),
        'ctx': nrm((BATCH, CTX_LEN, D), 1.0),
        'c_ctx': nrm((D,), 1.0),
        'ada_w': nrm((DEPTH, D, 6 * D), 0.5 * D ** -0.5),
        'ada_b': nrm((DEPTH, 6 * D), 0.02),
        'norm1_g': gain((DEPTH, D)),
        'norm2_g': gain((DEPTH, D)),
        'ffn_w_up': nrm((DEPTH, D, 2 * D_FF), D ** -0.5),
        'ffn_conv_w': nrm((DEPTH, FFN_CONV, D_FF), 0.5),
        'ffn_conv_b': nrm((DEPTH, D_FF), 0.02),
        'ffn_w_down': nrm((DEPTH, D_FF, D), D_FF ** -0.5),
        'att_w_in': nrm((N_EVEN, D, EVEN_IN), D ** -0.5),
        'mla_qa_g': gain((N_EVEN, MLA_Q_RANK)),
        'mla_w_qb': nrm((N_EVEN, MLA_Q_RANK, MLA_HEADS * MLA_QK), MLA_Q_RANK ** -0.5),
        'mla_kva_g': gain((N_EVEN, MLA_KV_RANK)),
        'mla_w_kvb': nrm((N_EVEN, MLA_KV_RANK, MLA_HEADS * (MLA_NOPE + MLA_V)), MLA_KV_RANK ** -0.5),
        'mla_q_g': gain((N_EVEN, MLA_QK)),
        'mla_k_g': gain((N_EVEN, MLA_QK)),
        'gqa_q_g': gain((N_EVEN, GQA_DIM)),
        'gqa_k_g': gain((N_EVEN, GQA_DIM)),
        'att_w_out': nrm((N_EVEN, EVEN_MIX, D), EVEN_MIX ** -0.5),
        'ml_w_in': nrm((N_ODD, D, ODD_IN), D ** -0.5),
        'ml_conv_w': nrm((N_ODD, MLSTM_CONV, 2 * H * MLSTM_QK), 0.5),
        'ml_conv_b': nrm((N_ODD, 2 * H * MLSTM_QK), 0.02),
        'ml_gate_b': ml_gate_b,
        'ml_out_g': gain((N_ODD, H, MLSTM_V)),
        'ml_w_out': nrm((N_ODD, H * MLSTM_V, D), (H * MLSTM_V) ** -0.5),
    }

def first_block(x, c, ctx, c_ctx, ada_w, ada_b, norm1_g, norm2_g, ffn_w_up, ffn_conv_w, ffn_conv_b,
              ffn_w_down, att_w_in, mla_qa_g, mla_w_qb, mla_kva_g, mla_w_kvb, mla_q_g, mla_k_g,
              gqa_q_g, gqa_k_g, att_w_out, ml_w_in, ml_conv_w, ml_conv_b, ml_gate_b, ml_out_g, ml_w_out):
    n_lat = x.shape[1]
    rope_mla = axial_rope_tables(n_lat, MLA_ROPE)
    rope_gqa = axial_rope_tables(n_lat, GQA_DIM)
    for layer in range(DEPTH):
        need_ctx_out = layer < DEPTH - 1
        j = layer // 2
        mod_lat = (jnp.dot(jax.nn.silu(c), ada_w[layer]) + ada_b[layer])[:, None, :]
        mod_ctx = jnp.dot(jax.nn.silu(c_ctx), ada_w[layer]) + ada_b[layer]
        sh1, sc1, gt1, sh2, sc2, gt2 = jnp.split(mod_lat, 6, axis=-1)
        csh1, csc1, cgt1, csh2, csc2, cgt2 = jnp.split(mod_ctx, 6, axis=-1)
        h_lat = modulate(rmsnorm(x, norm1_g[layer]), sh1, sc1)
        h_ctx = modulate(rmsnorm(ctx, norm1_g[layer]), csh1, csc1)
        if layer % 2 == 0:
            out_lat, out_ctx = even_mixer(h_lat, h_ctx, att_w_in[j], mla_qa_g[j], mla_w_qb[j], mla_kva_g[j],
                                          mla_w_kvb[j], mla_q_g[j], mla_k_g[j], gqa_q_g[j], gqa_k_g[j],
                                          att_w_out[j], rope_mla, rope_gqa, need_ctx_out)
        else:
            out_lat, out_ctx = odd_mixer(h_lat, h_ctx, ml_w_in[j], ml_conv_w[j], ml_conv_b[j], ml_gate_b[j],
                                         ml_out_g[j], ml_w_out[j], need_ctx_out)
        x = x + gt1 * out_lat
        x = x + gt2 * conv_ffn(modulate(rmsnorm(x, norm2_g[layer]), sh2, sc2),
                               ffn_w_up[layer], ffn_conv_w[layer], ffn_conv_b[layer], ffn_w_down[layer])
        if need_ctx_out:
            ctx = ctx + cgt1 * out_ctx
            ctx = ctx + cgt2 * conv_ffn(modulate(rmsnorm(ctx, norm2_g[layer]), csh2, csc2),
                                       ffn_w_up[layer], ffn_conv_w[layer], ffn_conv_b[layer], ffn_w_down[layer])
    return x


DEPTH_2 = 1

CHUNK = 64
HEAD_DIM = 64
A_HEADS = 4
A_LEFT_CHUNKS = 8
A_BAND = (A_LEFT_CHUNKS + 1) * CHUNK
REL_CLIP = 128
B_HEADS = 4
IDX_HEADS = 4
IDX_DIM = 64
TOPK_MAX = 256
C_WIDTH = 512
C_BLOCKS = 8
C_BLOCK_DIM = C_WIDTH // C_BLOCKS
C_CONV = 4
LRU_C = 8.0
N_BRANCH = 3
A_WIDTH = A_HEADS * HEAD_DIM
B_WIDTH = B_HEADS * HEAD_DIM
MIX_WIDTH = A_WIDTH + B_WIDTH + C_WIDTH
D_FF_2 = -(-8 * D_MODEL // (3 * 256)) * 256
IN_SPLITS = (A_WIDTH, A_WIDTH, A_WIDTH,
             B_WIDTH, B_WIDTH, B_WIDTH,
             IDX_HEADS * IDX_DIM, IDX_DIM, IDX_HEADS,
             C_WIDTH, C_WIDTH,
             N_BRANCH * D_MODEL)
D_IN = sum(IN_SPLITS)


def rms_norm(x, g):
    x32 = x.astype(jnp.float32)
    y = x32 * lax.rsqrt(jnp.mean(x32 * x32, axis=-1, keepdims=True) + EPS)
    return (y * g.astype(jnp.float32)).astype(x.dtype)

def rope_tables(seq):
    pos = jnp.arange(seq, dtype=jnp.float32)
    inv = 1.0 / (ROPE_THETA ** (jnp.arange(0, HEAD_DIM, 2, dtype=jnp.float32) / HEAD_DIM))
    ang = pos[:, None] * inv[None, :]
    ang = jnp.concatenate([ang, ang], axis=-1)
    return jnp.cos(ang), jnp.sin(ang)

def apply_rope_2(x, cos, sin):
    shape = (cos.shape[0],) + (1,) * (x.ndim - 3) + (cos.shape[1],)
    c, s = cos.reshape(shape), sin.reshape(shape)
    x32 = x.astype(jnp.float32)
    x1, x2 = jnp.split(x32, 2, axis=-1)
    rot = jnp.concatenate([-x2, x1], axis=-1)
    return (x32 * c + rot * s).astype(x.dtype)

def split_cols_2(z):
    offs, acc = [], 0
    for w in IN_SPLITS[:-1]:
        acc += w
        offs.append(acc)
    return jnp.split(z, offs, axis=-1)

def chunk_relpos_attention(q, k, v, rel_bias, rel_idx):
    b, s, h, d = q.shape
    n_c = s // CHUNK
    qc = q.reshape(b, n_c, CHUNK, h, d)
    pad = ((0, 0), (A_LEFT_CHUNKS, 0), (0, 0), (0, 0), (0, 0))
    kp = jnp.pad(k.reshape(b, n_c, CHUNK, h, d), pad)
    vp = jnp.pad(v.reshape(b, n_c, CHUNK, h, d), pad)
    kb = jnp.concatenate([kp[:, j:j + n_c] for j in range(A_LEFT_CHUNKS + 1)], axis=2)
    vb = jnp.concatenate([vp[:, j:j + n_c] for j in range(A_LEFT_CHUNKS + 1)], axis=2)
    sc = jnp.einsum('bcqhd,bckhd->bhcqk', qc, kb).astype(jnp.float32) * (d ** -0.5)
    bias = rel_bias.astype(jnp.float32)[:, rel_idx]
    sc = sc + bias[:, None]
    key_chunk = jnp.arange(n_c)[:, None] - A_LEFT_CHUNKS + jnp.arange(A_BAND)[None, :] // CHUNK
    valid = key_chunk >= 0
    sc = jnp.where(valid[None, None, :, None, :], sc, -jnp.inf)
    p = jax.nn.softmax(sc, axis=-1).astype(v.dtype)
    o = jnp.einsum('bhcqk,bckhd->bcqhd', p, vb)
    return o.reshape(b, s, h * d)

def indexer_sparse_attention(q, k, v, qi, ki, wi):
    b, s, h, d = q.shape
    topk = min(TOPK_MAX, s // 4)
    n_blk = s // Q_BLOCK
    key_chunk = jnp.arange(s) // CHUNK
    bidx = jnp.arange(b)[:, None, None]
    scale = d ** -0.5

    def to_blocks(t):
        return jnp.moveaxis(t.reshape((b, n_blk, Q_BLOCK) + t.shape[2:]), 1, 0)

    def block(args):
        blk, qb, qib, wib = args
        q_chunk = (blk * Q_BLOCK + jnp.arange(Q_BLOCK)) // CHUNK
        admissible = key_chunk[None, :] <= q_chunk[:, None]
        dots = jnp.einsum('bqhe,bse->bqhs', qib, ki).astype(jnp.float32)
        score = jnp.einsum('bqhs,bqh->bqs', jax.nn.relu(dots), wib.astype(jnp.float32))
        score = jnp.where(admissible[None], score, -jnp.inf)
        _, idx = lax.top_k(score, topk)
        sel_valid = (idx // CHUNK) <= q_chunk[None, :, None]
        ks = k[bidx, idx]
        vs = v[bidx, idx]
        att = jnp.einsum('bqhd,bqkhd->bhqk', qb, ks).astype(jnp.float32) * scale
        att = jnp.where(sel_valid[:, None], att, -jnp.inf)
        p = jax.nn.softmax(att, axis=-1).astype(v.dtype)
        return jnp.einsum('bhqk,bqkhd->bqhd', p, vs)

    out = lax.map(block, (jnp.arange(n_blk), to_blocks(q), to_blocks(qi), to_blocks(wi)))
    return jnp.moveaxis(out, 0, 1).reshape(b, s, h * d)

def rglru_branch(xc, yc, conv_w, conv_b, wa, ba, wx, bx, lam):
    b, s, c = xc.shape
    xp = jnp.pad(xc, ((0, 0), (C_CONV - 1, 0), (0, 0)))
    u = conv_b + sum(xp[:, j:j + s] * conv_w[j] for j in range(C_CONV))
    ub = u.reshape(b, s, C_BLOCKS, C_BLOCK_DIM)
    r = jax.nn.sigmoid(jnp.einsum('bsgi,gij->bsgj', ub, wa).reshape(b, s, c) + ba)
    i = jax.nn.sigmoid(jnp.einsum('bsgi,gij->bsgj', ub, wx).reshape(b, s, c) + bx)
    log_a = -LRU_C * r.astype(jnp.float32) * jax.nn.softplus(-lam.astype(jnp.float32))
    a = jnp.exp(log_a)
    gated_in = jnp.sqrt(-jnp.expm1(2.0 * log_a)) * (i * u).astype(jnp.float32)

    def combine(left, right):
        a1, b1 = left
        a2, b2 = right
        return a1 * a2, a2 * b1 + b2

    _, hs = lax.associative_scan(combine, (a, gated_in), axis=1)
    return hs.astype(xc.dtype) * jax.nn.gelu(yc)

def second_inputs(seed: int = 0) -> dict:
    key = jax.random.key(seed)
    ks = jax.random.split(key, 20)
    f32 = jnp.float32
    nrm = lambda k, shp: jax.random.normal(k, shp, f32)
    x = nrm(ks[0], (BATCH, SEQ, D_MODEL))
    g_mix = 1.0 + 0.02 * nrm(ks[1], (DEPTH_2, D_MODEL))
    w_in = nrm(ks[2], (DEPTH_2, D_MODEL, D_IN)) * D_MODEL ** -0.5
    qk_gain_a = 1.0 + 0.02 * nrm(ks[3], (DEPTH_2, 2, HEAD_DIM))
    rel_bias = 0.1 * nrm(ks[4], (DEPTH_2, A_HEADS, 2 * REL_CLIP + 1))
    qk_gain_b = 1.0 + 0.02 * nrm(ks[5], (DEPTH_2, 2, HEAD_DIM))
    g_idx_k = 1.0 + 0.02 * nrm(ks[6], (DEPTH_2, IDX_DIM))
    conv_w = nrm(ks[7], (DEPTH_2, C_CONV, C_WIDTH)) * C_CONV ** -0.5
    conv_b = 0.01 * nrm(ks[8], (DEPTH_2, C_WIDTH))
    lru_wa = nrm(ks[9], (DEPTH_2, C_BLOCKS, C_BLOCK_DIM, C_BLOCK_DIM)) * C_BLOCK_DIM ** -0.5
    lru_ba = 0.01 * nrm(ks[10], (DEPTH_2, C_WIDTH))
    lru_wx = nrm(ks[11], (DEPTH_2, C_BLOCKS, C_BLOCK_DIM, C_BLOCK_DIM)) * C_BLOCK_DIM ** -0.5
    lru_bx = 0.01 * nrm(ks[12], (DEPTH_2, C_WIDTH))
    a_c = jax.random.uniform(ks[13], (DEPTH_2, C_WIDTH), f32, 0.9, 0.999)
    a0 = a_c ** (1.0 / LRU_C)
    lru_lambda = jnp.log(a0) - jnp.log1p(-a0)
    b_gate = 0.01 * nrm(ks[14], (DEPTH_2, N_BRANCH * D_MODEL))
    row_scale = jnp.concatenate([jnp.full((A_WIDTH,), A_WIDTH ** -0.5, f32),
                                 jnp.full((B_WIDTH,), B_WIDTH ** -0.5, f32),
                                 jnp.full((C_WIDTH,), C_WIDTH ** -0.5, f32)])
    w_branch = nrm(ks[15], (DEPTH_2, MIX_WIDTH, D_MODEL)) * row_scale[None, :, None]
    w_out = nrm(ks[16], (DEPTH_2, D_MODEL, D_MODEL)) * D_MODEL ** -0.5
    g_ffn = 1.0 + 0.02 * nrm(ks[17], (DEPTH_2, D_MODEL))
    w_ffn_in = nrm(ks[18], (DEPTH_2, D_MODEL, 2 * D_FF_2)) * D_MODEL ** -0.5
    w_ffn_out = nrm(ks[19], (DEPTH_2, D_FF_2, D_MODEL)) * D_FF_2 ** -0.5
    return {"x": x, "g_mix": g_mix, "w_in": w_in, "qk_gain_a": qk_gain_a, "rel_bias": rel_bias,
            "qk_gain_b": qk_gain_b, "g_idx_k": g_idx_k, "conv_w": conv_w, "conv_b": conv_b,
            "lru_wa": lru_wa, "lru_ba": lru_ba, "lru_wx": lru_wx, "lru_bx": lru_bx,
            "lru_lambda": lru_lambda, "b_gate": b_gate, "w_branch": w_branch, "w_out": w_out,
            "g_ffn": g_ffn, "w_ffn_in": w_ffn_in, "w_ffn_out": w_ffn_out}

def second_block(x, g_mix, w_in, qk_gain_a, rel_bias, qk_gain_b, g_idx_k, conv_w, conv_b,
              lru_wa, lru_ba, lru_wx, lru_bx, lru_lambda, b_gate, w_branch, w_out,
              g_ffn, w_ffn_in, w_ffn_out):
    b, s, _ = x.shape
    cos, sin = rope_tables(s)
    q_in_band = A_LEFT_CHUNKS * CHUNK + jnp.arange(CHUNK)
    rel_idx = jnp.clip(q_in_band[:, None] - jnp.arange(A_BAND)[None, :], -REL_CLIP, REL_CLIP) + REL_CLIP
    for l in range(DEPTH_2):
        h = rms_norm(x, g_mix[l])
        z = h @ w_in[l]
        aq, ak, av, bq, bk, bv, iq, ik, iw, cx, cy, gt = split_cols_2(z)
        hd = lambda t, n: t.reshape(b, s, n, HEAD_DIM)
        y_a = chunk_relpos_attention(rms_norm(hd(aq, A_HEADS), qk_gain_a[l, 0]),
                                     rms_norm(hd(ak, A_HEADS), qk_gain_a[l, 1]),
                                     hd(av, A_HEADS), rel_bias[l], rel_idx)
        q_b = apply_rope_2(rms_norm(hd(bq, B_HEADS), qk_gain_b[l, 0]), cos, sin)
        k_b = apply_rope_2(rms_norm(hd(bk, B_HEADS), qk_gain_b[l, 1]), cos, sin)
        q_i = apply_rope_2(iq.reshape(b, s, IDX_HEADS, IDX_DIM), cos, sin)
        k_i = apply_rope_2(rms_norm(ik, g_idx_k[l]), cos, sin)
        w_i = iw * (IDX_HEADS ** -0.5 * IDX_DIM ** -0.5)
        y_b = indexer_sparse_attention(q_b, k_b, hd(bv, B_HEADS), q_i, k_i, w_i)
        y_c = rglru_branch(cx, cy, conv_w[l], conv_b[l], lru_wa[l], lru_ba[l],
                           lru_wx[l], lru_bx[l], lru_lambda[l])
        gates = jax.nn.sigmoid(gt + b_gate[l]).reshape(b, s, N_BRANCH, D_MODEL)
        wb = w_branch[l]
        merged = (gates[:, :, 0] * (y_a @ wb[:A_WIDTH])
                  + gates[:, :, 1] * (y_b @ wb[A_WIDTH:A_WIDTH + B_WIDTH])
                  + gates[:, :, 2] * (y_c @ wb[A_WIDTH + B_WIDTH:]))
        x = x + merged @ w_out[l]
        gu = rms_norm(x, g_ffn[l]) @ w_ffn_in[l]
        g_, u_ = jnp.split(gu, 2, axis=-1)
        x = x + (jax.nn.silu(g_) * u_) @ w_ffn_out[l]
    return x


def setup_inputs(seed=0):
    out = dict(first_inputs(seed))
    for name, value in second_inputs(seed + 1).items():
        if name != "x":
            out[name + "_2"] = value
    return out


def reference(
    x, c, ctx, c_ctx, ada_w, ada_b, norm1_g, norm2_g, ffn_w_up, ffn_conv_w, ffn_conv_b,
    ffn_w_down, att_w_in, mla_qa_g, mla_w_qb, mla_kva_g, mla_w_kvb, mla_q_g, mla_k_g, gqa_q_g,
    gqa_k_g, att_w_out, ml_w_in, ml_conv_w, ml_conv_b, ml_gate_b, ml_out_g, ml_w_out, g_mix_2,
    w_in_2, qk_gain_a_2, rel_bias_2, qk_gain_b_2, g_idx_k_2, conv_w_2, conv_b_2, lru_wa_2,
    lru_ba_2, lru_wx_2, lru_bx_2, lru_lambda_2, b_gate_2, w_branch_2, w_out_2, g_ffn_2,
    w_ffn_in_2, w_ffn_out_2,
):
    x = first_block(
        x, c, ctx, c_ctx, ada_w, ada_b, norm1_g, norm2_g, ffn_w_up, ffn_conv_w, ffn_conv_b,
        ffn_w_down, att_w_in, mla_qa_g, mla_w_qb, mla_kva_g, mla_w_kvb, mla_q_g, mla_k_g,
        gqa_q_g, gqa_k_g, att_w_out, ml_w_in, ml_conv_w, ml_conv_b, ml_gate_b, ml_out_g,
        ml_w_out,
    )
    return second_block(
        x, g_mix_2, w_in_2, qk_gain_a_2, rel_bias_2, qk_gain_b_2, g_idx_k_2, conv_w_2, conv_b_2,
        lru_wa_2, lru_ba_2, lru_wx_2, lru_bx_2, lru_lambda_2, b_gate_2, w_branch_2, w_out_2,
        g_ffn_2, w_ffn_in_2, w_ffn_out_2,
    )


_drawn_inputs = setup_inputs


def setup_inputs(seed=0):
    import zlib

    import numpy as np

    out = dict(_drawn_inputs(seed))
    spreads = {}
    factors = {'norm1_g': 3.468,
     'ffn_conv_b': 6.473,
     'mla_qa_g': 8.0,
     'mla_kva_g': 8.0,
     'mla_q_g': 8.0,
     'mla_k_g': 8.0,
     'gqa_q_g': 8.0,
     'gqa_k_g': 8.0,
     'ml_conv_b': 6.783,
     'ml_out_g': 4.331,
     'g_mix_2': 3.97,
     'qk_gain_a_2': 8.0,
     'rel_bias_2': 8.0,
     'qk_gain_b_2': 8.0,
     'g_idx_k_2': 7.298,
     'conv_b_2': 3.386,
     'lru_ba_2': 36.422,
     'lru_bx_2': 25.45,
     'b_gate_2': 22.596,
     'g_ffn_2': 4.125}
    for name, (base, spread) in spreads.items():
        noise = np.random.default_rng([zlib.crc32(name.encode()), seed]).standard_normal(out[name].shape)
        drawn = base * np.exp(spread * noise) if base else spread * noise
        out[name] = __import__('jax').numpy.asarray(drawn.astype(out[name].dtype))
    for name, factor in factors.items():
        out[name] = (out[name] * factor).astype(out[name].dtype)
    return out
```

```python
from contextlib import ExitStack, contextmanager

import numpy as np
import concourse.bass as bass
from concourse import mybir

F32 = mybir.dt.float32
ALU = mybir.AluOpType
ACT = mybir.ActivationFunctionType
AX = mybir.AxisListType

P = 128
D, KD = 1024, 8
LAT, CTX = 512, 256
ALL = LAT + CTX
D_FF, KF = 2816, 22
EPS = 1e-6
RING = 4
SLOT = KF * P
BIG = 1e30

VEC_ORDER = [
    ("norm1_0", 8), ("norm1_1", 8), ("norm2_0", 8), ("norm2_1", 8), ("ada_b0", 48), ("ada_b1", 48),
    ("silu_in", 16), ("fcw0", 66), ("fcb0", 22), ("fcw1", 66), ("fcb1", 22),
    ("qa_g", 3), ("kva_g", 2), ("mq_g", 1), ("mk_g", 1), ("gq_g", 1), ("gk_g", 1),
    ("mcw", 24), ("mcb", 8), ("gate_i", 1), ("gate_f", 1), ("out_g", 8),
    ("g_mix", 8), ("g_ffn", 8), ("aq_g", 1), ("ak_g", 1), ("bq_g", 1), ("bk_g", 1), ("ik_g", 1),
    ("ccw", 16), ("ccb", 4), ("ba", 4), ("bx", 4), ("lam", 4), ("b_gate", 24),
]
VEC, _n = {}, 0
for _name, _w in VEC_ORDER:
    VEC[_name] = (_n, _w)
    _n += _w
NVEC = _n


Q_GAINS = [("mq_g", 96), ("gq_g", 64), ("aq_g", 64), ("bq_g", 64)]


class Count:

    def __init__(self, sem):
        self.sem, self.base = sem, 0


class Chain:

    def __init__(self, engine, count):
        self.engine, self.count, self.n, self.turn = engine, count, 0, None

    def step(self, instruction):
        instruction.then_inc(self.count.sem, 1)
        self.n += 1

    def sync(self):
        if self.turn is None:
            self.engine.wait_ge(self.count.sem, self.count.base + self.n)
        else:
            i, per = self.turn
            self.engine.wait_ge(self.count.sem, i * per + (self.count.base + self.n))

    @contextmanager
    def loop(self, turns, per):
        with self.engine.Fori(0, turns) as i:
            start = self.n
            self.turn = (i, per)
            yield i
            assert self.n - start == per, (self.n - start, per)
            self.turn = None
        self.n = start + turns * per

    def close(self):
        self.count.base += self.n


def weight_plan():
    return [
        ("w_ada0", 24, 2048), ("w_att_lo", 3, 2048), ("w_att_gqa", 3, 2048), ("w_gv", 1, 1024),
        ("w_qb", 1, 2304), ("w_kvb", 1, 1536), ("w_va", 1, 1024), ("w_att_out", 4, 2048),
        ("w_up0", 22, 2048), ("w_down0", 8, 2816),
        ("w_ada1", 24, 2048), ("w_ml_gate", 1, 1024), ("w_ml_qk", 4, 2048), ("w_ml_o", 4, 2048),
        ("w_ml_v", 4, 2048), ("w_ml_out", 4, 2048), ("w_up1", 22, 2048), ("w_down1", 8, 2816),
        ("w2_heads", 6, 2048), ("w2_c", 4, 2048), ("w2_v", 2, 2048), ("w2_iw", 1, 32),
        ("w2_lru", 1, 1024), ("w2_merge", 16, 2048), ("w2_out", 4, 2048),
        ("w_up2", 22, 2048), ("w_down2", 8, 2816),
    ]


class Kernel:

    def __init__(self, nc, arrays, stack):
        self.nc, self.d, self.temps = nc, arrays, 0
        sem = lambda name: Count(stack.enter_context(nc.semaphore(name)))
        self.sb = lambda name, shape: stack.enter_context(nc.sbuf_tensor(name, shape, F32))
        self.w_ready = [sem(f"w_ready{s}") for s in range(RING)]
        self.w_used = sem("w_used")
        self.ring = self.sb("ring", [P, RING, SLOT])
        self.plan, n = {}, 0
        self.chunks = []
        for name, count, floats in weight_plan():
            self.plan[name] = (n, count, floats)
            self.chunks += [(name, c, floats) for c in range(count)]
            n += count
        self.loaded = sem("loaded")
        self.pe_a = sem("pe_a")
        self.pe_b = sem("pe_b")
        self.pe_c = sem("pe_c")
        self.pe_d = sem("pe_d")
        self.act_a = sem("act_a")
        self.act_b = sem("act_b")
        self.act_c = sem("act_c")
        self.dve_a = sem("dve_a")
        self.dve_b = sem("dve_b")
        self.dve_c = sem("dve_c")
        self.dve_d = sem("dve_d")
        self.dve_e = sem("dve_e")
        self.pool_a = sem("pool_a")
        self.stored = sem("stored")
        self.dve_chain = sem("dve_chain")
        self.act_chain = sem("act_chain")
        self.pool_chain = sem("pool_chain")
        self.free = [sem(f"psum_free{s}") for s in range(4)]
        self.pairs = [stack.enter_context(nc.psum_tensor(f"pair{i}", [P, 1024], F32)) for i in range(4)]
        self.xT = self.sb("xT", [P, KD, ALL])
        self.hT = self.sb("hT", [P, KD, ALL])
        self.vec = self.sb("vec", [P, NVEC])
        self.ident = self.sb("ident", [P, P])
        self.ones = self.sb("ones", [P, P])
        self.ones64 = self.sb("ones64", [P, P])
        self.cvec = self.sb("cvec", [P, KD, 2])
        self.mod = self.sb("mod", [P, 48, 2])
        self.eps = self.sb("eps", [P, 1])
        self.qgain = self.sb("qgain", [P, 4])
        self.coef = self.sb("coef", [P, 2, KD])
        self.rinv = self.sb("rinv", [P, ALL])

    def temp(self, name, shape):
        self.temps += 1
        return self.nc.sbuf_tensor(f"{name}_{self.temps}", shape, F32)

    def v(self, name, k=0, n=1, rows=P):
        at, _ = VEC[name]
        return self.vec[0:rows, at + k:at + k + n]

    def first(self, name):
        return self.plan[name][0]

    def slot(self, chunk, k, cols):
        return self.ring[:, chunk % RING, 0:k * cols].rearrange("p (k c) -> p k c", k=k)

    def wait_weights(self, pe, chunk):
        pe.wait_ge(self.w_ready[chunk % RING].sem, 16 * (chunk // RING + 1))

    def send(self, sp, chunk):
        name, c, floats = self.chunks[chunk]
        if chunk >= RING:
            sp.wait_ge(self.w_used.sem, chunk - RING + 1)
        sp.dma_start(self.ring[:, chunk % RING, 0:floats], self.d[name][c]).then_inc(
            self.w_ready[chunk % RING].sem, 16)

    def stream(self, sp, names):
        lo = self.first(names[0]) + RING
        n0, count, _ = self.plan[names[-1]]
        hi = min(n0 + count + RING, len(self.chunks))
        at = lo
        while at < hi:
            name, c, floats = self.chunks[at]
            run = min(self.plan[name][1] - c, hi - at)
            turns = run // RING
            if turns >= 2:
                with sp.Fori(0, turns) as i:
                    for s in range(RING):
                        sp.wait_ge(self.w_used.sem, i * RING + (at + s - RING + 1))
                        sp.dma_start(self.ring[:, (at + s) % RING, 0:floats],
                                     self.d[name][bass.ds(i * RING + (c + s), 1)].rearrange("o p f -> (o p) f")
                                     ).then_inc(self.w_ready[(at + s) % RING].sem, 16)
                at += turns * RING
            else:
                self.send(sp, at)
                at += 1


def spans(tokens):
    return [(0, LAT)] if tokens == LAT else [(0, LAT), (LAT, ALL)]



def load_stage(K):
    nc = K.nc
    with nc.Block() as block:
        @block.sync
        def _(sp):
            sp.dma_start(K.vec[:], K.d["vec"]).then_inc(K.loaded.sem, 16)
            for c in range(RING):
                K.send(sp, c)
            for t, name in ((K.ident, "ident"), (K.ones64, "ones64")):
                sp.dma_start(t[:], K.d[name]).then_inc(K.loaded.sem, 16)
            sp.dma_start(K.xT[:], K.d["xT"]).then_inc(K.loaded.sem, 16)
            sp.wait_ge(K.loaded.sem, 64)

        @block.vector
        def _(dve):
            nc.vector.memset(K.ones[:], 1.0)
            nc.vector.memset(K.eps[:], EPS)
            dve.wait_ge(K.loaded.sem, 64)
            for c, (name, dim) in enumerate(Q_GAINS):
                nc.vector.tensor_scalar(K.qgain[:, c:c + 1], K.v(name), float(dim) ** -0.5, None, ALU.mult)

        @block.scalar
        def _(act):
            act.wait_ge(K.loaded.sem, 64)
            nc.scalar.activation(K.cvec[:].rearrange("p k c -> p (k c)"), K.v("silu_in", 0, 16), ACT.Silu)
    K.loaded.base += 64


def reload_x_stage(K):
    with K.nc.Block() as block:
        @block.sync
        def _(sp):
            sp.dma_start(K.xT[:], K.d["xT"]).then_inc(K.loaded.sem, 16)
            sp.wait_ge(K.loaded.sem, K.loaded.base + 16)
    K.loaded.base += 16


def ada_stage(K, layer):
    nc = K.nc
    name = f"w_ada{layer}"
    first = K.first(name)
    acc = K.pairs[0]
    with nc.Block() as block:
        @block.sync
        def _(sp):
            K.stream(sp, [name])

        @block.tensor
        def _(pe):
            with pe.Fori(0, 24 // RING) as i:
                for s in range(RING):
                    g = first + s
                    pe.wait_ge(K.w_ready[g % RING].sem, i * 16 + 16 * (g // RING + 1))
                    w = K.slot(g, KD, 256)
                    for b in range(2):
                        for k in range(KD):
                            mm = nc.tensor.matmul(acc[:, bass.ds(i * 16 + (4 * s + 2 * b), 2)],
                                                  w[:, k, b * P:b * P + P], K.cvec[:, k, :],
                                                  start=k == 0, stop=k == KD - 1)
                    mm.then_inc(K.w_used.sem, 1)

        @block.vector
        def _(dve):
            dve.wait_ge(K.w_used.sem, first + 24)
            bias = K.v(f"ada_b{layer}", 0, 48)
            nc.vector.tensor_tensor(K.mod[:], acc[:, 0:96].rearrange("p (b c) -> p b c", c=2),
                                    bias.unsqueeze(2).broadcast_to([P, 48, 2]), ALU.add)


def norm_stage(K, src, dst, nt, tokens, gain, scale=None, shift=None):
    nc = K.nc
    parts = spans(tokens)
    stat = K.pairs[3]
    sq_ready, stat_used, std_ready, out_ready = K.act_a, K.pe_a, K.act_b, K.dve_a
    with ExitStack() as stack:
        sq = stack.enter_context(K.temp("sq", [P, 2, ALL]))
        block = stack.enter_context(nc.Block())

        @block.scalar
        def _(act):
            for k in range(nt):
                if k >= 2:
                    act.wait_ge(stat_used.sem, stat_used.base + k - 1)
                nc.scalar.activation(sq[:, k % 2, 0:tokens], src[:, k, 0:tokens], ACT.Square).then_inc(sq_ready.sem, 1)
            act.wait_ge(stat_used.sem, stat_used.base + nt)
            nc.scalar.activation(K.rinv[:, 0:tokens], stat[:, 0:tokens], ACT.Sqrt, bias=K.eps[:],
                                 scale=1.0 / (nt * P)).then_inc(std_ready.sem, 1)
            if shift is not None:
                for k in range(nt):
                    act.wait_ge(out_ready.sem, out_ready.base + k + 1)
                    for j, (a, b) in enumerate(parts):
                        nc.scalar.activation(dst[:, k, a:b], dst[:, k, a:b], ACT.Identity,
                                             bias=K.mod[:, shift * KD + k, j:j + 1])

        @block.tensor
        def _(pe):
            for k in range(nt):
                pe.wait_ge(sq_ready.sem, sq_ready.base + k + 1)
                for a, b in parts:
                    mm = nc.tensor.matmul(stat[:, a:b], K.ones[:], sq[:, k % 2, a:b], start=k == 0, stop=k == nt - 1)
                mm.then_inc(stat_used.sem, 1)

        @block.vector
        def _(dve):
            chain = Chain(dve, K.dve_chain)
            coef = K.coef
            for j in range(len(parts)):
                if scale is None:
                    chain.step(nc.vector.tensor_copy(coef[:, j, 0:nt], gain))
                else:
                    chain.step(nc.vector.scalar_tensor_tensor(
                        coef[:, j, 0:nt], K.mod[:, scale * KD:scale * KD + nt, j], 1.0, gain, ALU.add, ALU.mult))
            dve.wait_ge(std_ready.sem, std_ready.base + 1)
            chain.step(nc.vector.reciprocal(K.rinv[:, 0:tokens], K.rinv[:, 0:tokens]))
            chain.sync()
            for k in range(nt):
                for j, (a, b) in enumerate(parts):
                    op = nc.vector.scalar_tensor_tensor(dst[:, k, a:b], src[:, k, a:b], coef[:, j, k:k + 1],
                                                        K.rinv[:, a:b], ALU.mult, ALU.mult)
                op.then_inc(out_ready.sem, 1)
            chain.close()
    sq_ready.base += nt
    stat_used.base += nt
    std_ready.base += 1
    out_ready.base += nt


def project_stage(K, names, src, tokens, blocks, store):
    nc = K.nc
    first = K.first(names[0])
    parts = spans(tokens)
    filled, free = K.pe_a, K.free
    engines = [store(b)[0] for b in range(blocks)]

    with nc.Block() as block:
        @block.sync
        def _(sp):
            K.stream(sp, names)

        @block.tensor
        def _(pe):
            for b in range(blocks):
                g = first + b // 2
                if b % 2 == 0:
                    K.wait_weights(pe, g)
                if b >= 4:
                    pe.wait_ge(free[b % 4].sem, free[b % 4].base + b // 4)
                w = K.slot(g, KD, 256)
                for a, e in parts:
                    for k in range(KD):
                        mm = nc.tensor.matmul(K.pairs[b % 4][:, a:e], w[:, k, b % 2 * P:b % 2 * P + P],
                                              src[:, k, a:e], start=k == 0, stop=k == KD - 1)
                mm.then_inc(filled.sem, 1)
                if b % 2 == 1:
                    pe.wait_ge(filled.sem, filled.base + b + 1)
                    pe.sem_inc(K.w_used.sem, 1)

        @block.scalar
        def _(act):
            for b in range(blocks):
                if engines[b] == "act":
                    act.wait_ge(filled.sem, filled.base + b + 1)
                    store(b)[1](act, K.pairs[b % 4]).then_inc(free[b % 4].sem, 1)

        @block.vector
        def _(dve):
            chain = Chain(dve, K.dve_chain)
            for b in range(blocks):
                if engines[b] == "dve":
                    dve.wait_ge(filled.sem, filled.base + b + 1)
                    store(b)[1](chain, K.pairs[b % 4]).then_inc(free[b % 4].sem, 1)
            chain.close()
    filled.base += blocks
    for s in range(4):
        free[s].base += len(range(s, blocks, 4))


def residual_stage(K, name, src, kt, tokens, gate):
    nc = K.nc
    first = K.first(name)
    parts = spans(tokens)
    per = 1 if kt == KF else 2
    unroll = per * RING
    filled, free = K.pe_a, K.free
    with nc.Block() as block:
        @block.sync
        def _(sp):
            K.stream(sp, [name])

        @block.tensor
        def _(pe):
            with pe.Fori(0, KD // unroll) as i:
                for b in range(unroll):
                    g = first + b // per
                    if b % per == 0:
                        pe.wait_ge(K.w_ready[g % RING].sem, i * 16 + 16 * (g // RING + 1))
                    pe.wait_ge(free[b % 4].sem, i * (unroll // 4) + (free[b % 4].base + b // 4 + 1))
                    w = K.slot(g, kt, P * per)
                    for a, e in parts:
                        for k in range(kt):
                            mm = nc.tensor.matmul(K.pairs[b % 4][:, a:e], w[:, k, b % per * P:b % per * P + P],
                                                  src[:, k, a:e], start=k == 0, stop=k == kt - 1)
                    mm.then_inc(filled.sem, 1)
                    if b % per == per - 1:
                        pe.wait_ge(filled.sem, i * unroll + (filled.base + b + 1))
                        pe.sem_inc(K.w_used.sem, 1)

        @block.vector
        def _(dve):
            for s in range(4):
                dve.sem_inc(free[s].sem, 1)
            with dve.Fori(0, KD // unroll) as i:
                for b in range(unroll):
                    dve.wait_ge(filled.sem, i * unroll + (filled.base + b + 1))
                    for j, (a, e) in enumerate(parts):
                        x = K.xT[:, bass.ds(i * unroll + b, 1), a:e].rearrange("p o t -> p (o t)")
                        if gate is None:
                            op = nc.vector.tensor_tensor(x, K.pairs[b % 4][:, a:e], x, ALU.add)
                        else:
                            g = K.mod[:, bass.ds(i * unroll + (gate * KD + b), 1), j:j + 1].rearrange("p o t -> p (o t)")
                            op = nc.vector.scalar_tensor_tensor(x, K.pairs[b % 4][:, a:e], g, x, ALU.mult, ALU.add)
                    op.then_inc(free[b % 4].sem, 1)
    filled.base += KD
    for s in range(4):
        free[s].base += 1 + KD // 4


def ffn_up_stage(K, layer, tokens, hidden):
    nc = K.nc
    name = f"w_up{layer}"
    first = K.first(name)
    parts = spans(tokens)
    conv = layer < 2
    gate_done, value_done, tap_ready, silu_ready = K.pe_a, K.pe_b, K.act_a, K.act_b
    conv_ready, hidden_ready = K.dve_a, K.dve_b
    gate_read = conv_ready if conv else silu_ready
    groups, rest = divmod(KF, RING)
    with ExitStack() as stack:
        gate = stack.enter_context(K.temp("gate", [P, RING, ALL]))
        block = stack.enter_context(nc.Block())

        def turns(eng, body):
            with eng.Fori(0, groups) as i:
                for s in range(RING):
                    body(i, s)
            for s in range(rest):
                body(groups, s)

        @block.sync
        def _(sp):
            K.stream(sp, [name])

        @block.tensor
        def _(pe):
            def body(i, s):
                g = first + s
                pe.wait_ge(K.w_ready[g % RING].sem, i * 16 + 16 * (g // RING + 1))
                w = K.slot(g, KD, 256)
                for half, read, done in ((0, gate_read, gate_done), (1, hidden_ready, value_done)):
                    pe.wait_ge(read.sem, i * RING + (read.base + s + 1))
                    for a, e in parts:
                        for k in range(KD):
                            mm = nc.tensor.matmul(K.pairs[2 * (s % 2) + half][:, a:e], w[:, k, half * P:half * P + P],
                                                  K.hT[:, k, a:e], start=k == 0, stop=k == KD - 1)
                    mm.then_inc(done.sem, 1)
                pe.wait_ge(value_done.sem, i * RING + (value_done.base + s + 1))
                pe.sem_inc(K.w_used.sem, 1)
            turns(pe, body)

        @block.scalar
        def _(act):
            if not conv:
                act.sem_inc(silu_ready.sem, 2)

            def body(i, s):
                act.wait_ge(gate_done.sem, i * RING + (gate_done.base + s + 1))
                ps = K.pairs[2 * (s % 2)]
                if not conv:
                    nc.scalar.activation(gate[:, s, 0:tokens], ps[:, 0:tokens], ACT.Silu).then_inc(silu_ready.sem, 1)
                    return
                middle = K.vec[:, bass.ds(i * RING + (VEC[f"fcw{layer}"][0] + KF + s), 1)]
                bias = K.vec[:, bass.ds(i * RING + (VEC[f"fcb{layer}"][0] + s), 1)]
                nc.scalar.activation(gate[:, s, 0:tokens], ps[:, 0:tokens], ACT.Identity, bias=bias,
                                     scale=middle).then_inc(tap_ready.sem, 1)
                act.wait_ge(conv_ready.sem, i * RING + (conv_ready.base + s + 3))
                nc.scalar.activation(gate[:, s, 0:tokens], gate[:, s, 0:tokens], ACT.Silu).then_inc(silu_ready.sem, 1)
            turns(act, body)

        @block.vector
        def _(dve):
            dve.sem_inc(hidden_ready.sem, 2)
            if conv:
                dve.sem_inc(conv_ready.sem, 2)

            def body(i, s):
                ps = K.pairs[2 * (s % 2)]
                if conv:
                    at = VEC[f"fcw{layer}"][0]
                    before = K.vec[:, bass.ds(i * RING + (at + s), 1)]
                    after = K.vec[:, bass.ds(i * RING + (at + 2 * KF + s), 1)]
                    dve.wait_ge(tap_ready.sem, i * RING + (tap_ready.base + s + 1))
                    for a, e in parts:
                        op = nc.vector.scalar_tensor_tensor(gate[:, s, a + 1:e], ps[:, a:e - 1], before,
                                                            gate[:, s, a + 1:e], ALU.mult, ALU.add)
                    op.then_inc(K.dve_c.sem, 1)
                    dve.wait_ge(K.dve_c.sem, i * RING + (K.dve_c.base + s + 1))
                    for a, e in parts:
                        op = nc.vector.scalar_tensor_tensor(gate[:, s, a:e - 1], ps[:, a + 1:e], after,
                                                            gate[:, s, a:e - 1], ALU.mult, ALU.add)
                    op.then_inc(conv_ready.sem, 1)
                dve.wait_ge(silu_ready.sem, i * RING + (silu_ready.base + s + (1 if conv else 3)))
                dve.wait_ge(value_done.sem, i * RING + (value_done.base + s + 1))
                out = hidden[:, bass.ds(i * RING + s, 1), 0:tokens].rearrange("p o t -> p (o t)")
                nc.vector.tensor_tensor(out, gate[:, s, 0:tokens], K.pairs[2 * (s % 2) + 1][:, 0:tokens],
                                        ALU.mult).then_inc(hidden_ready.sem, 1)
            turns(dve, body)
    gate_done.base += KF
    value_done.base += KF
    hidden_ready.base += KF + 2
    if conv:
        tap_ready.base += KF
        conv_ready.base += KF + 2
        K.dve_c.base += KF
        silu_ready.base += KF
    else:
        silu_ready.base += KF + 2


def ffn(K, layer, tokens, gate):
    with K.temp("hidden", [P, KF, tokens]) as hidden:
        ffn_up_stage(K, layer, tokens, hidden)
        residual_stage(K, f"w_down{layer}", hidden, KF, tokens, gate)


def heads_stage(K, names, tiles, tokens, tables, rot):
    nc = K.nc
    parts = spans(tokens)
    n = len(tiles)
    raw_done, stat_done, rot_done = K.pe_a, K.pe_b, K.pe_c
    sq_ready, std_ready = K.act_a, K.act_b
    gained, normed, sin_ready = K.dve_a, K.dve_b, K.dve_c
    rotated = K.pool_a
    normal = [t["gain"] is not None for t in tiles]
    roped = [t["rope"] for t in tiles]
    upto = lambda flags, j: sum(flags[:j + 1])
    stat, rots = K.pairs[2], K.pairs[3]
    last_of = {t["chunk"]: j for j, t in enumerate(tiles)}
    with ExitStack() as stack:
        sb = lambda name, shape: stack.enter_context(K.temp(name, shape))
        sq, std = sb("sq", [P, ALL]), sb("std", [P, ALL])
        y0, y1 = sb("y0", [P, 2, ALL]), sb("y1", [P, 3, ALL])
        ys = sb("ys", [P, LAT])
        trig = sb("trig", [P, 2, LAT])
        rotm = sb("rotm", [P, P])
        block = stack.enter_context(nc.Block())

        @block.sync
        def _(sp):
            sp.dma_start(trig[:], K.d[tables]).then_inc(K.loaded.sem, 16)
            sp.dma_start(rotm[:], K.d[rot]).then_inc(K.loaded.sem, 16)
            K.stream(sp, names)

        @block.tensor
        def _(pe):
            for j in range(n + 2):
                if j < n:
                    t = tiles[j]
                    if j == 0 or tiles[j - 1]["chunk"] != t["chunk"]:
                        K.wait_weights(pe, t["chunk"])
                    if j >= 2:
                        pe.wait_ge(gained.sem, gained.base + j - 1)
                        if normal[j - 2]:
                            pe.wait_ge(sq_ready.sem, sq_ready.base + upto(normal, j - 2))
                    for a, e in parts:
                        for m, (lhs, rhs) in enumerate(t["mms"]):
                            mm = nc.tensor.matmul(K.pairs[j % 2][0:t["rows"], a:e], lhs, rhs(a, e),
                                                  start=m == 0, stop=m == len(t["mms"]) - 1)
                    mm.then_inc(raw_done.sem, 1)
                    if last_of[t["chunk"]] == j:
                        pe.wait_ge(raw_done.sem, raw_done.base + j + 1)
                        pe.sem_inc(K.w_used.sem, 1)
                if 1 <= j <= n and normal[j - 1]:
                    t, r = tiles[j - 1], tiles[j - 1]["rows"]
                    pe.wait_ge(sq_ready.sem, sq_ready.base + upto(normal, j - 1))
                    if upto(normal, j - 1) > 1:
                        pe.wait_ge(std_ready.sem, std_ready.base + upto(normal, j - 1) - 1)
                    for a, e in parts:
                        mm = nc.tensor.matmul(stat[0:r, a:e], t["sums"], sq[0:r, a:e], start=True, stop=True)
                    mm.then_inc(stat_done.sem, 1)
                if j >= 2 and roped[j - 2]:
                    t, r = tiles[j - 2], tiles[j - 2]["rows"]
                    if upto(roped, j - 2) == 1:
                        pe.wait_ge(K.loaded.sem, K.loaded.base + 32)
                    else:
                        pe.wait_ge(sin_ready.sem, sin_ready.base + upto(roped, j - 2) - 1)
                    pe.wait_ge(normed.sem, normed.base + j - 1)
                    nc.tensor.matmul(rots[0:r, 0:LAT], rotm[0:r, 0:r], y1[0:r, (j - 2) % 3, 0:LAT],
                                     start=True, stop=True).then_inc(rot_done.sem, 1)

        @block.scalar
        def _(act):
            for j in range(n + 1):
                if j < n and normal[j]:
                    r = tiles[j]["rows"]
                    act.wait_ge(gained.sem, gained.base + j + 1)
                    if upto(normal, j) > 1:
                        act.wait_ge(stat_done.sem, stat_done.base + upto(normal, j) - 1)
                    nc.scalar.activation(sq[0:r, 0:tokens], K.pairs[j % 2][0:r, 0:tokens],
                                         ACT.Square).then_inc(sq_ready.sem, 1)
                if j >= 1 and normal[j - 1]:
                    t, r = tiles[j - 1], tiles[j - 1]["rows"]
                    act.wait_ge(stat_done.sem, stat_done.base + upto(normal, j - 1))
                    if j >= 2:
                        act.wait_ge(normed.sem, normed.base + j - 1)
                    nc.scalar.activation(std[0:r, 0:tokens], stat[0:r, 0:tokens], ACT.Sqrt,
                                         bias=K.eps[0:r], scale=t["scale"]).then_inc(std_ready.sem, 1)

        @block.vector
        def _(dve):
            chain = Chain(dve, K.dve_chain)
            for j in range(n + 2):
                if j < n:
                    r = tiles[j]["rows"]
                    dve.wait_ge(raw_done.sem, raw_done.base + j + 1)
                    if j >= 2:
                        dve.wait_ge(normed.sem, normed.base + j - 1)
                    raw = K.pairs[j % 2][0:r, 0:tokens]
                    if normal[j]:
                        op = nc.vector.tensor_scalar(y0[0:r, j % 2, 0:tokens], raw, tiles[j]["gain"], None, ALU.mult)
                    else:
                        op = nc.vector.tensor_copy(y0[0:r, j % 2, 0:tokens], raw)
                    op.then_inc(gained.sem, 1)
                if 1 <= j <= n:
                    t, r, b = tiles[j - 1], tiles[j - 1]["rows"], (j - 1) % 3
                    if normal[j - 1]:
                        dve.wait_ge(std_ready.sem, std_ready.base + upto(normal, j - 1))
                        chain.step(nc.vector.reciprocal(std[0:r, 0:tokens], std[0:r, 0:tokens]))
                        chain.sync()
                    else:
                        dve.wait_ge(gained.sem, gained.base + j)
                    if j >= 4 and roped[j - 4]:
                        dve.wait_ge(rotated.sem, rotated.base + upto(roped, j - 4))
                    to = y1[0:r, b, 0:tokens] if t["rope"] else t["dst"]
                    if normal[j - 1]:
                        op = nc.vector.tensor_tensor(to, y0[0:r, (j - 1) % 2, 0:tokens], std[0:r, 0:tokens], ALU.mult)
                    else:
                        op = nc.vector.tensor_copy(to, y0[0:r, (j - 1) % 2, 0:tokens])
                    op.then_inc(normed.sem, 1)
                if j >= 2 and roped[j - 2]:
                    r = tiles[j - 2]["rows"]
                    dve.wait_ge(rot_done.sem, rot_done.base + upto(roped, j - 2))
                    if upto(roped, j - 2) > 1:
                        dve.wait_ge(rotated.sem, rotated.base + upto(roped, j - 2) - 1)
                    nc.vector.tensor_tensor(ys[0:r, :], rots[0:r, 0:LAT], trig[0:r, 1, :],
                                            ALU.mult).then_inc(sin_ready.sem, 1)
            chain.close()

        @block.gpsimd
        def _(pool):
            chain = Chain(pool, K.pool_chain)
            pool.wait_ge(K.loaded.sem, K.loaded.base + 32)
            for j in range(n):
                if not roped[j]:
                    continue
                t, r, b = tiles[j], tiles[j]["rows"], j % 3
                pool.wait_ge(normed.sem, normed.base + j + 1)
                if tokens > LAT:
                    chain.step(nc.gpsimd.tensor_copy(t["dst"][:, LAT:tokens], y1[0:r, b, LAT:tokens]))
                chain.step(nc.gpsimd.tensor_tensor(t["dst"][:, 0:LAT], y1[0:r, b, 0:LAT], trig[0:r, 0, :], ALU.mult))
                chain.sync()
                pool.wait_ge(sin_ready.sem, sin_ready.base + upto(roped, j))
                nc.gpsimd.tensor_tensor(t["dst"][:, 0:LAT], t["dst"][:, 0:LAT], ys[0:r, :],
                                        ALU.add).then_inc(rotated.sem, 1)
            chain.close()
    K.loaded.base += 32
    for c in (raw_done, gained, normed):
        c.base += n
    for c in (stat_done, sq_ready, std_ready):
        c.base += sum(normal)
    for c in (rot_done, sin_ready, rotated):
        c.base += sum(roped)


def token_major_stage(K, names, jobs, ones=None):
    nc = K.nc
    filled, free = K.pe_a, K.free
    with nc.Block() as block:
        @block.sync
        def _(sp):
            K.stream(sp, names)

        @block.tensor
        def _(pe):
            for j, (chunk, last, mms, cols, dst) in enumerate(jobs):
                if j == 0 or jobs[j - 1][0] != chunk:
                    K.wait_weights(pe, chunk)
                if j >= 4:
                    pe.wait_ge(free[j % 4].sem, free[j % 4].base + j // 4)
                for m, (lhs, rhs) in enumerate(mms):
                    mm = nc.tensor.matmul(K.pairs[j % 4][:, 0:cols], lhs, rhs, start=m == 0, stop=m == len(mms) - 1)
                mm.then_inc(filled.sem, 1)
                if last:
                    pe.wait_ge(filled.sem, filled.base + j + 1)
                    pe.sem_inc(K.w_used.sem, 1)

        def source(j):
            ps = K.pairs[j % 4][:, 0:jobs[j][3]]
            shape = jobs[j][4].shape
            return ps.rearrange("p (h c) -> p h c", h=shape[1]) if len(shape) == 3 else ps

        @block.scalar
        def _(act):
            for j in range(0, len(jobs), 2):
                act.wait_ge(filled.sem, filled.base + j + 1)
                nc.scalar.activation(jobs[j][4], source(j), ACT.Copy).then_inc(free[j % 4].sem, 1)

        @block.vector
        def _(dve):
            if ones is not None:
                nc.vector.memset(ones, 1.0)
            for j in range(1, len(jobs), 2):
                dve.wait_ge(filled.sem, filled.base + j + 1)
                nc.vector.tensor_copy(jobs[j][4], source(j)).then_inc(free[j % 4].sem, 1)
    filled.base += len(jobs)
    for s in range(4):
        free[s].base += len(range(s, len(jobs), 4))


def attention_stage(K, turns, steps_of, stage_q, bias_of=None):
    nc = K.nc
    scored, transposed, summed = K.pe_a, K.pe_b, K.pe_c
    maxed, copied, out_ready, biased = K.dve_a, K.dve_b, K.dve_c, K.dve_d
    exped, staged = K.act_a, K.pool_a
    probe = steps_of(0)
    n = len(probe)
    assert n % 4 == 0 or turns == 1
    with_bias = "bias" in probe[0]
    pt = K.pairs[2]
    with ExitStack() as stack:
        sb = lambda name, shape: stack.enter_context(K.temp(name, shape))
        width = max(s["nk"] for s in probe)
        prob, probT = sb("prob", [P, 2, width]), sb("probT", [P, 2, width])
        scores = sb("scores", [P, 2, width]) if with_bias else None
        stats = sb("stats", [P, 3, 4])
        block = stack.enter_context(nc.Block())

        def loop(eng, body):
            if turns == 1:
                body(0)
            else:
                with eng.Fori(0, turns) as i:
                    body(i)

        if stage_q is not None:
            @block.gpsimd
            def _(pool):
                pool.sem_inc(scored.sem, 1)

                def body(i):
                    pool.wait_ge(scored.sem, i * n + (scored.base + 1))
                    stage_q(pool, i).then_inc(staged.sem, 1)
                loop(pool, body)
        lead = 0 if stage_q is None else 1

        @block.tensor
        def _(pe):
            def body(i):
                steps = steps_of(i)
                if stage_q is not None:
                    pe.wait_ge(staged.sem, i + (staged.base + 1))
                for m in range(n + 2):
                    if m < n:
                        s = steps[m]
                        for at, rhs in s["keys"]:
                            mm = nc.tensor.matmul(K.pairs[m % 2][:, at:at + rhs.shape[-1]], s["q"], rhs,
                                                  start=True, stop=True)
                        mm.then_inc(scored.sem, 1)
                    if m >= 2:
                        j = m - 2
                        pe.wait_ge(copied.sem, i * n + (copied.base + j + 1))
                        tiles = steps[j]["v"]
                        for c, v in enumerate(tiles):
                            mm = nc.tensor.matmul(K.pairs[3][:, 512 * (j % 2):512 * (j % 2) + 64],
                                                  probT[:, j % 2, c * P:c * P + P], v,
                                                  start=c == 0, stop=c == len(tiles) - 1)
                        mm.then_inc(summed.sem, 1)
                    if 1 <= m <= n:
                        j = m - 1
                        pe.wait_ge(exped.sem, i * n + (exped.base + j + 1))
                        for c in range(steps[j]["nk"] // P):
                            mm = nc.tensor.transpose(pt[:, c * P:c * P + P], prob[:, j % 2, c * P:c * P + P], K.ident[:])
                        mm.then_inc(transposed.sem, 1)
            loop(pe, body)

        @block.scalar
        def _(act):
            def body(i):
                for m, s in enumerate(steps_of(i)):
                    act.wait_ge(maxed.sem, i * n + (maxed.base + m + 1))
                    lo = s["keys"][0][0]
                    src = scores[:, m % 2, 0:s["nk"]] if with_bias else K.pairs[m % 2][:, lo:lo + s["nk"]]
                    nc.scalar.activation(prob[:, m % 2, 0:s["nk"]], src, ACT.Exp, bias=stats[:, 0, m % 4:m % 4 + 1],
                                         accum_out=stats[:, 1, m % 4:m % 4 + 1]).then_inc(exped.sem, 1)
            loop(act, body)

        @block.vector
        def _(dve):
            chain = Chain(dve, K.dve_chain)

            def body(i):
                steps = steps_of(i)
                for m in range(n + 2):
                    if m < n:
                        s = steps[m]
                        dve.wait_ge(scored.sem, i * n + (scored.base + lead + m + 1))
                        lo = s["keys"][0][0]
                        src = K.pairs[m % 2][:, lo:lo + s["nk"]]
                        if with_bias:
                            to = scores[:, m % 2, 0:s["nk"]]
                            chain.step(nc.vector.tensor_tensor(to, src, s["bias"], ALU.add))
                            chain.sync()
                            src = to
                        nc.vector.tensor_reduce(stats[:, 0, m % 4:m % 4 + 1], src, AX.X, ALU.max,
                                                negate=True).then_inc(maxed.sem, 1)
                    if 1 <= m <= n:
                        j = m - 1
                        dve.wait_ge(transposed.sem, i * n + (transposed.base + j + 1))
                        nk = steps[j]["nk"]
                        nc.vector.tensor_copy(probT[:, j % 2, 0:nk], pt[:, 0:nk]).then_inc(copied.sem, 1)
                    if m >= 2:
                        j = m - 2
                        dve.wait_ge(summed.sem, i * n + (summed.base + j + 1))
                        chain.step(nc.vector.reciprocal(stats[:, 2, j % 4:j % 4 + 1], stats[:, 1, j % 4:j % 4 + 1]))
                        chain.sync()
                        nc.vector.tensor_scalar(steps[j]["out"], K.pairs[3][:, 512 * (j % 2):512 * (j % 2) + 64],
                                                stats[:, 2, j % 4:j % 4 + 1], None, ALU.mult).then_inc(out_ready.sem, 1)
            if turns == 1:
                body(0)
            else:
                with chain.loop(turns, n * (2 if with_bias else 1)) as i:
                    body(i)
            chain.close()
    for c in (transposed, summed, maxed, copied, out_ready, exped):
        c.base += n * turns
    scored.base += n * turns + lead
    if stage_q is not None:
        staged.base += turns


def untoken_stage(K, src, dst, tiles_k, tiles_t):
    nc = K.nc
    filled, free = K.pe_a, K.free
    width = tiles_t * P
    with nc.Block() as block:
        @block.tensor
        def _(pe):
            for k in range(tiles_k):
                if k >= 4:
                    pe.wait_ge(free[k % 4].sem, free[k % 4].base + k // 4)
                for t in range(tiles_t):
                    mm = nc.tensor.transpose(K.pairs[k % 4][:, t * P:t * P + P], src[:, t, k * P:k * P + P], K.ident[:])
                mm.then_inc(filled.sem, 1)

        @block.scalar
        def _(act):
            for k in range(0, tiles_k, 2):
                act.wait_ge(filled.sem, filled.base + k + 1)
                nc.scalar.activation(dst[:, k, 0:width], K.pairs[k % 4][:, 0:width], ACT.Copy).then_inc(free[k % 4].sem, 1)

        @block.vector
        def _(dve):
            for k in range(1, tiles_k, 2):
                dve.wait_ge(filled.sem, filled.base + k + 1)
                nc.vector.tensor_copy(dst[:, k, 0:width], K.pairs[k % 4][:, 0:width]).then_inc(free[k % 4].sem, 1)
    filled.base += tiles_k
    for s in range(4):
        free[s].base += len(range(s, tiles_k, 4))



def layer0(K):
    nc = K.nc
    ada_stage(K, 0)
    norm_stage(K, K.xT, K.hT, KD, ALL, K.v("norm1_0", 0, 8), scale=1, shift=0)
    with ExitStack() as outer:
        sb = lambda name, shape: outer.enter_context(K.temp(name, shape))
        kT = sb("kT", [96, 8, ALL])
        gqT, gkT = sb("gqT", [P, 4, ALL]), sb("gkT", [P, 2, ALL])
        val = sb("val", [P, 6, 640])
        qT = K.xT
        with K.temp("low", [P, 6, ALL]) as low:
            def store(b):
                if b % 2 == 0:
                    return "act", lambda act, ps: nc.scalar.activation(low[:, b, :], ps[:, 0:ALL], ACT.Copy)
                return "dve", lambda chain, ps: nc.vector.tensor_copy(low[:, b, :], ps[:, 0:ALL])
            project_stage(K, ["w_att_lo"], K.hT, ALL, 6, store)
            first = K.first("w_att_gqa")
            tiles = []
            for b in range(6):
                w = K.slot(first + b // 2, KD, 256)
                tiles.append(dict(
                    chunk=first + b // 2, rows=P, sums=K.ones64[:], scale=1 / 64, rope=True,
                    mms=[(w[:, k, b % 2 * P:b % 2 * P + P], lambda a, e, k=k: K.hT[:, k, a:e]) for k in range(KD)],
                    gain=K.qgain[:, 1:2] if b < 4 else K.v("gk_g"), dst=gqT[:, b, :] if b < 4 else gkT[:, b - 4, :]))
            heads_stage(K, ["w_att_gqa"], tiles, ALL, "trig_gqa", "rot_gqa")
            g = K.first("w_gv")
            token_major_stage(K, ["w_gv"], [
                (g, t == 5, [(K.hT[:, k, t * P:t * P + P], K.slot(g, KD, P)[:, k, :]) for k in range(KD)],
                 P, val[:, t, 512:640]) for t in range(6)])
            norm_stage(K, low, low, 3, ALL, K.v("qa_g", 0, 3))
            norm_stage(K, low[:, 3:5, :], low[:, 3:5, :], 2, ALL, K.v("kva_g", 0, 2))
            gq, gkv = K.first("w_qb"), K.first("w_kvb")
            tiles = []
            for h in range(8):
                tiles.append(dict(
                    chunk=gq, rows=96, sums=K.ones[0:96, 0:96], scale=1 / 96, rope=True, gain=K.qgain[0:96, 0:1],
                    mms=[(K.slot(gq, 3, 768)[:, k, h * 96:h * 96 + 96], lambda a, e, k=k: low[:, k, a:e]) for k in range(3)],
                    dst=qT[0:96, h, :]))
            for h in range(8):
                tiles.append(dict(
                    chunk=gkv, rows=96, sums=K.ones[0:96, 0:96], scale=1 / 96, rope=True, gain=K.v("mk_g", rows=96),
                    mms=[(K.slot(gkv, 2, 768)[:, k, h * 96:h * 96 + 96], lambda a, e, k=k: low[:, 3 + k, a:e])
                         for k in range(2)] + [(K.ident[:, 0:96], lambda a, e: low[:, 5, a:e])],
                    dst=kT[:, h, :]))
            heads_stage(K, ["w_qb", "w_kvb"], tiles, ALL, "trig_mla", "rot_mla")
            g = K.first("w_va")
            token_major_stage(K, ["w_va"], [
                (g, t == 5, [(low[:, 3 + k, t * P:t * P + P], K.slot(g, 2, 512)[:, k, :]) for k in range(2)],
                 512, val[:, t, 0:512]) for t in range(6)])
        mixed = K.hT[:].rearrange("p k t -> p (k t)").rearrange("p (t c) -> p t c", t=6)
        order = [0, 1, 2, 3, 4, 5]
        with K.temp("qs", [P, 2, ALL]) as qs, K.temp("ks", [P, ALL]) as ks:
            one = lambda ap: ap.rearrange("p o t -> p (o t)")

            def step(t, q, key, v, out):
                lat = t < 4
                return dict(q=q, nk=ALL if lat else CTX, out=out,
                            keys=[(0, key(0, LAT)), (LAT, key(LAT, ALL))] if lat else [(0, key(LAT, ALL))],
                            v=[v(c) for c in (range(6) if lat else range(4, 6))])

            def mla_steps(i):
                steps = []
                for b in range(2):
                    for t in order:
                        steps.append(step(
                            t, qs[0:96, b, t * P:t * P + P],
                            lambda a, e, b=b: one(kT[:, bass.ds(i * 2 + b, 1), a:e]),
                            lambda c, b=b: val[:, c, bass.ds(i * 128 + b * 64, 64)],
                            mixed[:, t, bass.ds(i * 128 + b * 64, 64)]))
                return steps

            def mla_stage(pool, i):
                return nc.gpsimd.tensor_copy(qs[0:96], qT[0:96, bass.ds(i * 2, 2), :])
            attention_stage(K, 4, mla_steps, mla_stage)

            def gqa_steps(i):
                steps = []
                for b in range(2):
                    for half in range(2):
                        r = slice(64 * half, 64 * half + 64)
                        for t in order:
                            steps.append(step(
                                t, qs[r, b, t * P:t * P + P],
                                lambda a, e, r=r: ks[r, a:e],
                                lambda c: val[:, c, bass.ds(i * 64 + 512, 64)],
                                mixed[:, t, bass.ds(i * 256 + (512 + b * 128 + half * 64), 64)]))
                return steps

            def gqa_stage(pool, i):
                nc.gpsimd.tensor_copy(ks[:], one(gkT[:, bass.ds(i, 1), :]))
                return nc.gpsimd.tensor_copy(qs[:], gqT[:, bass.ds(i * 2, 2), :])
            attention_stage(K, 2, gqa_steps, gqa_stage)
    with K.temp("mixT", [P, KD, ALL]) as mixT:
        untoken_stage(K, mixed, mixT, KD, 6)
        reload_x_stage(K)
        residual_stage(K, "w_att_out", mixT, KD, ALL, 2)
    norm_stage(K, K.xT, K.hT, KD, ALL, K.v("norm2_0", 0, 8), scale=4, shift=3)
    ffn(K, 0, ALL, 5)



def gate_stage(K, keysT, floorT, top):
    nc = K.nc
    g = K.first("w_ml_gate")
    w = K.slot(g, KD, P)
    R = 64
    with ExitStack() as stack:
        sb = lambda name, shape: stack.enter_context(K.temp(name, shape))
        gi, gx, soft, run = (sb(n, [R, ALL]) for n in ("gi", "gx", "soft", "run"))
        zero, high = sb("zero", [R, ALL]), sb("high", [R, ALL])
        block = stack.enter_context(nc.Block())

        @block.sync
        def _(sp):
            K.stream(sp, ["w_ml_gate"])

        @block.tensor
        def _(pe):
            K.wait_weights(pe, g)
            for half in range(2):
                for a, e in spans(ALL):
                    for k in range(KD):
                        mm = nc.tensor.matmul(K.pairs[half][0:R, a:e], w[:, k, half * R:half * R + R],
                                              K.hT[:, k, a:e], start=k == 0, stop=k == KD - 1)
            mm.then_inc(K.pe_a.sem, 1)
            pe.wait_ge(K.pe_a.sem, K.pe_a.base + 1)
            pe.sem_inc(K.w_used.sem, 1)
            pe.wait_ge(K.dve_b.sem, K.dve_b.base + 1)
            for t in range(6):
                mm = nc.tensor.transpose(K.pairs[2][:, t * R:t * R + R], gi[:, t * P:t * P + P], K.ident[0:R, 0:R])
            mm.then_inc(K.pe_b.sem, 1)
            pe.wait_ge(K.act_b.sem, K.act_b.base + 1)
            for t in range(4):
                mm = nc.tensor.transpose(K.pairs[3][:, t * R:t * R + R], soft[:, t * P:t * P + P], K.ident[0:R, 0:R])
            mm.then_inc(K.pe_b.sem, 1)

        @block.scalar
        def _(act):
            chain = Chain(act, K.act_chain)
            act.wait_ge(K.dve_a.sem, K.dve_a.base + 1)
            chain.step(nc.scalar.activation(soft[:], gx[:], ACT.Abs))
            chain.sync()
            chain.step(nc.scalar.activation(soft[:], soft[:], ACT.Exp, scale=-1.0))
            chain.sync()
            nc.scalar.activation(soft[:], soft[:], ACT.Ln, bias=K.ones[0:R, 0:1]).then_inc(K.act_a.sem, 1)
            act.wait_ge(K.dve_c.sem, K.dve_c.base + 1)
            nc.scalar.activation(soft[:, 0:LAT], gx[:, 0:LAT], ACT.Exp, scale=-1.0).then_inc(K.act_b.sem, 1)
            chain.close()

        @block.vector
        def _(dve):
            chain = Chain(dve, K.dve_chain)
            chain.step(nc.vector.memset(zero[:], 0.0))
            dve.wait_ge(K.pe_a.sem, K.pe_a.base + 1)
            chain.step(nc.vector.tensor_scalar(gi[:], K.pairs[0][0:R, 0:ALL], K.v("gate_i", rows=R), None, ALU.add))
            nc.vector.tensor_scalar(gx[:], K.pairs[1][0:R, 0:ALL], K.v("gate_f", rows=R), None,
                                    ALU.add).then_inc(K.dve_a.sem, 1)
            dve.wait_ge(K.act_a.sem, K.act_a.base + 1)
            chain.step(nc.vector.scalar_tensor_tensor(gx[:], gx[:], 0.0, soft[:], ALU.min, ALU.subtract))
            chain.sync()

            def scan(out, data, op):
                for r, rev in ((slice(0, 32), 1), (slice(32, 64), -1)):
                    part = lambda x, a, e: x[r, a:e] if rev == 1 else x[r, a:e][:, ::-1]
                    chain.step(nc.vector.tensor_tensor_scan(part(out, LAT, ALL), part(zero, LAT, ALL),
                                                            part(data, LAT, ALL), 0.0, ALU.add, op))
                chain.sync()
                for r, rev, last in ((slice(0, 32), 1, ALL - 1), (slice(32, 64), -1, LAT)):
                    part = lambda x, a, e: x[r, a:e] if rev == 1 else x[r, a:e][:, ::-1]
                    chain.step(nc.vector.tensor_tensor_scan(part(out, 0, LAT), part(zero, 0, LAT), part(data, 0, LAT),
                                                            out[r, last:last + 1], ALU.add, op))
                chain.sync()

            scan(run, gx, ALU.add)
            nc.vector.tensor_tensor(gi[:], gi[:], run[:], ALU.subtract).then_inc(K.dve_b.sem, 1)
            dve.wait_ge(K.dve_b.sem, K.dve_b.base + 1)
            scan(high, gi, ALU.max)
            chain.step(nc.vector.tensor_copy(top[:], high[:, 0:LAT]))
            nc.vector.tensor_tensor(gx[:, 0:LAT], high[:, 0:LAT], run[:, 0:LAT], ALU.add).then_inc(K.dve_c.sem, 1)
            dve.wait_ge(K.pe_b.sem, K.pe_b.base + 1)
            nc.vector.tensor_copy(keysT[:].rearrange("p t c -> p (t c)"), K.pairs[2][:, 0:6 * R])
            dve.wait_ge(K.pe_b.sem, K.pe_b.base + 2)
            nc.vector.tensor_copy(floorT[:].rearrange("p t c -> p (t c)"), K.pairs[3][:, 0:4 * R])
            chain.close()
    for c, n in ((K.pe_a, 1), (K.pe_b, 2), (K.dve_a, 1), (K.dve_b, 1), (K.dve_c, 1), (K.act_a, 1), (K.act_b, 1)):
        c.base += n


def conv_qk_stage(K, qT, kT):
    nc = K.nc
    first = K.first("w_ml_qk")
    done, tap, silu, conved = K.pe_a, K.act_a, K.act_b, K.dve_a
    cw, cb = VEC["mcw"][0], VEC["mcb"][0]
    parts_of = lambda b: [(0, LAT)] if b < 4 else spans(ALL)
    with ExitStack() as stack:
        buf = stack.enter_context(K.temp("buf", [P, 2, ALL]))
        block = stack.enter_context(nc.Block())

        @block.sync
        def _(sp):
            K.stream(sp, ["w_ml_qk"])

        @block.tensor
        def _(pe):
            for b in range(8):
                g = first + b // 2
                if b % 2 == 0:
                    K.wait_weights(pe, g)
                if b >= 4:
                    pe.wait_ge(conved.sem, conved.base + b - 3)
                for a, e in parts_of(b):
                    for k in range(KD):
                        mm = nc.tensor.matmul(K.pairs[b % 4][:, a:e], K.slot(g, KD, 256)[:, k, b % 2 * P:b % 2 * P + P],
                                              K.hT[:, k, a:e], start=k == 0, stop=k == KD - 1)
                mm.then_inc(done.sem, 1)
                if b % 2 == 1:
                    pe.wait_ge(done.sem, done.base + b + 1)
                    pe.sem_inc(K.w_used.sem, 1)

        @block.scalar
        def _(act):
            for b in range(8):
                n = parts_of(b)[-1][1]
                act.wait_ge(done.sem, done.base + b + 1)
                if b >= 2:
                    act.wait_ge(silu.sem, silu.base + b - 1)
                nc.scalar.activation(buf[:, b % 2, 0:n], K.pairs[b % 4][:, 0:n], ACT.Identity,
                                     bias=K.vec[:, cb + b:cb + b + 1],
                                     scale=K.vec[:, cw + 8 + b:cw + 9 + b]).then_inc(tap.sem, 1)
                act.wait_ge(conved.sem, conved.base + b + 1)
                dst = qT[:, b, :] if b < 4 else kT[:, b - 4, :]
                nc.scalar.activation(dst, buf[:, b % 2, 0:n], ACT.Silu).then_inc(silu.sem, 1)

        @block.vector
        def _(dve):
            chain = Chain(dve, K.dve_chain)
            for b in range(8):
                dve.wait_ge(tap.sem, tap.base + b + 1)
                ps = K.pairs[b % 4]
                for a, e in parts_of(b):
                    chain.step(nc.vector.scalar_tensor_tensor(
                        buf[:, b % 2, a + 1:e], ps[:, a:e - 1], K.vec[:, cw + b:cw + b + 1],
                        buf[:, b % 2, a + 1:e], ALU.mult, ALU.add))
                chain.sync()
                for a, e in parts_of(b):
                    op = nc.vector.scalar_tensor_tensor(
                        buf[:, b % 2, a:e - 1], ps[:, a + 1:e], K.vec[:, cw + 16 + b:cw + 17 + b],
                        buf[:, b % 2, a:e - 1], ALU.mult, ALU.add)
                op.then_inc(conved.sem, 1)
            chain.close()
    for c in (done, tap, silu, conved):
        c.base += 8


def mlstm_stage(K, qT, kT, keysT, floorT, top, val, sig, yT):
    nc = K.nc
    spread, scored, summed, turned = K.pe_a, K.pe_b, K.pe_c, K.pe_d
    weighed, rooted = K.act_a, K.act_b
    mixed, read, normed, diag_ready, out_ready = K.dve_a, K.dve_b, K.dve_c, K.dve_d, K.dve_e
    staged = K.pool_a
    order = [4, 5, 0, 1, 2, 3]
    one = lambda ap: ap.rearrange("p o t -> p (o t)")
    beyond = lambda s, d: (0, LAT) if s >= 4 else (((s + 1) * P, LAT) if d == 0 else (0, s * P))
    with ExitStack() as stack:
        sb = lambda name, shape: stack.enter_context(K.temp(name, shape))
        kS, qS, hot = sb("kS", [P, ALL]), sb("qS", [P, LAT]), sb("hot", [64, 4])
        diag = sb("diag", [P, 2, 4, P])
        wgt = sb("wgt", [P, 2, 2, LAT])
        prob = sb("prob", [P, 2, 6, LAT])
        hs = sb("hs", [P, 4, P])
        hn, junk = K.rinv[:, P:5 * P].rearrange("p (t c) -> p t c", t=4), K.rinv[:, 0:P]
        den, ss = sb("den", [P, 2, 2]), sb("ss", [P, 4])
        causal = sb("causal", [P, 2, P])
        block = stack.enter_context(nc.Block())

        @block.sync
        def _(sp):
            sp.dma_start(causal[:], K.d["causal"]).then_inc(K.loaded.sem, 16)

        @block.gpsimd
        def _(pool):
            pool.sem_inc(scored.sem, 1)
            with pool.Fori(0, 4) as i:
                pool.wait_ge(scored.sem, i * 12 + (scored.base + 1))
                nc.gpsimd.tensor_copy(kS[:], one(kT[:, bass.ds(i, 1), :]))
                nc.gpsimd.tensor_copy(qS[:], one(qT[:, bass.ds(i, 1), :]))
                nc.gpsimd.tensor_copy(hot[:, 0:2], K.ident[0:64, bass.ds(i * 2, 2)])
                nc.gpsimd.tensor_copy(hot[:, 2:4], K.ident[0:64, bass.ds(i * 2 + 32, 2)]).then_inc(staged.sem, 1)

        @block.tensor
        def _(pe):
            with pe.Fori(0, 4) as i:
                pe.wait_ge(staged.sem, i + (staged.base + 1))
                for b in range(2):
                    r = slice(64 * b, 64 * b + 64)
                    for d in range(2):
                        mm = nc.tensor.matmul(K.pairs[2][:, d * 512:d * 512 + LAT],
                                              hot[:, 2 * d + b:2 * d + b + 1].broadcast_to([64, P]), top[:],
                                              start=True, stop=True)
                    mm.then_inc(spread.sem, 1)
                    for j, s in enumerate(order):
                        pe.wait_ge(mixed.sem, i * 12 + (mixed.base + 6 * b + j + 1))
                        nc.tensor.matmul(K.pairs[0][:, 512 * (j % 2):512 * (j % 2) + LAT], kS[r, s * P:s * P + P],
                                         qS[r, :], start=True, stop=True).then_inc(scored.sem, 1)
                    pe.wait_ge(mixed.sem, i * 12 + (mixed.base + 6 * b + 8))
                    for j in range(4):
                        d, half = j % 2, j // 2
                        pe.wait_ge(read.sem, i * 8 + (read.base + 4 * b + j + 1))
                        for u in range(2):
                            t = 2 * half + u
                            keys = [4, 5] + (list(range(t + 1)) if d == 0 else list(range(t, 4)))
                            for n, s in enumerate(keys):
                                mm = nc.tensor.matmul(
                                    K.pairs[3][:, 512 * d + u * 129:512 * d + u * 129 + 129],
                                    prob[:, d, s, t * P:t * P + P], one(val[:, s, bass.ds(i * 2 + b, 1), :]),
                                    start=n == 0, stop=n == len(keys) - 1)
                        mm.then_inc(summed.sem, 1)
                    pe.wait_ge(normed.sem, i * 2 + (normed.base + b + 1))
                    for t in range(4):
                        mm = nc.tensor.transpose(K.pairs[1][:, t * P:t * P + P], hn[:, t, :], K.ident[:])
                    mm.then_inc(turned.sem, 1)

        @block.scalar
        def _(act):
            with act.Fori(0, 4) as i:
                for b in range(2):
                    act.wait_ge(diag_ready.sem, i * 2 + (diag_ready.base + b + 1))
                    flat = diag[:].rearrange("p d s t -> p (d s t)")
                    nc.scalar.activation(flat, flat, ACT.Exp, scale=-1.0)
                    for j, s in enumerate(order):
                        act.wait_ge(mixed.sem, i * 12 + (mixed.base + 6 * b + j + 1))
                        for d in range(2):
                            lo, hi = beyond(s, d)
                            if hi > lo:
                                op = nc.scalar.activation(wgt[:, j % 2, d, lo:hi], K.pairs[2][:, 512 * d + lo:512 * d + hi],
                                                          ACT.Exp, bias=one(keysT[:, s:s + 1, bass.ds(i * 2 + (32 * d + b), 1)]),
                                                          scale=-1.0)
                        op.then_inc(weighed.sem, 1)
                    act.wait_ge(read.sem, i * 8 + (read.base + 4 * b + 6))
                    for t in range(4):
                        nc.scalar.activation(junk, hs[:, t, :], ACT.Square, accum_out=ss[:, t:t + 1]).then_inc(K.act_c.sem, 1)
                        act.wait_ge(K.act_c.sem, i * 8 + (K.act_c.base + 4 * b + t + 1))
                    nc.scalar.activation(ss[:], ss[:], ACT.Sqrt, bias=K.eps[:], scale=1.0 / P).then_inc(rooted.sem, 1)

        @block.vector
        def _(dve):
            dve.sem_inc(mixed.sem, 2)
            dve.sem_inc(read.sem, 2)
            chain = Chain(dve, K.dve_chain)
            dve.wait_ge(K.loaded.sem, K.loaded.base + 16)
            with chain.loop(4, 2 * (3 * 4 + 1 + 3 + 1)) as i:
                for b in range(2):
                    dve.wait_ge(spread.sem, i * 2 + (spread.base + b + 1))
                    for d in range(2):
                        for s in range(4):
                            op = nc.vector.scalar_tensor_tensor(
                                diag[:, d, s, :], K.pairs[2][:, 512 * d + s * P:512 * d + s * P + P],
                                one(keysT[:, s:s + 1, bass.ds(i * 2 + (32 * d + b), 1)]), causal[:, d, :],
                                ALU.subtract, ALU.max)
                    op.then_inc(diag_ready.sem, 1)
                    for j, s in enumerate(order):
                        dve.wait_ge(scored.sem, i * 12 + (scored.base + 6 * b + j + 2))
                        dve.wait_ge(weighed.sem, i * 12 + (weighed.base + 6 * b + j + 1))
                        bank = 512 * (j % 2)
                        for d in range(2):
                            lo, hi = beyond(s, d)
                            if s < 4:
                                op = nc.vector.scalar_tensor_tensor(
                                    prob[:, d, s, s * P:s * P + P], K.pairs[0][:, bank + s * P:bank + s * P + P], 0.125,
                                    diag[:, d, s, :], ALU.mult, ALU.mult)
                            if hi > lo:
                                op = nc.vector.scalar_tensor_tensor(
                                    prob[:, d, s, lo:hi], K.pairs[0][:, bank + lo:bank + hi], 0.125,
                                    wgt[:, j % 2, d, lo:hi], ALU.mult, ALU.mult)
                        op.then_inc(mixed.sem, 1)
                    for j in range(4):
                        d, half = j % 2, j // 2
                        dve.wait_ge(summed.sem, i * 8 + (summed.base + 4 * b + j + 1))
                        ps = K.pairs[3][:, 512 * d:512 * d + 258].rearrange("p (u c) -> p u c", u=2)
                        total = ps[:, :, 128:129].rearrange("p u c -> p (u c)")
                        chain.step(nc.vector.scalar_tensor_tensor(
                            den[:, d, :], total, -1.0,
                            floorT[:, 2 * half:2 * half + 2, bass.ds(i * 2 + (32 * d + b), 1)].rearrange("p u c -> p (u c)"),
                            ALU.mult, ALU.max))
                        chain.sync()
                        chain.step(nc.vector.scalar_tensor_tensor(den[:, d, :], total, 1.0, den[:, d, :], ALU.mult, ALU.max))
                        chain.sync()
                        chain.step(nc.vector.reciprocal(den[:, d, :], den[:, d, :]))
                        chain.sync()
                        for u in range(2):
                            t = 2 * half + u
                            if d == 0:
                                op = nc.vector.tensor_scalar(hs[:, t, :], ps[:, u, 0:P], den[:, d, u:u + 1], None, ALU.mult)
                            else:
                                op = nc.vector.scalar_tensor_tensor(hs[:, t, :], ps[:, u, 0:P], den[:, d, u:u + 1],
                                                                    hs[:, t, :], ALU.mult, ALU.add)
                        op.then_inc(read.sem, 1)
                        if d == 0:
                            dve.wait_ge(read.sem, i * 8 + (read.base + 4 * b + j + 3))
                    dve.wait_ge(rooted.sem, i * 2 + (rooted.base + b + 1))
                    chain.step(nc.vector.reciprocal(ss[:], ss[:]))
                    chain.sync()
                    for t in range(4):
                        op = nc.vector.tensor_scalar(hn[:, t, :], hs[:, t, :], ss[:, t:t + 1], None, ALU.mult)
                        if t < 3:
                            chain.step(op)
                    op.then_inc(normed.sem, 1)
                    dve.wait_ge(turned.sem, i * 2 + (turned.base + b + 1))
                    head = bass.ds(i * 2 + b, 1)
                    chain.step(nc.vector.scalar_tensor_tensor(
                        one(yT[:, head, 0:LAT]), K.pairs[1][:, 0:LAT], K.vec[:, bass.ds(i * 2 + (VEC["out_g"][0] + b), 1)],
                        one(sig[:, head, :]), ALU.mult, ALU.mult))
                    chain.sync()
            chain.close()
    K.loaded.base += 16
    for c, n in ((spread, 8), (scored, 49), (summed, 32), (turned, 8), (weighed, 48), (rooted, 8), (K.act_c, 32),
                 (mixed, 50), (read, 34), (normed, 8), (diag_ready, 8), (staged, 4)):
        c.base += n


def layer1(K):
    nc = K.nc
    ada_stage(K, 1)
    norm_stage(K, K.xT, K.hT, KD, ALL, K.v("norm1_1", 0, 8), scale=1, shift=0)
    with ExitStack() as outer:
        sb = lambda name, shape: outer.enter_context(K.temp(name, shape))
        keysT, floorT, top = sb("keysT", [P, 6, 64]), sb("floorT", [P, 4, 64]), sb("top", [64, LAT])
        gate_stage(K, keysT, floorT, top)
        qT, kT = sb("qT", [P, 4, LAT]), sb("kT", [P, 4, ALL])
        conv_qk_stage(K, qT, kT)
        sig = sb("sig", [P, 8, LAT])
        project_stage(K, ["w_ml_o"], K.hT, LAT, 8, lambda b: ("act", lambda act, ps: nc.scalar.activation(
            sig[:, b, :], ps[:, 0:LAT], ACT.Sigmoid)))
        val = sb("val", [P, 6, 8, 129])
        g = K.first("w_ml_v")
        token_major_stage(K, ["w_ml_v"], [
            (g + c, t == 5, [(K.hT[:, k, t * P:t * P + P], K.slot(g + c, KD, 256)[:, k, :]) for k in range(KD)],
             256, val[:, t, 2 * c:2 * c + 2, 0:128]) for c in range(4) for t in range(6)],
            ones=val[:].rearrange("p t h c -> p (t h) c")[:, :, 128:129])
        mlstm_stage(K, qT, kT, keysT, floorT, top, val, sig, K.hT)
    residual_stage(K, "w_ml_out", K.hT, KD, LAT, 2)
    norm_stage(K, K.xT, K.hT, KD, LAT, K.v("norm2_1", 0, 8), scale=4, shift=3)
    ffn(K, 1, LAT, 5)



TOPK = 128


def index_stage(K, iqT, ikT, iw, pen):
    nc = K.nc
    dots, relus, added = K.pe_a, K.act_a, K.dve_a
    jobs = [(t, h) for t in range(1, 4) for h in range(4)]
    with ExitStack() as stack:
        sb = lambda name, shape: stack.enter_context(K.temp(name, shape))
        rl, score, best = sb("rl", [P, 2, LAT]), sb("score", [P, LAT]), sb("best", [P, 8])
        block = stack.enter_context(nc.Block())

        @block.tensor
        def _(pe):
            for j, (t, h) in enumerate(jobs):
                if j >= 4:
                    pe.wait_ge(relus.sem, relus.base + j - 3)
                r = slice(64 * (h % 2), 64 * (h % 2) + 64)
                nc.tensor.matmul(K.pairs[j % 4][:, 0:P * (t + 1)], iqT[r, h // 2, t * P:t * P + P],
                                 ikT[r, 0:P * (t + 1)], start=True, stop=True).then_inc(dots.sem, 1)

        @block.scalar
        def _(act):
            for j, (t, h) in enumerate(jobs):
                act.wait_ge(dots.sem, dots.base + j + 1)
                if j >= 2:
                    act.wait_ge(added.sem, added.base + j - 1)
                nc.scalar.activation(rl[:, j % 2, 0:P * (t + 1)], K.pairs[j % 4][:, 0:P * (t + 1)],
                                     ACT.Relu).then_inc(relus.sem, 1)

        @block.vector
        def _(dve):
            chain = Chain(dve, K.dve_chain)
            flat = iw[:].rearrange("p t h -> p (t h)")
            chain.step(nc.vector.tensor_scalar(flat, flat, 4.0 ** -0.5 * 64.0 ** -0.5, None, ALU.mult))
            chain.step(nc.vector.memset(pen[:, 0, 0:P], 0.0))
            chain.sync()
            chain.step(nc.vector.memset(pen[0:64, 0, 64:P], -BIG))
            for j, (t, h) in enumerate(jobs):
                nk = P * (t + 1)
                dve.wait_ge(relus.sem, relus.base + j + 1)
                chain.sync()
                w = iw[:, t, h:h + 1]
                if h == 0:
                    nc.vector.tensor_scalar(score[:, 0:nk], rl[:, j % 2, 0:nk], w, None, ALU.mult).then_inc(added.sem, 1)
                else:
                    nc.vector.scalar_tensor_tensor(score[:, 0:nk], rl[:, j % 2, 0:nk], w, score[:, 0:nk],
                                                   ALU.mult, ALU.add).then_inc(added.sem, 1)
                dve.wait_ge(added.sem, added.base + j + 1)
                if h < 3:
                    continue
                chain.step(nc.vector.memset(score[0:64, nk - 64:nk], -BIG))
                for _ in range(TOPK // 8):
                    chain.sync()
                    chain.step(nc.vector.max(best[:], score[:, 0:nk]))
                    chain.sync()
                    chain.step(nc.vector.match_replace(score[:, 0:nk], best[:], score[:, 0:nk], -3 * BIG * 1e8))
                chain.sync()
                chain.step(nc.vector.tensor_scalar(pen[:, t, 0:nk], score[:, 0:nk], -2 * BIG * 1e8, -BIG,
                                                   ALU.is_gt, ALU.mult))
            chain.close()
    for c in (dots, relus, added):
        c.base += len(jobs)


def lru_stage(K, cx, cy, yc):
    nc = K.nc
    g = K.first("w2_lru")
    w = K.slot(g, 8, P)
    with ExitStack() as stack:
        sb = lambda name, shape: stack.enter_context(K.temp(name, shape))
        u, rec, inp, dec, th = (sb(n, [P, 4, LAT]) for n in ("u", "rec", "inp", "dec", "th"))
        ge = yc
        soft, rate = sb("soft", [P, 4]), sb("rate", [P, 2, 4])
        block = stack.enter_context(nc.Block())

        @block.sync
        def _(sp):
            K.stream(sp, ["w2_lru"])

        @block.tensor
        def _(pe):
            K.wait_weights(pe, g)
            for t in range(4):
                pe.wait_ge(K.dve_a.sem, K.dve_a.base + t + 1)
                for m in range(2):
                    mm = nc.tensor.matmul(K.pairs[t][:, 512 * m:512 * m + LAT], w[:, 4 * m + t, :], u[:, t, :],
                                          start=True, stop=True)
                mm.then_inc(K.pe_a.sem, 1)
            pe.wait_ge(K.pe_a.sem, K.pe_a.base + 4)
            pe.sem_inc(K.w_used.sem, 1)

        @block.scalar
        def _(act):
            chain = Chain(act, K.act_chain)
            chain.step(nc.scalar.activation(soft[:], K.v("lam", 0, 4), ACT.Abs))
            chain.sync()
            chain.step(nc.scalar.activation(soft[:], soft[:], ACT.Exp, scale=-1.0))
            chain.sync()
            nc.scalar.activation(soft[:], soft[:], ACT.Ln, bias=K.ones[:, 0:1]).then_inc(K.act_a.sem, 1)
            for t in range(4):
                act.wait_ge(K.pe_a.sem, K.pe_a.base + t + 1)
                nc.scalar.activation(rec[:, t, :], K.pairs[t][:, 0:LAT], ACT.Sigmoid, bias=K.v("ba", t))
                chain.step(nc.scalar.activation(inp[:, t, :], K.pairs[t][:, 512:512 + LAT], ACT.Sigmoid, bias=K.v("bx", t)))
            act.wait_ge(K.pool_a.sem, K.pool_a.base + 1)
            nc.scalar.activation(ge, ge, ACT.Sigmoid, scale=2 * 0.7978845608028654).then_inc(K.act_c.sem, 1)
            chain.sync()
            act.wait_ge(K.dve_b.sem, K.dve_b.base + 1)
            for t in range(4):
                op = nc.scalar.activation(th[:, t, :], rec[:, t, :], ACT.Tanh, scale=rate[:, 0, t:t + 1])
            for t in range(4):
                op = nc.scalar.activation(dec[:, t, :], rec[:, t, :], ACT.Exp, scale=rate[:, 1, t:t + 1])
            op.then_inc(K.act_b.sem, 1)
            act.wait_ge(K.dve_c.sem, K.dve_c.base + 1)
            nc.scalar.activation(th[:], th[:], ACT.Sqrt).then_inc(K.act_b.sem, 1)
            chain.close()

        @block.gpsimd
        def _(pool):
            chain = Chain(pool, K.pool_chain)
            chain.step(nc.gpsimd.tensor_tensor(ge, cy, cy, ALU.mult))
            chain.sync()
            chain.step(nc.gpsimd.tensor_scalar(ge, ge, 0.044715, 1.0, ALU.mult, ALU.add))
            chain.sync()
            nc.gpsimd.tensor_tensor(ge, ge, cy, ALU.mult).then_inc(K.pool_a.sem, 1)
            pool.wait_ge(K.act_c.sem, K.act_c.base + 1)
            nc.gpsimd.tensor_tensor(ge, ge, cy, ALU.mult).then_inc(K.pool_a.sem, 1)
            chain.close()

        @block.vector
        def _(dve):
            chain = Chain(dve, K.dve_chain)
            tap = lambda j, t: K.v("ccw", 4 * j + t)
            for t in range(4):
                chain.step(nc.vector.tensor_scalar(u[:, t, :], cx[:, t, :], tap(3, t), K.v("ccb", t), ALU.mult, ALU.add))
                for back in range(1, 4):
                    chain.sync()
                    op = nc.vector.scalar_tensor_tensor(u[:, t, back:], cx[:, t, 0:LAT - back], tap(3 - back, t),
                                                        u[:, t, back:], ALU.mult, ALU.add)
                    if back < 3:
                        chain.step(op)
                op.then_inc(K.dve_a.sem, 1)
            dve.wait_ge(K.act_a.sem, K.act_a.base + 1)
            chain.step(nc.vector.tensor_scalar(rate[:, 0, :], K.v("lam", 0, 4), -1.0, 0.0, ALU.mult, ALU.max))
            chain.sync()
            chain.step(nc.vector.tensor_tensor(rate[:, 0, :], rate[:, 0, :], soft[:], ALU.add))
            chain.sync()
            chain.step(nc.vector.tensor_scalar(rate[:, 1, :], rate[:, 0, :], -8.0, None, ALU.mult))
            chain.sync()
            nc.vector.tensor_scalar(rate[:, 0, :], rate[:, 0, :], 8.0, None, ALU.mult).then_inc(K.dve_b.sem, 1)
            dve.wait_ge(K.act_b.sem, K.act_b.base + 1)
            chain.step(nc.vector.tensor_tensor(rec[:], dec[:], dec[:], ALU.mult))
            chain.sync()
            nc.vector.scalar_tensor_tensor(th[:], rec[:], 1.0, th[:], ALU.add, ALU.mult).then_inc(K.dve_c.sem, 1)
            chain.step(nc.vector.tensor_tensor(inp[:], inp[:], u[:], ALU.mult))
            chain.sync()
            dve.wait_ge(K.act_b.sem, K.act_b.base + 2)
            chain.step(nc.vector.tensor_tensor(inp[:], inp[:], th[:], ALU.mult))
            chain.sync()
            for t in range(4):
                chain.step(nc.vector.tensor_tensor_scan(u[:, t, :], dec[:, t, :], inp[:, t, :], 0.0, ALU.mult, ALU.add))
            chain.sync()
            dve.wait_ge(K.pool_a.sem, K.pool_a.base + 2)
            nc.vector.tensor_tensor(yc, u[:], ge, ALU.mult)
            chain.close()
    for c, n in ((K.dve_a, 4), (K.pe_a, 4), (K.act_a, 1), (K.act_b, 2), (K.act_c, 1), (K.dve_b, 1), (K.dve_c, 1),
                 (K.pool_a, 2)):
        c.base += n


def merge_stage(K, yT, merged):
    nc = K.nc
    first = K.first("w2_merge")
    multiplied, gated, summed = K.pe_a, K.act_a, K.dve_a
    bank = lambda c: K.pairs[c // 2][:, 512 * (c % 2):512 * (c % 2) + LAT]
    with ExitStack() as stack:
        sb = lambda name, shape: stack.enter_context(K.temp(name, shape))
        sg, part = sb("sg", [P, 3, LAT]), sb("part", [P, LAT])
        block = stack.enter_context(nc.Block())

        @block.sync
        def _(sp):
            K.stream(sp, ["w2_merge"])

        @block.tensor
        def _(pe):
            with pe.Fori(0, 4) as i:
                for b in range(2):
                    for c in range(2):
                        g = first + 2 * b + c
                        pe.wait_ge(K.w_ready[g % RING].sem, i * 16 + 16 * (g // RING + 1))
                        w = K.slot(g, KD, 256)
                        for half in range(2):
                            branch = 2 * c + half
                            if branch < 3:
                                pe.wait_ge(gated.sem, i * 6 + (gated.base + 3 * b + branch + 1))
                                for k in range(KD):
                                    mm = nc.tensor.matmul(bank(branch), w[:, k, half * P:half * P + P], K.hT[:, k, 0:LAT],
                                                          start=k == 0, stop=k == KD - 1)
                                mm.then_inc(multiplied.sem, 1)
                            else:
                                pe.wait_ge(summed.sem, i * 2 + (summed.base + b + 1))
                                for y, ks in enumerate(((0, 1), (2, 3), (4, 5, 6, 7))):
                                    for k in ks:
                                        mm = nc.tensor.matmul(bank(4 + y), w[:, k, P:2 * P], yT[:, k, :],
                                                              start=k == ks[0], stop=k == ks[-1])
                                    mm.then_inc(multiplied.sem, 1)
                        pe.wait_ge(multiplied.sem, i * 12 + (multiplied.base + 6 * b + (2 if c == 0 else 6)))
                        pe.sem_inc(K.w_used.sem, 1)

        @block.scalar
        def _(act):
            act.sem_inc(gated.sem, 3)
            with act.Fori(0, 4) as i:
                for b in range(2):
                    act.wait_ge(summed.sem, i * 2 + (summed.base + b + 1))
                    for c in range(3):
                        act.wait_ge(multiplied.sem, i * 12 + (multiplied.base + 6 * b + c + 1))
                        nc.scalar.activation(sg[:, c, :], bank(c), ACT.Sigmoid, bias=K.vec[
                            :, bass.ds(i * 2 + (VEC["b_gate"][0] + 8 * c + b), 1)]).then_inc(gated.sem, 1)

        @block.vector
        def _(dve):
            dve.sem_inc(summed.sem, 1)
            chain = Chain(dve, K.dve_chain)
            with chain.loop(4, 8) as i:
                for b in range(2):
                    out = merged[:, bass.ds(i * 2 + b, 1), :].rearrange("p o t -> p (o t)")
                    dve.wait_ge(gated.sem, i * 6 + (gated.base + 3 * b + 6))
                    for c in range(3):
                        dve.wait_ge(multiplied.sem, i * 12 + (multiplied.base + 6 * b + c + 4))
                        to = out if c == 0 else part[:]
                        chain.step(nc.vector.tensor_tensor(to, sg[:, c, :], bank(4 + c), ALU.mult))
                        chain.sync()
                        if c > 0:
                            op = nc.vector.tensor_tensor(out, out, part[:], ALU.add)
                            if c == 1:
                                chain.step(op)
                                chain.sync()
                            else:
                                op.then_inc(summed.sem, 1)
            chain.close()
    multiplied.base += 48
    gated.base += 27
    summed.base += 9


def layer2(K):
    nc = K.nc
    norm_stage(K, K.xT, K.hT, KD, LAT, K.v("g_mix", 0, 8))
    with ExitStack() as outer:
        sb = lambda name, shape: outer.enter_context(K.temp(name, shape))
        hd = sb("hd", [P, 11, LAT])
        val, iw = sb("val", [P, 4, 512]), sb("iw", [P, 4, 4])
        yT = sb("yT", [P, 8, LAT])
        first = K.first("w2_heads")
        kinds = [(K.qgain[:, 2:3], False), (K.v("ak_g"), False), (K.qgain[:, 3:4], True), (K.v("bk_g"), True),
                 (None, True), (K.v("ik_g"), True)]
        tiles = []
        for b in range(11):
            w = K.slot(first + b // 2, KD, 256)
            gain, rope = kinds[b // 2]
            tiles.append(dict(
                chunk=first + b // 2, rows=P, sums=K.ones64[:], scale=1 / 64, rope=rope, gain=gain, dst=hd[:, b, :],
                mms=[(w[:, k, b % 2 * P:b % 2 * P + P], lambda a, e, k=k: K.hT[:, k, a:e]) for k in range(KD)]))
        heads_stage(K, ["w2_heads"], tiles, LAT, "trig_seq", "rot_seq")
        with K.temp("cc", [P, 8, LAT]) as cc:
            def store(b):
                if b % 2 == 0:
                    return "act", lambda act, ps: nc.scalar.activation(cc[:, b, :], ps[:, 0:LAT], ACT.Copy)
                return "dve", lambda chain, ps: nc.vector.tensor_copy(cc[:, b, :], ps[:, 0:LAT])
            project_stage(K, ["w2_c"], K.hT, LAT, 8, store)
            g = K.first("w2_v")
            jobs = [(g + c, t == 3, [(K.hT[:, k, t * P:t * P + P], K.slot(g + c, KD, 256)[:, k, :]) for k in range(KD)],
                     256, val[:, t, 256 * c:256 * c + 256]) for c in range(2) for t in range(4)]
            gw = K.first("w2_iw")
            jobs += [(gw, t == 3, [(K.hT[:, k, t * P:t * P + P], K.slot(gw, KD, 4)[:, k, :]) for k in range(KD)],
                      4, iw[:, t, :]) for t in range(4)]
            token_major_stage(K, ["w2_v", "w2_iw"], jobs)
            lru_stage(K, cc[:, 0:4, :], cc[:, 4:8, :], yT[:, 4:8, :])
        pen, rel = sb("pen", [P, 4, LAT]), sb("rel", [P, 4, LAT])
        mix = sb("mix", [P, 4, 512])
        index_stage(K, hd[:, 8:10, :], hd[:, 10, :], iw, pen)
        with nc.Block() as block:
            @block.sync
            def _(sp):
                sp.dma_start(rel[:], K.d["rel"]).then_inc(K.loaded.sem, 16)

            @block.vector
            def _(dve):
                dve.wait_ge(K.loaded.sem, K.loaded.base + 16)
                nc.vector.memset(rel[0:64, :, LAT - 64:LAT], -BIG)
        K.loaded.base += 16

        def steps(_):
            out = []
            for t in range(4):
                nk = P * (t + 1)
                for h in range(8):
                    kind, hh = h // 4, h % 4
                    r, blk = slice(64 * (hh % 2), 64 * (hh % 2) + 64), hh // 2
                    out.append(dict(
                        q=hd[r, 4 * kind + blk, t * P:t * P + P], keys=[(0, hd[r, 4 * kind + 2 + blk, 0:nk])], nk=nk,
                        bias=rel[:, hh, LAT - nk:LAT] if kind == 0 else pen[:, t, 0:nk],
                        v=[val[:, c, 64 * h:64 * h + 64] for c in range(t + 1)],
                        out=mix[:, t, 64 * h:64 * h + 64]))
            return out
        attention_stage(K, 1, steps, None)
        untoken_stage(K, mix, yT, 4, 4)
        merged = sb("merged", [P, KD, LAT])
        merge_stage(K, yT, merged)
        residual_stage(K, "w2_out", merged, KD, LAT, None)
    norm_stage(K, K.xT, K.hT, KD, LAT, K.v("g_ffn", 0, 8))
    ffn(K, 2, LAT, None)


def store_stage(K, tokens=LAT):
    with K.nc.Block() as block:
        @block.sync
        def _(sp):
            sp.dma_start(K.d["out"], K.xT[:, :, 0:tokens]).then_inc(K.stored.sem, 16)
            sp.wait_ge(K.stored.sem, 16)

def build(nc, arrays):
    with ExitStack() as stack:
        K = Kernel(nc, arrays, stack)
        load_stage(K)
        layer0(K)
        layer1(K)
        layer2(K)
        store_stage(K)


def lay_out(inp):
    a = {k: np.asarray(v) for k, v in inp.items()}
    out = {}

    def pack(w, cols):
        k, n = w.shape
        return np.ascontiguousarray(w.reshape(k // P, P, n // cols, cols).transpose(2, 1, 0, 3)).reshape(
            n // cols, P, -1)

    def pair(left, right):
        k, n = left.shape
        both = np.stack([left.reshape(k, n // P, P), right.reshape(k, n // P, P)], 2)
        return pack(both.reshape(k, 2 * n), 256)

    zeros = lambda *shape: np.zeros(shape, np.float32)
    for layer in range(2):
        out[f"w_ada{layer}"] = pack(a["ada_w"][layer], 256)
        up = a["ffn_w_up"][layer]
        out[f"w_up{layer}"] = pair(up[:, :D_FF], up[:, D_FF:])
        out[f"w_down{layer}"] = pack(a["ffn_w_down"][layer], P)
    w = a["att_w_in"][0]
    cq, ckv, kr, gq, gk, gv = np.split(w, np.cumsum([384, 256, 32, 512, 128])[:5], axis=1)
    out["w_att_lo"] = pack(np.concatenate([cq, ckv, zeros(D, 64), kr, zeros(D, 32)], 1), 256)
    out["w_att_gqa"] = pack(np.concatenate([gq, gk[:, :64], gk[:, :64], gk[:, 64:], gk[:, 64:]], 1), 256)
    out["w_gv"] = pack(gv, P)
    out["w_qb"] = pack(a["mla_w_qb"][0], 768)
    kvb = a["mla_w_kvb"][0].reshape(256, 8, 128)
    out["w_kvb"] = pack(np.concatenate([kvb[:, :, :64], zeros(256, 8, 32)], 2).reshape(256, 768), 768)
    out["w_va"] = pack(kvb[:, :, 64:].reshape(256, 512), 512)
    out["w_att_out"] = pack(a["att_w_out"][0], 256)

    w = a["ml_w_in"][0]
    g = w[:, 3072:3104]
    gates = zeros(D, P)
    gate_i, gate_f = zeros(P), zeros(P)
    gb = a["ml_gate_b"][0]
    for d in range(2):
        gates[:, 32 * d:32 * d + 8] = g[:, 16 * d:16 * d + 8]
        gates[:, 64 + 32 * d:72 + 32 * d] = g[:, 16 * d + 8:16 * d + 16]
        gate_i[32 * d:32 * d + 8] = gb[16 * d:16 * d + 8]
        gate_f[32 * d:32 * d + 8] = gb[16 * d + 8:16 * d + 16]
    out["w_ml_gate"] = pack(gates, P)
    out["w_ml_qk"] = pack(w[:, :1024], 256)
    out["w_ml_v"] = pack(w[:, 1024:2048], 256)
    out["w_ml_o"] = pack(w[:, 2048:3072], 256)
    out["w_ml_out"] = pack(a["ml_w_out"][0], 256)

    w = a["w_in_2"][0]
    cuts = np.cumsum([256] * 6 + [256, 64, 4, 512, 512])
    aq, ak, av, bq, bk, bv, iq, ik, iw, cx, cy, gt = np.split(w, cuts, axis=1)
    out["w2_heads"] = pack(np.concatenate([aq, ak, bq, bk, iq, ik, ik, zeros(D, P)], 1), 256)
    out["w2_c"] = pack(np.concatenate([cx, cy], 1), 256)
    out["w2_v"] = pack(np.concatenate([av, bv], 1), 256)
    out["w2_iw"] = pack(iw, 4)
    lru = zeros(P, 8, P)
    for m, name in enumerate(("lru_wa_2", "lru_wx_2")):
        for t in range(4):
            for h in range(2):
                lru[64 * h:64 * h + 64, 4 * m + t, 64 * h:64 * h + 64] = a[name][0, 2 * t + h]
    out["w2_lru"] = lru.reshape(1, P, 1024)
    both = np.concatenate([pair(gt[:, :D], gt[:, D:2 * D]), pair(gt[:, 2 * D:], a["w_branch_2"][0])], 1)
    out["w2_merge"] = both.reshape(16, P, 2048)
    out["w2_out"] = pack(a["w_out_2"][0], 256)
    up = a["w_ffn_in_2"][0]
    out["w_up2"] = pair(up[:, :D_FF], up[:, D_FF:])
    out["w_down2"] = pack(a["w_ffn_out_2"][0], P)

    vec = zeros(P, NVEC)

    def put(name, v):
        at, n = VEC[name]
        v = np.asarray(v, np.float32)
        vec[:, at:at + n] = np.concatenate([v, zeros(n * P - v.size)]).reshape(n, P).T

    for layer in range(2):
        put(f"norm1_{layer}", a["norm1_g"][layer])
        put(f"norm2_{layer}", a["norm2_g"][layer])
        put(f"ada_b{layer}", a["ada_b"][layer])
        put(f"fcw{layer}", a["ffn_conv_w"][layer].ravel())
        put(f"fcb{layer}", a["ffn_conv_b"][layer])
    put("silu_in", np.stack([a["c"][0].reshape(8, P), a["c_ctx"].reshape(8, P)], 1).ravel())
    put("qa_g", a["mla_qa_g"][0])
    put("kva_g", a["mla_kva_g"][0])
    put("mq_g", a["mla_q_g"][0])
    put("mk_g", a["mla_k_g"][0])
    twice = lambda v: np.concatenate([v, v])
    put("gq_g", twice(a["gqa_q_g"][0]))
    put("gk_g", twice(a["gqa_k_g"][0]))
    put("mcw", a["ml_conv_w"][0].ravel())
    put("mcb", a["ml_conv_b"][0])
    put("gate_i", gate_i)
    put("gate_f", gate_f)
    put("out_g", a["ml_out_g"][0].ravel())
    put("g_mix", a["g_mix_2"][0])
    put("g_ffn", a["g_ffn_2"][0])
    put("aq_g", twice(a["qk_gain_a_2"][0, 0]))
    put("ak_g", twice(a["qk_gain_a_2"][0, 1]))
    put("bq_g", twice(a["qk_gain_b_2"][0, 0]))
    put("bk_g", twice(a["qk_gain_b_2"][0, 1]))
    put("ik_g", twice(a["g_idx_k_2"][0]))
    put("ccw", a["conv_w_2"][0].ravel())
    put("ccb", a["conv_b_2"][0])
    put("ba", a["lru_ba_2"][0])
    put("bx", a["lru_bx_2"][0])
    put("lam", a["lru_lambda_2"][0])
    put("b_gate", a["b_gate_2"][0])
    out["vec"] = vec

    tokens = np.concatenate([a["x"][0], a["ctx"][0]], 0)
    out["xT"] = np.ascontiguousarray(tokens.T.reshape(KD, P, ALL).transpose(1, 0, 2))
    rel = a["rel_bias_2"][0]
    n = LAT
    ext = np.concatenate([np.repeat(rel[:, :1], 1024, 1), rel, np.repeat(rel[:, -1:], 1024, 1)], 1)
    flip = ext[:, ::-1]
    out["rel"] = np.ascontiguousarray(np.stack(
        [flip[:, 1152 - 384 - p:1152 - 384 - p + n] for p in range(P)], 0))

    out["ident"] = np.eye(P, dtype=np.float32)
    out["ones64"] = np.kron(np.eye(2), np.ones((64, 64))).astype(np.float32)

    def axial(dim):
        rows = LAT // 64
        row = np.repeat(np.arange(rows), 64).astype(np.float32)
        col = np.tile(np.arange(64), rows).astype(np.float32)
        nf = dim // 4
        inv = (np.float32(10000.0) ** (-np.arange(nf, dtype=np.float32) / nf)).astype(np.float32)
        ar, ac = row[:, None] * inv, col[:, None] * inv
        return np.concatenate([ar, ar, ac, ac], 1)

    def table(ang, rows):
        t = zeros(P, 2, LAT)
        t[:, 0] = 1.0
        for r in rows:
            t[r:r + ang.shape[1], 0] = np.cos(ang).T
            t[r:r + ang.shape[1], 1] = np.sin(ang).T
        return t

    def rotation(q, starts):
        m = zeros(P, P)
        for s in starts:
            for j in range(q):
                m[s + q + j, s + j] = -1.0
                m[s + j, s + q + j] = 1.0
        return m

    out["trig_mla"] = table(axial(32), [64])
    out["trig_gqa"] = table(axial(64), [0, 64])
    out["rot_mla"] = rotation(8, [64, 80])
    out["rot_gqa"] = rotation(16, [0, 32, 64, 96])
    pos = np.arange(LAT, dtype=np.float32)
    inv = (1.0 / (np.float32(10000.0) ** (np.arange(0, 64, 2, dtype=np.float32) / 64))).astype(np.float32)
    ang = pos[:, None] * inv[None]
    out["trig_seq"] = table(np.concatenate([ang, ang], 1), [0, 64])
    out["rot_seq"] = rotation(32, [0, 64])
    s, t = np.arange(P)[:, None], np.arange(P)[None]
    out["causal"] = np.stack([np.where(s <= t, 0, 1e4), np.where(s >= t, 0, 1e4)], 1).astype(np.float32)
    return out


def kernel(**inputs):
    import concourse.bacc as bacc
    from concourse.bass_utils import run_bass_kernel_spmd

    nc = bacc.Bacc("TRN2", target_bir_lowering=False, num_devices=1)
    arrays = lay_out(inputs)
    aps = {name: nc.dram_tensor(f"in_{name}", a.shape, F32, kind="ExternalInput").ap() for name, a in arrays.items()}
    aps["out"] = nc.dram_tensor("out_y", (P, KD, LAT), F32, kind="ExternalOutput").ap()
    build(nc, aps)
    run = run_bass_kernel_spmd(nc, [{f"in_{n}": a for n, a in arrays.items()}], core_ids=[0])
    y = run.results[0]["out_y"]
    return np.ascontiguousarray(y.transpose(2, 1, 0)).reshape(1, LAT, D)
```

```python
from contextlib import ExitStack, contextmanager

import numpy as np
import concourse.bass as bass
from concourse import mybir

F32 = mybir.dt.float32
F32R = mybir.dt.float32r
ALU = mybir.AluOpType
ACT = mybir.ActivationFunctionType
AX = mybir.AxisListType

P = 128
D, KD = 1024, 8
LAT, CTX = 512, 256
ALL = LAT + CTX
D_FF, KF = 2816, 22
HIDDEN_PARTS = {0: (8, 8, 6), 1: (11, 11), 2: (11, 11)}
EPS = 1e-6
RING = 4
SLOT = 2 * KD * P
BIG = 1e30

VEC_ORDER = [
    ("norm1_0", 8), ("norm1_1", 8), ("norm2_0", 8), ("norm2_1", 8), ("ada_b0", 48), ("ada_b1", 48),
    ("silu_in", 16), ("fcw0", 66), ("fcb0", 22), ("fcw1", 66), ("fcb1", 22),
    ("qa_g", 3), ("kva_g", 2), ("mq_g", 1), ("mk_g", 1), ("gq_g", 1), ("gk_g", 1),
    ("mcw", 24), ("mcb", 8), ("gate_i", 1), ("gate_f", 1), ("out_g", 8),
    ("g_mix", 8), ("g_ffn", 8), ("aq_g", 1), ("ak_g", 1), ("bq_g", 1), ("bk_g", 1), ("ik_g", 1),
    ("ccw", 16), ("ccb", 4), ("ba", 4), ("bx", 4), ("lam", 4), ("b_gate", 24),
]
VEC, _n = {}, 0
for _name, _w in VEC_ORDER:
    VEC[_name] = (_n, _w)
    _n += _w
NVEC = _n


Q_GAINS = [("mq_g", 96), ("gq_g", 64), ("aq_g", 64), ("bq_g", 64)]


class Count:

    def __init__(self, sem):
        self.sem, self.base = sem, 0


class Chain:

    def __init__(self, engine, count):
        self.engine, self.count, self.n, self.turn = engine, count, 0, None

    def step(self, instruction):
        instruction.then_inc(self.count.sem, 1)
        self.n += 1

    def sync(self):
        if self.turn is None:
            self.engine.wait_ge(self.count.sem, self.count.base + self.n)
        else:
            i, per = self.turn
            self.engine.wait_ge(self.count.sem, i * per + (self.count.base + self.n))

    @contextmanager
    def loop(self, turns, per):
        with self.engine.Fori(0, turns) as i:
            start = self.n
            self.turn = (i, per)
            yield i
            assert self.n - start == per, (self.n - start, per)
            self.turn = None
        self.n = start + turns * per

    def close(self):
        self.count.base += self.n


def weight_plan():
    def ffn_of(layer):
        plan = []
        for part, kt in enumerate(HIDDEN_PARTS[layer]):
            per = down_blocks(kt)
            plan += [(f"w_up{layer}_{part}", kt, 2048), (f"w_down{layer}_{part}", KD // per, kt * P * per)]
        return plan
    return [
        ("w_ada0", 24, 2048), ("w_att_lo", 3, 2048), ("w_att_gqa", 3, 2048), ("w_gv", 1, 1024),
        ("w_qb", 2, 1152), ("w_kvb", 1, 1536), ("w_va", 1, 1024), ("w_att_out", 4, 2048),
        *ffn_of(0),
        ("w_ada1", 24, 2048), ("w_ml_gate", 1, 1024), ("w_ml_qk", 4, 2048), ("w_ml_o", 4, 2048),
        ("w_ml_v", 4, 2048), ("w_ml_out", 4, 2048), *ffn_of(1),
        ("w2_heads", 6, 2048), ("w2_v", 2, 2048), ("w2_iw", 1, 32), ("w2_c", 4, 2048),
        ("w2_lru", 1, 1024), ("w2_merge", 16, 2048), ("w2_out", 4, 2048),
        *ffn_of(2),
    ]


def down_blocks(kt):
    return 2 if kt <= KD else 1


def is_split(name):
    return name.startswith(("w_up", "w_down"))


class Kernel:

    def __init__(self, nc, arrays, stack):
        self.nc, self.d, self.temps = nc, arrays, 0
        sem = lambda name: Count(stack.enter_context(nc.semaphore(name)))
        self.sb = lambda name, shape: stack.enter_context(nc.sbuf_tensor(name, shape, F32))
        self.w_ready = [sem(f"w_ready{s}") for s in range(RING)]
        self.w_used = sem("w_used")
        self.ring = self.sb("ring", [P, RING, SLOT])
        self.plan, n = {}, 0
        self.chunks = []
        for name, count, floats in weight_plan():
            self.plan[name] = (n, count, floats)
            self.chunks += [(name, c, floats) for c in range(count)]
            n += count
        self.split_number, splits = {}, 0
        for chunk, (name, _, _) in enumerate(self.chunks):
            if is_split(name):
                self.split_number[chunk] = splits
                splits += 1
        self.high_ready = sem("high_ready")
        self.w_high = self.w_low = None
        self.loaded = sem("loaded")
        self.pe_a = sem("pe_a")
        self.pe_b = sem("pe_b")
        self.pe_c = sem("pe_c")
        self.pe_d = sem("pe_d")
        self.act_a = sem("act_a")
        self.act_b = sem("act_b")
        self.act_c = sem("act_c")
        self.dve_a = sem("dve_a")
        self.dve_b = sem("dve_b")
        self.dve_c = sem("dve_c")
        self.dve_d = sem("dve_d")
        self.dve_e = sem("dve_e")
        self.pool_a = sem("pool_a")
        self.stored = sem("stored")
        self.dve_chain = sem("dve_chain")
        self.act_chain = sem("act_chain")
        self.pool_chain = sem("pool_chain")
        self.free = [sem(f"psum_free{s}") for s in range(4)]
        self.pairs = [stack.enter_context(nc.psum_tensor(f"pair{i}", [P, 1024], F32)) for i in range(4)]
        self.xT = self.sb("xT", [P, KD, ALL])
        self.vec = self.sb("vec", [P, NVEC])
        self.ident = self.sb("ident", [P, P])
        self.ones = self.sb("ones", [P, P])
        self.ones64 = self.sb("ones64", [P, P])
        self.cvec = self.sb("cvec", [P, KD, 2])
        self.mod = self.sb("mod", [P, 48, 2])
        self.eps = self.sb("eps", [P, 1])
        self.qgain = self.sb("qgain", [P, 4])
        self.coef = self.sb("coef", [P, 2, KD])
        self.rinv = self.sb("rinv", [P, ALL])

    def temp(self, name, shape, dtype=F32):
        self.temps += 1
        return self.nc.sbuf_tensor(f"{name}_{self.temps}", shape, dtype)

    @contextmanager
    def activations(self):
        with self.temp("hT", [P, KD, ALL]) as self.hT:
            yield

    @contextmanager
    def split_weights(self):
        with self.temp("w_high", [P, 2, SLOT], F32R) as self.w_high, \
                self.temp("w_low", [P, 2, SLOT], F32R) as self.w_low:
            yield

    def split_high(self, act, chunk, i=0):
        if isinstance(i, int):
            chunk, i = chunk + i * RING, 0
        if chunk not in self.split_number:
            return
        floats, n = self.chunks[chunk][2], self.split_number[chunk]
        act.wait_ge(self.w_ready[chunk % RING].sem, i * 16 + 16 * (chunk // RING + 1))
        self.nc.scalar.activation(self.w_high[:, n % 2, 0:floats], self.ring[:, chunk % RING, 0:floats],
                                  ACT.Copy).then_inc(self.high_ready.sem, 1)

    def split_low(self, dve, chunk, i=0):
        if isinstance(i, int):
            chunk, i = chunk + i * RING, 0
        if chunk not in self.split_number:
            return
        floats, n = self.chunks[chunk][2], self.split_number[chunk]
        dve.wait_ge(self.high_ready.sem, i * RING + (n + 1))
        self.nc.vector.tensor_tensor(self.w_low[:, n % 2, 0:floats], self.ring[:, chunk % RING, 0:floats],
                                     self.w_high[:, n % 2, 0:floats].bitcast(F32),
                                     ALU.subtract).then_inc(self.w_used.sem, 1)

    def product(self, pe, out, chunk, kt, cols, block, high, low, tokens, i=0):
        if isinstance(i, int):
            chunk, i = chunk + i * RING, 0
        n = self.split_number[chunk]
        w_high, w_low = (w[:, n % 2, 0:kt * cols].rearrange("p (k c) -> p k c", k=kt) for w in (self.w_high, self.w_low))
        at = slice(block * P, block * P + P)
        pe.wait_ge(self.high_ready.sem, i * RING + (n + 1))
        for j, (a, e) in enumerate(spans(tokens)):
            for k in range(kt):
                self.nc.tensor.matmul(out[:, a:e], w_high[:, k, at], high[:, k, a:e], start=k == 0, stop=False)
                self.nc.tensor.matmul(out[:, a:e], w_high[:, k, at], low[:, k, a:e], start=False, stop=False)
            if j == 0:
                pe.wait_ge(self.w_used.sem, i * RING + (chunk + 1))
            for k in range(kt):
                mm = self.nc.tensor.matmul(out[:, a:e], w_low[:, k, at], high[:, k, a:e], start=False, stop=k == kt - 1)
        return mm

    def v(self, name, k=0, n=1, rows=P):
        at, _ = VEC[name]
        return self.vec[0:rows, at + k:at + k + n]

    def first(self, name):
        return self.plan[name][0]

    def slot(self, chunk, k, cols):
        return self.ring[:, chunk % RING, 0:k * cols].rearrange("p (k c) -> p k c", k=k)

    def wait_weights(self, pe, chunk):
        pe.wait_ge(self.w_ready[chunk % RING].sem, 16 * (chunk // RING + 1))

    def send(self, sp, chunk):
        name, c, floats = self.chunks[chunk]
        if chunk >= RING:
            sp.wait_ge(self.w_used.sem, chunk - RING + 1)
        sp.dma_start(self.ring[:, chunk % RING, 0:floats], self.d[name][c]).then_inc(
            self.w_ready[chunk % RING].sem, 16)

    def stream(self, sp, names):
        lo = self.first(names[0]) + RING
        n0, count, _ = self.plan[names[-1]]
        hi = min(n0 + count + RING, len(self.chunks))
        at = lo
        while at < hi:
            name, c, floats = self.chunks[at]
            run = min(self.plan[name][1] - c, hi - at)
            turns = run // RING
            if turns >= 2:
                with sp.Fori(0, turns) as i:
                    for s in range(RING):
                        sp.wait_ge(self.w_used.sem, i * RING + (at + s - RING + 1))
                        sp.dma_start(self.ring[:, (at + s) % RING, 0:floats],
                                     self.d[name][bass.ds(i * RING + (c + s), 1)].rearrange("o p f -> (o p) f")
                                     ).then_inc(self.w_ready[(at + s) % RING].sem, 16)
                at += turns * RING
            else:
                self.send(sp, at)
                at += 1


def spans(tokens):
    return [(0, LAT)] if tokens == LAT else [(0, LAT), (LAT, ALL)]



def load_stage(K):
    nc = K.nc
    with nc.Block() as block:
        @block.sync
        def _(sp):
            sp.dma_start(K.vec[:], K.d["vec"]).then_inc(K.loaded.sem, 16)
            for c in range(RING):
                K.send(sp, c)
            for t, name in ((K.ident, "ident"), (K.ones64, "ones64")):
                sp.dma_start(t[:], K.d[name]).then_inc(K.loaded.sem, 16)
            sp.dma_start(K.xT[:], K.d["xT"]).then_inc(K.loaded.sem, 16)
            sp.wait_ge(K.loaded.sem, 64)

        @block.vector
        def _(dve):
            nc.vector.memset(K.ones[:], 1.0)
            nc.vector.memset(K.eps[:], EPS)
            dve.wait_ge(K.loaded.sem, 64)
            for c, (name, dim) in enumerate(Q_GAINS):
                nc.vector.tensor_scalar(K.qgain[:, c:c + 1], K.v(name), float(dim) ** -0.5, None, ALU.mult)

        @block.scalar
        def _(act):
            act.wait_ge(K.loaded.sem, 64)
            nc.scalar.activation(K.cvec[:].rearrange("p k c -> p (k c)"), K.v("silu_in", 0, 16), ACT.Silu)
    K.loaded.base += 64


def reload_x_stage(K):
    with K.nc.Block() as block:
        @block.sync
        def _(sp):
            sp.dma_start(K.xT[:], K.d["xT"]).then_inc(K.loaded.sem, 16)
            sp.wait_ge(K.loaded.sem, K.loaded.base + 16)
    K.loaded.base += 16


def ada_stage(K, layer):
    nc = K.nc
    name = f"w_ada{layer}"
    first = K.first(name)
    filled, free, turned = K.pe_a, K.free, K.pe_b
    turns = 24 // RING
    with K.temp("mod_rows", [2, 6 * D]) as rows, nc.Block() as block:
        @block.sync
        def _(sp):
            K.stream(sp, [name])

        @block.tensor
        def _(pe):
            with pe.Fori(0, turns) as i:
                for s in range(RING):
                    g = first + s
                    pe.wait_ge(K.w_ready[g % RING].sem, i * 16 + 16 * (g // RING + 1))
                    pe.wait_ge(free[s].sem, i + (free[s].base + 1))
                    w = K.slot(g, KD, 256)
                    for k in range(KD):
                        mm = nc.tensor.matmul(K.pairs[s][0:2, 0:256], K.cvec[:, k, :], w[:, k, :],
                                              start=k == 0, stop=k == KD - 1)
                    mm.then_inc(filled.sem, 1)
                    pe.wait_ge(filled.sem, i * RING + (filled.base + s + 1))
                    pe.sem_inc(K.w_used.sem, 1)
            for s in range(4):
                pe.wait_ge(free[s].sem, free[s].base + turns + 1)
            for b in range(48):
                mm = nc.tensor.transpose(K.pairs[0][:, 2 * b:2 * b + 2], rows[:, b * P:b * P + P], K.ident[0:2, 0:2])
            mm.then_inc(turned.sem, 1)

        @block.scalar
        def _(act):
            for s in range(RING):
                act.sem_inc(free[s].sem, 1)
            with act.Fori(0, turns) as i:
                for s in range(RING):
                    act.wait_ge(filled.sem, i * RING + (filled.base + s + 1))
                    nc.scalar.activation(rows[:, bass.ds(i * 1024 + 256 * s, 256)], K.pairs[s][0:2, 0:256],
                                         ACT.Copy).then_inc(free[s].sem, 1)

        @block.vector
        def _(dve):
            dve.wait_ge(turned.sem, turned.base + 1)
            bias = K.v(f"ada_b{layer}", 0, 48)
            nc.vector.tensor_tensor(K.mod[:], K.pairs[0][:, 0:96].rearrange("p (b c) -> p b c", c=2),
                                    bias.unsqueeze(2).broadcast_to([P, 48, 2]), ALU.add)
    filled.base += 24
    turned.base += 1
    for s in range(4):
        free[s].base += turns + 1


def norm_stage(K, src, dst, nt, tokens, gain, scale=None, shift=None):
    nc = K.nc
    parts = spans(tokens)
    stat = K.pairs[3]
    sq_ready, stat_used, std_ready, out_ready = K.act_a, K.pe_a, K.act_b, K.dve_a
    with ExitStack() as stack:
        sq = stack.enter_context(K.temp("sq", [P, 2, ALL]))
        block = stack.enter_context(nc.Block())

        @block.scalar
        def _(act):
            for k in range(nt):
                if k >= 2:
                    act.wait_ge(stat_used.sem, stat_used.base + k - 1)
                nc.scalar.activation(sq[:, k % 2, 0:tokens], src[:, k, 0:tokens], ACT.Square).then_inc(sq_ready.sem, 1)
            act.wait_ge(stat_used.sem, stat_used.base + nt)
            nc.scalar.activation(K.rinv[:, 0:tokens], stat[:, 0:tokens], ACT.Sqrt, bias=K.eps[:],
                                 scale=1.0 / (nt * P)).then_inc(std_ready.sem, 1)
            if shift is not None:
                for k in range(nt):
                    act.wait_ge(out_ready.sem, out_ready.base + k + 1)
                    for j, (a, b) in enumerate(parts):
                        nc.scalar.activation(dst[:, k, a:b], dst[:, k, a:b], ACT.Identity,
                                             bias=K.mod[:, shift * KD + k, j:j + 1])

        @block.tensor
        def _(pe):
            for k in range(nt):
                pe.wait_ge(sq_ready.sem, sq_ready.base + k + 1)
                for a, b in parts:
                    mm = nc.tensor.matmul(stat[:, a:b], K.ones[:], sq[:, k % 2, a:b], start=k == 0, stop=k == nt - 1)
                mm.then_inc(stat_used.sem, 1)

        @block.vector
        def _(dve):
            chain = Chain(dve, K.dve_chain)
            coef = K.coef
            for j in range(len(parts)):
                if scale is None:
                    chain.step(nc.vector.tensor_copy(coef[:, j, 0:nt], gain))
                else:
                    chain.step(nc.vector.scalar_tensor_tensor(
                        coef[:, j, 0:nt], K.mod[:, scale * KD:scale * KD + nt, j], 1.0, gain, ALU.add, ALU.mult))
            dve.wait_ge(std_ready.sem, std_ready.base + 1)
            chain.step(nc.vector.reciprocal(K.rinv[:, 0:tokens], K.rinv[:, 0:tokens]))
            chain.sync()
            for k in range(nt):
                for j, (a, b) in enumerate(parts):
                    op = nc.vector.scalar_tensor_tensor(dst[:, k, a:b], src[:, k, a:b], coef[:, j, k:k + 1],
                                                        K.rinv[:, a:b], ALU.mult, ALU.mult)
                op.then_inc(out_ready.sem, 1)
            chain.close()
    sq_ready.base += nt
    stat_used.base += nt
    std_ready.base += 1
    out_ready.base += nt


def norm_split_stage(K, high, low, tokens, gain, scale, shift, ahead):
    nc = K.nc
    parts = spans(tokens)
    stat = K.pairs[3]
    sq_ready, stat_used, std_ready, scaled, high_done, low_done = K.act_a, K.pe_a, K.act_b, K.dve_a, K.act_c, K.dve_b
    with ExitStack() as stack:
        sq = stack.enter_context(K.temp("sq", [P, 2, ALL]))
        y = stack.enter_context(K.temp("normed", [P, 3, ALL]))
        block = stack.enter_context(nc.Block())

        @block.scalar
        def _(act):
            for k in range(KD):
                if k >= 2:
                    act.wait_ge(stat_used.sem, stat_used.base + k - 1)
                nc.scalar.activation(sq[:, k % 2, 0:tokens], K.xT[:, k, 0:tokens], ACT.Square).then_inc(sq_ready.sem, 1)
            act.wait_ge(stat_used.sem, stat_used.base + KD)
            nc.scalar.activation(K.rinv[:, 0:tokens], stat[:, 0:tokens], ACT.Sqrt, bias=K.eps[:],
                                 scale=1.0 / D).then_inc(std_ready.sem, 1)
            K.split_high(act, ahead)
            for k in range(KD):
                act.wait_ge(scaled.sem, scaled.base + k + 1)
                for j, (a, b) in enumerate(parts):
                    if shift is None:
                        op = nc.scalar.activation(high[:, k, a:b], y[:, k % 3, a:b], ACT.Copy)
                    else:
                        op = nc.scalar.activation(high[:, k, a:b], y[:, k % 3, a:b], ACT.Identity,
                                                  bias=K.mod[:, shift * KD + k, j:j + 1])
                op.then_inc(high_done.sem, 1)

        @block.tensor
        def _(pe):
            for k in range(KD):
                pe.wait_ge(sq_ready.sem, sq_ready.base + k + 1)
                for a, b in parts:
                    mm = nc.tensor.matmul(stat[:, a:b], K.ones[:], sq[:, k % 2, a:b], start=k == 0, stop=k == KD - 1)
                mm.then_inc(stat_used.sem, 1)

        @block.vector
        def _(dve):
            chain = Chain(dve, K.dve_chain)
            coef = K.coef
            for j in range(len(parts)):
                if scale is None:
                    chain.step(nc.vector.tensor_copy(coef[:, j, :], gain))
                else:
                    chain.step(nc.vector.scalar_tensor_tensor(
                        coef[:, j, :], K.mod[:, scale * KD:scale * KD + KD, j], 1.0, gain, ALU.add, ALU.mult))
            dve.wait_ge(std_ready.sem, std_ready.base + 1)
            chain.step(nc.vector.reciprocal(K.rinv[:, 0:tokens], K.rinv[:, 0:tokens]))
            chain.sync()
            for k in range(KD + 2):
                if k < KD:
                    if k >= 3:
                        dve.wait_ge(low_done.sem, low_done.base + k - 2)
                    for j, (a, b) in enumerate(parts):
                        op = nc.vector.scalar_tensor_tensor(y[:, k % 3, a:b], K.xT[:, k, a:b], coef[:, j, k:k + 1],
                                                            K.rinv[:, a:b], ALU.mult, ALU.mult)
                    op.then_inc(scaled.sem, 1)
                if k >= 2:
                    t = k - 2
                    dve.wait_ge(scaled.sem, scaled.base + t + 1)
                    dve.wait_ge(high_done.sem, high_done.base + t + 1)
                    for j, (a, b) in enumerate(parts):
                        add = 0.0 if shift is None else K.mod[:, shift * KD + t, j:j + 1]
                        op = nc.vector.scalar_tensor_tensor(low[:, t, a:b], y[:, t % 3, a:b], add,
                                                            high[:, t, a:b].bitcast(F32), ALU.add, ALU.subtract)
                    op.then_inc(low_done.sem, 1)
            K.split_low(dve, ahead)
            chain.close()
    for count in (sq_ready, stat_used, scaled, high_done, low_done):
        count.base += KD
    std_ready.base += 1


def project_stage(K, names, src, tokens, blocks, store, beside=None):
    nc = K.nc
    first = K.first(names[0])
    parts = spans(tokens)
    filled, free = K.pe_a, K.free
    engines = [store(b)[0] for b in range(blocks)]

    with nc.Block() as block:
        @block.sync
        def _(sp):
            K.stream(sp, names)

        @block.tensor
        def _(pe):
            for b in range(blocks):
                g = first + b // 2
                if b % 2 == 0:
                    K.wait_weights(pe, g)
                if b >= 4:
                    pe.wait_ge(free[b % 4].sem, free[b % 4].base + b // 4)
                w = K.slot(g, KD, 256)
                for a, e in parts:
                    for k in range(KD):
                        mm = nc.tensor.matmul(K.pairs[b % 4][:, a:e], w[:, k, b % 2 * P:b % 2 * P + P],
                                              src[:, k, a:e], start=k == 0, stop=k == KD - 1)
                mm.then_inc(filled.sem, 1)
                if b % 2 == 1:
                    pe.wait_ge(filled.sem, filled.base + b + 1)
                    pe.sem_inc(K.w_used.sem, 1)

        @block.scalar
        def _(act):
            for b in range(blocks):
                if engines[b] == "act":
                    act.wait_ge(filled.sem, filled.base + b + 1)
                    store(b)[1](act, K.pairs[b % 4]).then_inc(free[b % 4].sem, 1)

        @block.vector
        def _(dve):
            chain = Chain(dve, K.dve_chain)
            for b in range(blocks):
                if engines[b] == "dve":
                    dve.wait_ge(filled.sem, filled.base + b + 1)
                    store(b)[1](chain, K.pairs[b % 4]).then_inc(free[b % 4].sem, 1)
            if beside is not None:
                beside(dve, chain)
            chain.close()
    filled.base += blocks
    for s in range(4):
        free[s].base += len(range(s, blocks, 4))


def residual_stage(K, name, src, kt, tokens, gate):
    nc = K.nc
    first = K.first(name)
    parts = spans(tokens)
    per = 2
    unroll = per * RING
    filled, free = K.pe_a, K.free
    with nc.Block() as block:
        @block.sync
        def _(sp):
            K.stream(sp, [name])

        @block.tensor
        def _(pe):
            with pe.Fori(0, KD // unroll) as i:
                for b in range(unroll):
                    g = first + b // per
                    if b % per == 0:
                        pe.wait_ge(K.w_ready[g % RING].sem, i * 16 + 16 * (g // RING + 1))
                    pe.wait_ge(free[b % 4].sem, i * (unroll // 4) + (free[b % 4].base + b // 4 + 1))
                    w = K.slot(g, kt, P * per)
                    for a, e in parts:
                        for k in range(kt):
                            mm = nc.tensor.matmul(K.pairs[b % 4][:, a:e], w[:, k, b % per * P:b % per * P + P],
                                                  src[:, k, a:e], start=k == 0, stop=k == kt - 1)
                    mm.then_inc(filled.sem, 1)
                    if b % per == per - 1:
                        pe.wait_ge(filled.sem, i * unroll + (filled.base + b + 1))
                        pe.sem_inc(K.w_used.sem, 1)

        @block.vector
        def _(dve):
            for s in range(4):
                dve.sem_inc(free[s].sem, 1)
            with dve.Fori(0, KD // unroll) as i:
                for b in range(unroll):
                    dve.wait_ge(filled.sem, i * unroll + (filled.base + b + 1))
                    for j, (a, e) in enumerate(parts):
                        x = K.xT[:, bass.ds(i * unroll + b, 1), a:e].rearrange("p o t -> p (o t)")
                        if gate is None:
                            op = nc.vector.tensor_tensor(x, K.pairs[b % 4][:, a:e], x, ALU.add)
                        else:
                            g = K.mod[:, bass.ds(i * unroll + (gate * KD + b), 1), j:j + 1].rearrange("p o t -> p (o t)")
                            op = nc.vector.scalar_tensor_tensor(x, K.pairs[b % 4][:, a:e], g, x, ALU.mult, ALU.add)
                    op.then_inc(free[b % 4].sem, 1)
    filled.base += KD
    for s in range(4):
        free[s].base += 1 + KD // 4


def ring_turns(eng, count, body, last_differs=False):
    groups = (count - last_differs) // RING
    rest = count - groups * RING
    if groups > 1:
        with eng.Fori(0, groups) as i:
            for s in range(RING):
                body(i, s)
    else:
        for s in range(groups * RING):
            body(0, s)
    for s in range(rest):
        body(groups, s)


def ffn_up_stage(K, layer, part, tokens, h_high, h_low, high, low):
    nc = K.nc
    name = f"w_up{layer}_{part}"
    first, kt, at = K.first(name), HIDDEN_PARTS[layer][part], sum(HIDDEN_PARTS[layer][:part])
    parts = spans(tokens)
    conv = layer < 2
    gate_done, value_done, tap_ready, silu_ready, high_done = K.pe_a, K.pe_b, K.act_a, K.act_b, K.act_c
    conv_ready, hidden_ready, low_done = K.dve_a, K.dve_b, K.dve_d
    gate_read = conv_ready if conv else silu_ready
    one = lambda ap: ap.rearrange("p o t -> p (o t)")
    with ExitStack() as stack:
        gate = stack.enter_context(K.temp("gate", [P, 2, ALL]))
        block = stack.enter_context(nc.Block())

        @block.sync
        def _(sp):
            K.stream(sp, [name])

        @block.tensor
        def _(pe):
            def body(i, s):
                for half, read, done in ((0, gate_read, gate_done), (1, hidden_ready, value_done)):
                    pe.wait_ge(read.sem, i * RING + (read.base + s + 1))
                    K.product(pe, K.pairs[2 * (s % 2) + half], first + s, KD, 256, half, h_high, h_low, tokens,
                              i).then_inc(done.sem, 1)
            ring_turns(pe, kt, body)

        @block.scalar
        def _(act):
            if not conv:
                act.sem_inc(silu_ready.sem, 2)
            act.sem_inc(high_done.sem, 1)

            def body(i, s):
                act.wait_ge(value_done.sem, i * RING + (value_done.base + s))
                K.split_high(act, first + s + 1, i)
                act.wait_ge(gate_done.sem, i * RING + (gate_done.base + s + 1))
                act.wait_ge(low_done.sem, i * RING + (low_done.base + s + 1))
                ps = K.pairs[2 * (s % 2)]
                g = gate[:, s % 2, 0:tokens]
                if conv:
                    middle = K.vec[:, bass.ds(i * RING + (VEC[f"fcw{layer}"][0] + KF + at + s), 1)]
                    bias = K.vec[:, bass.ds(i * RING + (VEC[f"fcb{layer}"][0] + at + s), 1)]
                    nc.scalar.activation(g, ps[:, 0:tokens], ACT.Identity, bias=bias,
                                         scale=middle).then_inc(tap_ready.sem, 1)
                    act.wait_ge(conv_ready.sem, i * RING + (conv_ready.base + s + 3))
                    nc.scalar.activation(g, g, ACT.Silu).then_inc(silu_ready.sem, 1)
                else:
                    nc.scalar.activation(g, ps[:, 0:tokens], ACT.Silu).then_inc(silu_ready.sem, 1)
                act.wait_ge(hidden_ready.sem, i * RING + (hidden_ready.base + s + 3))
                nc.scalar.activation(one(high[:, bass.ds(i * RING + s, 1), 0:tokens]), g,
                                     ACT.Copy).then_inc(high_done.sem, 1)
            ring_turns(act, kt, body, last_differs=True)

        @block.vector
        def _(dve):
            dve.sem_inc(hidden_ready.sem, 2)
            dve.sem_inc(low_done.sem, 2)
            if conv:
                dve.sem_inc(conv_ready.sem, 2)

            def body(i, s):
                K.split_low(dve, first + s + 1, i)
                ps = K.pairs[2 * (s % 2)]
                g = gate[:, s % 2, :]
                if conv:
                    taps = VEC[f"fcw{layer}"][0] + at
                    before = K.vec[:, bass.ds(i * RING + (taps + s), 1)]
                    after = K.vec[:, bass.ds(i * RING + (taps + 2 * KF + s), 1)]
                    dve.wait_ge(tap_ready.sem, i * RING + (tap_ready.base + s + 1))
                    for a, e in parts:
                        op = nc.vector.scalar_tensor_tensor(g[:, a + 1:e], ps[:, a:e - 1], before,
                                                            g[:, a + 1:e], ALU.mult, ALU.add)
                    op.then_inc(K.dve_c.sem, 1)
                    dve.wait_ge(K.dve_c.sem, i * RING + (K.dve_c.base + s + 1))
                    for a, e in parts:
                        op = nc.vector.scalar_tensor_tensor(g[:, a:e - 1], ps[:, a + 1:e], after,
                                                            g[:, a:e - 1], ALU.mult, ALU.add)
                    op.then_inc(conv_ready.sem, 1)
                dve.wait_ge(silu_ready.sem, i * RING + (silu_ready.base + s + (1 if conv else 3)))
                dve.wait_ge(value_done.sem, i * RING + (value_done.base + s + 1))
                nc.vector.tensor_tensor(g[:, 0:tokens], g[:, 0:tokens], K.pairs[2 * (s % 2) + 1][:, 0:tokens],
                                        ALU.mult).then_inc(hidden_ready.sem, 1)
                dve.wait_ge(hidden_ready.sem, i * RING + (hidden_ready.base + s + 3))
                dve.wait_ge(high_done.sem, i * RING + (high_done.base + s + 2))
                tile = bass.ds(i * RING + s, 1)
                nc.vector.tensor_tensor(one(low[:, tile, 0:tokens]), g[:, 0:tokens],
                                        one(high[:, tile, 0:tokens]).bitcast(F32), ALU.subtract).then_inc(low_done.sem, 1)
            ring_turns(dve, kt, body, last_differs=True)
    gate_done.base += kt
    value_done.base += kt
    hidden_ready.base += kt + 2
    low_done.base += kt + 2
    high_done.base += kt + 1
    if conv:
        tap_ready.base += kt
        conv_ready.base += kt + 2
        K.dve_c.base += kt
        silu_ready.base += kt
    else:
        silu_ready.base += kt + 2


def residual_split_stage(K, name, high, low, kt, per, tokens, gate):
    nc = K.nc
    first = K.first(name)
    parts = spans(tokens)
    filled, free = K.pe_a, K.free
    with nc.Block() as block:
        @block.sync
        def _(sp):
            K.stream(sp, [name])

        @block.tensor
        def _(pe):
            def body(i, s):
                for b in range(s * per, s * per + per):
                    pe.wait_ge(free[b % 4].sem, i * per + (free[b % 4].base + b // 4 + 1))
                    K.product(pe, K.pairs[b % 4], first + s, kt, per * P, b % per, high, low, tokens,
                              i).then_inc(filled.sem, 1)
            ring_turns(pe, KD // per, body)

        @block.scalar
        def _(act):
            def body(i, s):
                act.wait_ge(filled.sem, i * (RING * per) + (filled.base + s * per))
                K.split_high(act, first + s + 1, i)
            ring_turns(act, KD // per, body, last_differs=True)

        @block.vector
        def _(dve):
            for s in range(4):
                dve.sem_inc(free[s].sem, 1)

            def body(i, s):
                K.split_low(dve, first + s + 1, i)
                for b in range(s * per, s * per + per):
                    dve.wait_ge(filled.sem, i * (RING * per) + (filled.base + b + 1))
                    for j, (a, e) in enumerate(parts):
                        x = K.xT[:, bass.ds(i * (RING * per) + b, 1), a:e].rearrange("p o t -> p (o t)")
                        if gate is None:
                            op = nc.vector.tensor_tensor(x, K.pairs[b % 4][:, a:e], x, ALU.add)
                        else:
                            m = K.mod[:, bass.ds(i * (RING * per) + (gate * KD + b), 1), j:j + 1]
                            op = nc.vector.scalar_tensor_tensor(x, K.pairs[b % 4][:, a:e],
                                                                m.rearrange("p o t -> p (o t)"), x, ALU.mult, ALU.add)
                    op.then_inc(free[b % 4].sem, 1)
            ring_turns(dve, KD // per, body, last_differs=True)
    filled.base += KD
    for s in range(4):
        free[s].base += 1 + KD // 4


def ffn(K, layer, tokens, gate, gain, scale=None, shift=None):
    with K.split_weights(), K.temp("h_high", [P, KD, tokens], F32R) as h_high, \
            K.temp("h_low", [P, KD, tokens], F32R) as h_low:
        norm_split_stage(K, h_high, h_low, tokens, gain, scale, shift, K.first(f"w_up{layer}_0"))
        most = max(HIDDEN_PARTS[layer])
        with K.temp("high", [P, most, tokens], F32R) as high, K.temp("low", [P, most, tokens], F32R) as low:
            for part, kt in enumerate(HIDDEN_PARTS[layer]):
                ffn_up_stage(K, layer, part, tokens, h_high, h_low, high, low)
                residual_split_stage(K, f"w_down{layer}_{part}", high, low, kt, down_blocks(kt), tokens, gate)


def heads_stage(K, names, tiles, tokens, tables, rot):
    nc = K.nc
    parts = spans(tokens)
    n = len(tiles)
    raw_done, stat_done, rot_done = K.pe_a, K.pe_b, K.pe_c
    sq_ready, std_ready = K.act_a, K.act_b
    gained, normed, sin_ready = K.dve_a, K.dve_b, K.dve_c
    rotated = K.pool_a
    normal = [t["gain"] is not None for t in tiles]
    roped = [t["rope"] for t in tiles]
    upto = lambda flags, j: sum(flags[:j + 1])
    stat, rots = K.pairs[2], K.pairs[3]
    last_of = {t["chunk"]: j for j, t in enumerate(tiles)}
    with ExitStack() as stack:
        sb = lambda name, shape: stack.enter_context(K.temp(name, shape))
        sq, std = sb("sq", [P, ALL]), sb("std", [P, ALL])
        y0, y1 = sb("y0", [P, 2, ALL]), sb("y1", [P, 3, ALL])
        ys = sb("ys", [P, LAT])
        trig = sb("trig", [P, 2, LAT])
        rotm = sb("rotm", [P, P])
        block = stack.enter_context(nc.Block())

        @block.sync
        def _(sp):
            sp.dma_start(trig[:], K.d[tables]).then_inc(K.loaded.sem, 16)
            sp.dma_start(rotm[:], K.d[rot]).then_inc(K.loaded.sem, 16)
            K.stream(sp, names)

        @block.tensor
        def _(pe):
            for j in range(n + 2):
                if j < n:
                    t = tiles[j]
                    if j == 0 or tiles[j - 1]["chunk"] != t["chunk"]:
                        K.wait_weights(pe, t["chunk"])
                    if j >= 2:
                        pe.wait_ge(gained.sem, gained.base + j - 1)
                        if normal[j - 2]:
                            pe.wait_ge(sq_ready.sem, sq_ready.base + upto(normal, j - 2))
                    for a, e in parts:
                        for m, (lhs, rhs) in enumerate(t["mms"]):
                            mm = nc.tensor.matmul(K.pairs[j % 2][0:t["rows"], a:e], lhs, rhs(a, e),
                                                  start=m == 0, stop=m == len(t["mms"]) - 1)
                    mm.then_inc(raw_done.sem, 1)
                    if last_of[t["chunk"]] == j:
                        pe.wait_ge(raw_done.sem, raw_done.base + j + 1)
                        pe.sem_inc(K.w_used.sem, 1)
                if 1 <= j <= n and normal[j - 1]:
                    t, r = tiles[j - 1], tiles[j - 1]["rows"]
                    pe.wait_ge(sq_ready.sem, sq_ready.base + upto(normal, j - 1))
                    if upto(normal, j - 1) > 1:
                        pe.wait_ge(std_ready.sem, std_ready.base + upto(normal, j - 1) - 1)
                    for a, e in parts:
                        mm = nc.tensor.matmul(stat[0:r, a:e], t["sums"], sq[0:r, a:e], start=True, stop=True)
                    mm.then_inc(stat_done.sem, 1)
                if j >= 2 and roped[j - 2]:
                    t, r = tiles[j - 2], tiles[j - 2]["rows"]
                    if upto(roped, j - 2) == 1:
                        pe.wait_ge(K.loaded.sem, K.loaded.base + 32)
                    else:
                        pe.wait_ge(sin_ready.sem, sin_ready.base + upto(roped, j - 2) - 1)
                    pe.wait_ge(normed.sem, normed.base + j - 1)
                    nc.tensor.matmul(rots[0:r, 0:LAT], rotm[0:r, 0:r], y1[0:r, (j - 2) % 3, 0:LAT],
                                     start=True, stop=True).then_inc(rot_done.sem, 1)

        @block.scalar
        def _(act):
            for j in range(n + 1):
                if j < n and normal[j]:
                    r = tiles[j]["rows"]
                    act.wait_ge(gained.sem, gained.base + j + 1)
                    if upto(normal, j) > 1:
                        act.wait_ge(stat_done.sem, stat_done.base + upto(normal, j) - 1)
                    nc.scalar.activation(sq[0:r, 0:tokens], K.pairs[j % 2][0:r, 0:tokens],
                                         ACT.Square).then_inc(sq_ready.sem, 1)
                if j >= 1 and normal[j - 1]:
                    t, r = tiles[j - 1], tiles[j - 1]["rows"]
                    act.wait_ge(stat_done.sem, stat_done.base + upto(normal, j - 1))
                    if j >= 2:
                        act.wait_ge(normed.sem, normed.base + j - 1)
                    nc.scalar.activation(std[0:r, 0:tokens], stat[0:r, 0:tokens], ACT.Sqrt,
                                         bias=K.eps[0:r], scale=t["scale"]).then_inc(std_ready.sem, 1)

        @block.vector
        def _(dve):
            chain = Chain(dve, K.dve_chain)
            for j in range(n + 2):
                if j < n:
                    r = tiles[j]["rows"]
                    dve.wait_ge(raw_done.sem, raw_done.base + j + 1)
                    if j >= 2:
                        dve.wait_ge(normed.sem, normed.base + j - 1)
                    raw = K.pairs[j % 2][0:r, 0:tokens]
                    if normal[j]:
                        op = nc.vector.tensor_scalar(y0[0:r, j % 2, 0:tokens], raw, tiles[j]["gain"], None, ALU.mult)
                    else:
                        op = nc.vector.tensor_copy(y0[0:r, j % 2, 0:tokens], raw)
                    op.then_inc(gained.sem, 1)
                if 1 <= j <= n:
                    t, r, b = tiles[j - 1], tiles[j - 1]["rows"], (j - 1) % 3
                    if normal[j - 1]:
                        dve.wait_ge(std_ready.sem, std_ready.base + upto(normal, j - 1))
                        chain.step(nc.vector.reciprocal(std[0:r, 0:tokens], std[0:r, 0:tokens]))
                        chain.sync()
                    else:
                        dve.wait_ge(gained.sem, gained.base + j)
                    if j >= 4 and roped[j - 4]:
                        dve.wait_ge(rotated.sem, rotated.base + upto(roped, j - 4))
                    to = y1[0:r, b, 0:tokens] if t["rope"] else t["dst"]
                    if normal[j - 1]:
                        op = nc.vector.tensor_tensor(to, y0[0:r, (j - 1) % 2, 0:tokens], std[0:r, 0:tokens], ALU.mult)
                    else:
                        op = nc.vector.tensor_copy(to, y0[0:r, (j - 1) % 2, 0:tokens])
                    op.then_inc(normed.sem, 1)
                if j >= 2 and roped[j - 2]:
                    r = tiles[j - 2]["rows"]
                    dve.wait_ge(rot_done.sem, rot_done.base + upto(roped, j - 2))
                    if upto(roped, j - 2) > 1:
                        dve.wait_ge(rotated.sem, rotated.base + upto(roped, j - 2) - 1)
                    nc.vector.tensor_tensor(ys[0:r, :], rots[0:r, 0:LAT], trig[0:r, 1, :],
                                            ALU.mult).then_inc(sin_ready.sem, 1)
            chain.close()

        @block.gpsimd
        def _(pool):
            chain = Chain(pool, K.pool_chain)
            pool.wait_ge(K.loaded.sem, K.loaded.base + 32)
            for j in range(n):
                if not roped[j]:
                    continue
                t, r, b = tiles[j], tiles[j]["rows"], j % 3
                pool.wait_ge(normed.sem, normed.base + j + 1)
                if tokens > LAT:
                    chain.step(nc.gpsimd.tensor_copy(t["dst"][:, LAT:tokens], y1[0:r, b, LAT:tokens]))
                chain.step(nc.gpsimd.tensor_tensor(t["dst"][:, 0:LAT], y1[0:r, b, 0:LAT], trig[0:r, 0, :], ALU.mult))
                chain.sync()
                pool.wait_ge(sin_ready.sem, sin_ready.base + upto(roped, j))
                nc.gpsimd.tensor_tensor(t["dst"][:, 0:LAT], t["dst"][:, 0:LAT], ys[0:r, :],
                                        ALU.add).then_inc(rotated.sem, 1)
            chain.close()
    K.loaded.base += 32
    for c in (raw_done, gained, normed):
        c.base += n
    for c in (stat_done, sq_ready, std_ready):
        c.base += sum(normal)
    for c in (rot_done, sin_ready, rotated):
        c.base += sum(roped)


def token_major_stage(K, names, jobs, ones=None, on_pool=None):
    nc = K.nc
    filled, free = K.pe_a, K.free
    with nc.Block() as block:
        @block.sync
        def _(sp):
            K.stream(sp, names)

        @block.tensor
        def _(pe):
            for j, (chunk, last, mms, cols, dst) in enumerate(jobs):
                if j == 0 or jobs[j - 1][0] != chunk:
                    K.wait_weights(pe, chunk)
                if j >= 4:
                    pe.wait_ge(free[j % 4].sem, free[j % 4].base + j // 4)
                for m, (lhs, rhs) in enumerate(mms):
                    mm = nc.tensor.matmul(K.pairs[j % 4][:, 0:cols], lhs, rhs, start=m == 0, stop=m == len(mms) - 1)
                mm.then_inc(filled.sem, 1)
                if last:
                    pe.wait_ge(filled.sem, filled.base + j + 1)
                    pe.sem_inc(K.w_used.sem, 1)

        if on_pool is not None:
            block.gpsimd(on_pool)

        def source(j):
            ps = K.pairs[j % 4][:, 0:jobs[j][3]]
            shape = jobs[j][4].shape
            return ps.rearrange("p (h c) -> p h c", h=shape[1]) if len(shape) == 3 else ps

        @block.scalar
        def _(act):
            for j in range(0, len(jobs), 2):
                act.wait_ge(filled.sem, filled.base + j + 1)
                nc.scalar.activation(jobs[j][4], source(j), ACT.Copy).then_inc(free[j % 4].sem, 1)

        @block.vector
        def _(dve):
            if ones is not None:
                nc.vector.memset(ones, 1.0)
            for j in range(1, len(jobs), 2):
                dve.wait_ge(filled.sem, filled.base + j + 1)
                nc.vector.tensor_copy(jobs[j][4], source(j)).then_inc(free[j % 4].sem, 1)
    filled.base += len(jobs)
    for s in range(4):
        free[s].base += len(range(s, len(jobs), 4))


def attention_stage(K, turns, steps_of, stage_q=None, stage_steps=0):
    nc = K.nc
    scored, transposed, summed = K.pe_a, K.pe_b, K.pe_c
    maxed, copied, out_ready, biased = K.dve_a, K.dve_b, K.dve_c, K.dve_d
    exped, staged = K.act_a, K.pool_a
    probe = steps_of(0)
    n = len(probe)
    assert n % 4 == 0 or turns == 1
    with_bias = "bias" in probe[0]
    pt = K.pairs[2]
    with ExitStack() as stack:
        sb = lambda name, shape: stack.enter_context(K.temp(name, shape))
        width = max(s["nk"] for s in probe)
        prob, probT = sb("prob", [P, 2, width]), sb("probT", [P, 2, width])
        scores = sb("scores", [P, 2, width]) if with_bias else None
        stats = sb("stats", [P, 3, 4])
        block = stack.enter_context(nc.Block())

        def loop(eng, body):
            if turns == 1:
                body(0)
            else:
                with eng.Fori(0, turns) as i:
                    body(i)

        if stage_q is not None:
            @block.gpsimd
            def _(pool):
                pool.sem_inc(scored.sem, 1)

                chain = Chain(pool, K.pool_chain)
                with chain.loop(turns, stage_steps) as i:
                    pool.wait_ge(scored.sem, i * n + (scored.base + 1))
                    stage_q(chain, i).then_inc(staged.sem, 1)
                chain.close()
        lead = 0 if stage_q is None else 1

        @block.tensor
        def _(pe):
            def body(i):
                steps = steps_of(i)
                if stage_q is not None:
                    pe.wait_ge(staged.sem, i + (staged.base + 1))
                for m in range(n + 2):
                    if m < n:
                        s = steps[m]
                        for at, rhs in s["keys"]:
                            mm = nc.tensor.matmul(K.pairs[m % 2][:, at:at + rhs.shape[-1]], s["q"], rhs,
                                                  start=True, stop=True)
                        mm.then_inc(scored.sem, 1)
                    if m >= 2:
                        j = m - 2
                        pe.wait_ge(copied.sem, i * n + (copied.base + j + 1))
                        tiles = steps[j]["v"]
                        for c, v in enumerate(tiles):
                            mm = nc.tensor.matmul(K.pairs[3][:, 512 * (j % 2):512 * (j % 2) + P],
                                                  probT[:, j % 2, c * P:c * P + P], v,
                                                  start=c == 0, stop=c == len(tiles) - 1)
                        mm.then_inc(summed.sem, 1)
                    if 1 <= m <= n:
                        j = m - 1
                        pe.wait_ge(exped.sem, i * n + (exped.base + j + 1))
                        for c in range(steps[j]["nk"] // P):
                            mm = nc.tensor.transpose(pt[:, c * P:c * P + P], prob[:, j % 2, c * P:c * P + P], K.ident[:])
                        mm.then_inc(transposed.sem, 1)
            loop(pe, body)

        @block.scalar
        def _(act):
            def body(i):
                for m, s in enumerate(steps_of(i)):
                    act.wait_ge(maxed.sem, i * n + (maxed.base + m + 1))
                    lo = s["keys"][0][0]
                    src = scores[:, m % 2, 0:s["nk"]] if with_bias else K.pairs[m % 2][:, lo:lo + s["nk"]]
                    nc.scalar.activation(prob[:, m % 2, 0:s["nk"]], src, ACT.Exp, bias=stats[:, 0, m % 4:m % 4 + 1],
                                         accum_out=stats[:, 1, m % 4:m % 4 + 1]).then_inc(exped.sem, 1)
            loop(act, body)

        @block.vector
        def _(dve):
            chain = Chain(dve, K.dve_chain)

            def body(i):
                steps = steps_of(i)
                for m in range(n + 2):
                    if m < n:
                        s = steps[m]
                        dve.wait_ge(scored.sem, i * n + (scored.base + lead + m + 1))
                        lo = s["keys"][0][0]
                        src = K.pairs[m % 2][:, lo:lo + s["nk"]]
                        if with_bias:
                            to = scores[:, m % 2, 0:s["nk"]]
                            chain.step(nc.vector.tensor_tensor(to, src, s["bias"], ALU.add))
                            chain.sync()
                            src = to
                        nc.vector.tensor_reduce(stats[:, 0, m % 4:m % 4 + 1], src, AX.X, ALU.max,
                                                negate=True).then_inc(maxed.sem, 1)
                    if 1 <= m <= n:
                        j = m - 1
                        dve.wait_ge(transposed.sem, i * n + (transposed.base + j + 1))
                        nk = steps[j]["nk"]
                        nc.vector.tensor_copy(probT[:, j % 2, 0:nk], pt[:, 0:nk]).then_inc(copied.sem, 1)
                    if m >= 2:
                        j = m - 2
                        dve.wait_ge(summed.sem, i * n + (summed.base + j + 1))
                        chain.step(nc.vector.reciprocal(stats[:, 2, j % 4:j % 4 + 1], stats[:, 1, j % 4:j % 4 + 1]))
                        chain.sync()
                        nc.vector.tensor_scalar(steps[j]["out"], K.pairs[3][:, steps[j]["col"](512 * (j % 2))],
                                                stats[:, 2, j % 4:j % 4 + 1], None, ALU.mult).then_inc(out_ready.sem, 1)
            if turns == 1:
                body(0)
            else:
                with chain.loop(turns, n * (2 if with_bias else 1)) as i:
                    body(i)
            chain.close()
    for c in (transposed, summed, maxed, copied, out_ready, exped):
        c.base += n * turns
    scored.base += n * turns + lead
    if stage_q is not None:
        staged.base += turns


def untoken_stage(K, src, dst, tiles_k, tiles_t):
    nc = K.nc
    filled, free = K.pe_a, K.free
    width = tiles_t * P
    with nc.Block() as block:
        @block.tensor
        def _(pe):
            for k in range(tiles_k):
                if k >= 4:
                    pe.wait_ge(free[k % 4].sem, free[k % 4].base + k // 4)
                for t in range(tiles_t):
                    mm = nc.tensor.transpose(K.pairs[k % 4][:, t * P:t * P + P], src[:, t, k * P:k * P + P], K.ident[:])
                mm.then_inc(filled.sem, 1)

        @block.scalar
        def _(act):
            for k in range(0, tiles_k, 2):
                act.wait_ge(filled.sem, filled.base + k + 1)
                nc.scalar.activation(dst[:, k, 0:width], K.pairs[k % 4][:, 0:width], ACT.Copy).then_inc(free[k % 4].sem, 1)

        @block.vector
        def _(dve):
            for k in range(1, tiles_k, 2):
                dve.wait_ge(filled.sem, filled.base + k + 1)
                nc.vector.tensor_copy(dst[:, k, 0:width], K.pairs[k % 4][:, 0:width]).then_inc(free[k % 4].sem, 1)
    filled.base += tiles_k
    for s in range(4):
        free[s].base += len(range(s, tiles_k, 4))



def mix0(K):
    nc = K.nc
    ada_stage(K, 0)
    norm_stage(K, K.xT, K.hT, KD, ALL, K.v("norm1_0", 0, 8), scale=1, shift=0)
    with ExitStack() as outer:
        sb = lambda name, shape: outer.enter_context(K.temp(name, shape))
        kT = sb("kT", [96, 8, ALL])
        gqT, gkT = sb("gqT", [P, 4, ALL]), sb("gkT", [P, 2, ALL])
        val = sb("val", [P, 6, 640])
        qT = K.xT
        with K.temp("low", [P, 6, ALL]) as low:
            def store(b):
                if b % 2 == 0:
                    return "act", lambda act, ps: nc.scalar.activation(low[:, b, :], ps[:, 0:ALL], ACT.Copy)
                return "dve", lambda chain, ps: nc.vector.tensor_copy(low[:, b, :], ps[:, 0:ALL])
            project_stage(K, ["w_att_lo"], K.hT, ALL, 6, store)
            first = K.first("w_att_gqa")
            tiles = []
            for b in range(6):
                w = K.slot(first + b // 2, KD, 256)
                tiles.append(dict(
                    chunk=first + b // 2, rows=P, sums=K.ones64[:], scale=1 / 64, rope=True,
                    mms=[(w[:, k, b % 2 * P:b % 2 * P + P], lambda a, e, k=k: K.hT[:, k, a:e]) for k in range(KD)],
                    gain=K.qgain[:, 1:2] if b < 4 else K.v("gk_g"), dst=gqT[:, b, :] if b < 4 else gkT[:, b - 4, :]))
            heads_stage(K, ["w_att_gqa"], tiles, ALL, "trig_gqa", "rot_gqa")
            g = K.first("w_gv")
            token_major_stage(K, ["w_gv"], [
                (g, t == 5, [(K.hT[:, k, t * P:t * P + P], K.slot(g, KD, P)[:, k, :]) for k in range(KD)],
                 P, val[:, t, 512:640]) for t in range(6)])
            norm_stage(K, low, low, 3, ALL, K.v("qa_g", 0, 3))
            norm_stage(K, low[:, 3:5, :], low[:, 3:5, :], 2, ALL, K.v("kva_g", 0, 2))
            gq, gkv = K.first("w_qb"), K.first("w_kvb")
            tiles = []
            for h in range(8):
                tiles.append(dict(
                    chunk=gq + h // 4, rows=96, sums=K.ones[0:96, 0:96], scale=1 / 96, rope=True, gain=K.qgain[0:96, 0:1],
                    mms=[(K.slot(gq + h // 4, 3, 384)[:, k, h % 4 * 96:h % 4 * 96 + 96], lambda a, e, k=k: low[:, k, a:e]) for k in range(3)],
                    dst=qT[0:96, h, :]))
            for h in range(8):
                tiles.append(dict(
                    chunk=gkv, rows=96, sums=K.ones[0:96, 0:96], scale=1 / 96, rope=True, gain=K.v("mk_g", rows=96),
                    mms=[(K.slot(gkv, 2, 768)[:, k, h * 96:h * 96 + 96], lambda a, e, k=k: low[:, 3 + k, a:e])
                         for k in range(2)] + [(K.ident[:, 0:96], lambda a, e: low[:, 5, a:e])],
                    dst=kT[:, h, :]))
            heads_stage(K, ["w_qb", "w_kvb"], tiles, ALL, "trig_mla", "rot_mla")
            g = K.first("w_va")
            token_major_stage(K, ["w_va"], [
                (g, t == 5, [(low[:, 3 + k, t * P:t * P + P], K.slot(g, 2, 512)[:, k, :]) for k in range(2)],
                 512, val[:, t, 0:512]) for t in range(6)])
        mixed = K.hT[:].rearrange("p k t -> p (k t)").rearrange("p (t c) -> p t c", t=6)
        order = [0, 1, 2, 3, 4, 5]
        with K.temp("qs", [P, 4, ALL]) as qs, K.temp("ks", [P, ALL]) as ks:
            one = lambda ap: ap.rearrange("p o t -> p (o t)")

            def step(t, q, key, v, col, out):
                lat = t < 4
                return dict(q=q, col=col, nk=ALL if lat else CTX, out=out,
                            keys=[(0, key(0, LAT)), (LAT, key(LAT, ALL))] if lat else [(0, key(LAT, ALL))],
                            v=[v(c) for c in (range(6) if lat else range(4, 6))])

            def mla_steps(i):
                steps = []
                for b in range(2):
                    for t in order:
                        steps.append(step(
                            t, qs[0:96, b, t * P:t * P + P],
                            lambda a, e, b=b: one(kT[:, bass.ds(i * 2 + b, 1), a:e]),
                            lambda c: val[:, c, bass.ds(i * 128, 128)],
                            lambda at, b=b: slice(at + 64 * b, at + 64 * b + 64),
                            mixed[:, t, bass.ds(i * 128 + b * 64, 64)]))
                return steps

            def mla_stage(chain, i):
                return nc.gpsimd.tensor_copy(qs[0:96, 0:2, :], qT[0:96, bass.ds(i * 2, 2), :])
            attention_stage(K, 4, mla_steps, mla_stage)

            def gqa_steps(i):
                steps = []
                for b in range(2):
                    for half in range(2):
                        for t in order:
                            steps.append(step(
                                t, qs[:, 2 * b + half, t * P:t * P + P],
                                lambda a, e: ks[:, a:e],
                                lambda c: val[:, c, 512:640],
                                lambda at: bass.ds(i * 64 + at, 64),
                                mixed[:, t, bass.ds(i * 256 + (512 + b * 128 + half * 64), 64)]))
                return steps

            def gqa_stage(chain, i):
                chain.step(nc.gpsimd.tensor_copy(ks[:], one(gkT[:, bass.ds(i, 1), :])))
                for half in range(2):
                    r = slice(64 * half, 64 * half + 64)
                    chain.sync()
                    op = nc.gpsimd.tensor_copy(qs[r, half::2, :], gqT[r, bass.ds(i * 2, 2), :])
                    if half == 0:
                        chain.step(op)
                return op
            with nc.Block() as block:
                @block.vector
                def _(dve):
                    for half in range(2):
                        nc.vector.memset(qs[64 - 64 * half:128 - 64 * half, half::2, :], 0.0)
            attention_stage(K, 2, gqa_steps, gqa_stage, 2)
    with K.temp("mixT", [P, KD, ALL]) as mixT:
        untoken_stage(K, mixed, mixT, KD, 6)
        reload_x_stage(K)
        residual_stage(K, "w_att_out", mixT, KD, ALL, 2)


def layer0(K):
    with K.activations():
        mix0(K)
    ffn(K, 0, ALL, 5, K.v("norm2_0", 0, 8), scale=4, shift=3)



def gate_stage(K, keysT, floorT, top):
    nc = K.nc
    g = K.first("w_ml_gate")
    w = K.slot(g, KD, P)
    R = 64
    with ExitStack() as stack:
        sb = lambda name, shape: stack.enter_context(K.temp(name, shape))
        gi, gx, soft, run = (sb(n, [R, ALL]) for n in ("gi", "gx", "soft", "run"))
        zero, high = sb("zero", [R, ALL]), sb("high", [R, ALL])
        block = stack.enter_context(nc.Block())

        @block.sync
        def _(sp):
            K.stream(sp, ["w_ml_gate"])

        @block.tensor
        def _(pe):
            K.wait_weights(pe, g)
            for half in range(2):
                for a, e in spans(ALL):
                    for k in range(KD):
                        mm = nc.tensor.matmul(K.pairs[half][0:R, a:e], w[:, k, half * R:half * R + R],
                                              K.hT[:, k, a:e], start=k == 0, stop=k == KD - 1)
            mm.then_inc(K.pe_a.sem, 1)
            pe.wait_ge(K.pe_a.sem, K.pe_a.base + 1)
            pe.sem_inc(K.w_used.sem, 1)
            pe.wait_ge(K.dve_b.sem, K.dve_b.base + 1)
            for t in range(6):
                mm = nc.tensor.transpose(K.pairs[2][:, t * R:t * R + R], gi[:, t * P:t * P + P], K.ident[0:R, 0:R])
            mm.then_inc(K.pe_b.sem, 1)
            pe.wait_ge(K.act_b.sem, K.act_b.base + 1)
            for t in range(4):
                mm = nc.tensor.transpose(K.pairs[3][:, t * R:t * R + R], soft[:, t * P:t * P + P], K.ident[0:R, 0:R])
            mm.then_inc(K.pe_b.sem, 1)

        @block.scalar
        def _(act):
            chain = Chain(act, K.act_chain)
            act.wait_ge(K.dve_a.sem, K.dve_a.base + 1)
            chain.step(nc.scalar.activation(soft[:], gx[:], ACT.Abs))
            chain.sync()
            chain.step(nc.scalar.activation(soft[:], soft[:], ACT.Exp, scale=-1.0))
            chain.sync()
            nc.scalar.activation(soft[:], soft[:], ACT.Ln, bias=K.ones[0:R, 0:1]).then_inc(K.act_a.sem, 1)
            act.wait_ge(K.dve_c.sem, K.dve_c.base + 1)
            nc.scalar.activation(soft[:, 0:LAT], gx[:, 0:LAT], ACT.Exp, scale=-1.0).then_inc(K.act_b.sem, 1)
            chain.close()

        @block.vector
        def _(dve):
            chain = Chain(dve, K.dve_chain)
            chain.step(nc.vector.memset(zero[:], 0.0))
            dve.wait_ge(K.pe_a.sem, K.pe_a.base + 1)
            chain.step(nc.vector.tensor_scalar(gi[:], K.pairs[0][0:R, 0:ALL], K.v("gate_i", rows=R), None, ALU.add))
            nc.vector.tensor_scalar(gx[:], K.pairs[1][0:R, 0:ALL], K.v("gate_f", rows=R), None,
                                    ALU.add).then_inc(K.dve_a.sem, 1)
            dve.wait_ge(K.act_a.sem, K.act_a.base + 1)
            chain.step(nc.vector.scalar_tensor_tensor(gx[:], gx[:], 0.0, soft[:], ALU.min, ALU.subtract))
            chain.sync()

            def scan(out, data, op):
                for r, rev in ((slice(0, 32), 1), (slice(32, 64), -1)):
                    part = lambda x, a, e: x[r, a:e] if rev == 1 else x[r, a:e][:, ::-1]
                    chain.step(nc.vector.tensor_tensor_scan(part(out, LAT, ALL), part(zero, LAT, ALL),
                                                            part(data, LAT, ALL), 0.0, ALU.add, op))
                chain.sync()
                for r, rev, last in ((slice(0, 32), 1, ALL - 1), (slice(32, 64), -1, LAT)):
                    part = lambda x, a, e: x[r, a:e] if rev == 1 else x[r, a:e][:, ::-1]
                    chain.step(nc.vector.tensor_tensor_scan(part(out, 0, LAT), part(zero, 0, LAT), part(data, 0, LAT),
                                                            out[r, last:last + 1], ALU.add, op))
                chain.sync()

            scan(run, gx, ALU.add)
            nc.vector.tensor_tensor(gi[:], gi[:], run[:], ALU.subtract).then_inc(K.dve_b.sem, 1)
            dve.wait_ge(K.dve_b.sem, K.dve_b.base + 1)
            scan(high, gi, ALU.max)
            chain.step(nc.vector.tensor_copy(top[:], high[:, 0:LAT]))
            nc.vector.tensor_tensor(gx[:, 0:LAT], high[:, 0:LAT], run[:, 0:LAT], ALU.add).then_inc(K.dve_c.sem, 1)
            dve.wait_ge(K.pe_b.sem, K.pe_b.base + 1)
            nc.vector.tensor_copy(keysT[:].rearrange("p t c -> p (t c)"), K.pairs[2][:, 0:6 * R])
            dve.wait_ge(K.pe_b.sem, K.pe_b.base + 2)
            nc.vector.tensor_copy(floorT[:].rearrange("p t c -> p (t c)"), K.pairs[3][:, 0:4 * R])
            chain.close()
    for c, n in ((K.pe_a, 1), (K.pe_b, 2), (K.dve_a, 1), (K.dve_b, 1), (K.dve_c, 1), (K.act_a, 1), (K.act_b, 1)):
        c.base += n


def conv_qk_stage(K, qT, kT):
    nc = K.nc
    first = K.first("w_ml_qk")
    done, tap, silu, conved = K.pe_a, K.act_a, K.act_b, K.dve_a
    cw, cb = VEC["mcw"][0], VEC["mcb"][0]
    parts_of = lambda b: [(0, LAT)] if b < 4 else spans(ALL)
    with ExitStack() as stack:
        buf = stack.enter_context(K.temp("buf", [P, 2, ALL]))
        block = stack.enter_context(nc.Block())

        @block.sync
        def _(sp):
            K.stream(sp, ["w_ml_qk"])

        @block.tensor
        def _(pe):
            for b in range(8):
                g = first + b // 2
                if b % 2 == 0:
                    K.wait_weights(pe, g)
                if b >= 4:
                    pe.wait_ge(conved.sem, conved.base + b - 3)
                for a, e in parts_of(b):
                    for k in range(KD):
                        mm = nc.tensor.matmul(K.pairs[b % 4][:, a:e], K.slot(g, KD, 256)[:, k, b % 2 * P:b % 2 * P + P],
                                              K.hT[:, k, a:e], start=k == 0, stop=k == KD - 1)
                mm.then_inc(done.sem, 1)
                if b % 2 == 1:
                    pe.wait_ge(done.sem, done.base + b + 1)
                    pe.sem_inc(K.w_used.sem, 1)

        @block.scalar
        def _(act):
            for b in range(8):
                n = parts_of(b)[-1][1]
                act.wait_ge(done.sem, done.base + b + 1)
                if b >= 2:
                    act.wait_ge(silu.sem, silu.base + b - 1)
                nc.scalar.activation(buf[:, b % 2, 0:n], K.pairs[b % 4][:, 0:n], ACT.Identity,
                                     bias=K.vec[:, cb + b:cb + b + 1],
                                     scale=K.vec[:, cw + 8 + b:cw + 9 + b]).then_inc(tap.sem, 1)
                act.wait_ge(conved.sem, conved.base + b + 1)
                dst = qT[:, b, :] if b < 4 else kT[:, b - 4, :]
                nc.scalar.activation(dst, buf[:, b % 2, 0:n], ACT.Silu).then_inc(silu.sem, 1)

        @block.vector
        def _(dve):
            chain = Chain(dve, K.dve_chain)
            for b in range(8):
                dve.wait_ge(tap.sem, tap.base + b + 1)
                ps = K.pairs[b % 4]
                for a, e in parts_of(b):
                    chain.step(nc.vector.scalar_tensor_tensor(
                        buf[:, b % 2, a + 1:e], ps[:, a:e - 1], K.vec[:, cw + b:cw + b + 1],
                        buf[:, b % 2, a + 1:e], ALU.mult, ALU.add))
                chain.sync()
                for a, e in parts_of(b):
                    op = nc.vector.scalar_tensor_tensor(
                        buf[:, b % 2, a:e - 1], ps[:, a + 1:e], K.vec[:, cw + 16 + b:cw + 17 + b],
                        buf[:, b % 2, a:e - 1], ALU.mult, ALU.add)
                op.then_inc(conved.sem, 1)
            chain.close()
    for c in (done, tap, silu, conved):
        c.base += 8


def mlstm_stage(K, qT, kT, keysT, floorT, top, val, sig, yT):
    nc = K.nc
    spread, scored, summed, turned = K.pe_a, K.pe_b, K.pe_c, K.pe_d
    weighed, rooted = K.act_a, K.act_b
    mixed, read, normed, diag_ready, out_ready = K.dve_a, K.dve_b, K.dve_c, K.dve_d, K.dve_e
    staged = K.pool_a
    order = [4, 5, 0, 1, 2, 3]
    one = lambda ap: ap.rearrange("p o t -> p (o t)")
    beyond = lambda s, d: (0, LAT) if s >= 4 else (((s + 1) * P, LAT) if d == 0 else (0, s * P))
    with ExitStack() as stack:
        sb = lambda name, shape: stack.enter_context(K.temp(name, shape))
        kS, qS, hot = sb("kS", [P, ALL]), sb("qS", [P, 2, LAT]), sb("hot", [64, 4])
        diag = sb("diag", [P, 2, 4, P])
        wgt = sb("wgt", [P, 2, 2, LAT])
        prob = sb("prob", [P, 2, 6, LAT])
        hs = lambda t: K.xT[:, t // 2, LAT + P * (t % 2):LAT + P * (t % 2) + P]
        hn, junk = K.rinv[:, P:5 * P].rearrange("p (t c) -> p t c", t=4), K.rinv[:, 0:P]
        den, ss = sb("den", [P, 2, 2]), sb("ss", [P, 4])
        causal = sb("causal", [P, 2, P])
        block = stack.enter_context(nc.Block())

        @block.sync
        def _(sp):
            sp.dma_start(causal[:], K.d["causal"]).then_inc(K.loaded.sem, 16)

        @block.gpsimd
        def _(pool):
            pool.sem_inc(scored.sem, 1)
            chain = Chain(pool, K.pool_chain)
            for b in range(2):
                chain.step(nc.gpsimd.memset(qS[64 - 64 * b:128 - 64 * b, b, :], 0.0))
                chain.sync()
            with chain.loop(4, 4) as i:
                pool.wait_ge(scored.sem, i * 12 + (scored.base + 1))
                chain.step(nc.gpsimd.tensor_copy(kS[:], one(kT[:, bass.ds(i, 1), :])))
                for b in range(2):
                    r = slice(64 * b, 64 * b + 64)
                    chain.sync()
                    chain.step(nc.gpsimd.tensor_copy(qS[r, b, :], one(qT[r, bass.ds(i, 1), :])))
                chain.sync()
                chain.step(nc.gpsimd.tensor_copy(hot[:, 0:2], K.ident[0:64, bass.ds(i * 2, 2)]))
                chain.sync()
                nc.gpsimd.tensor_copy(hot[:, 2:4], K.ident[0:64, bass.ds(i * 2 + 32, 2)]).then_inc(staged.sem, 1)
            chain.close()

        @block.tensor
        def _(pe):
            with pe.Fori(0, 4) as i:
                pe.wait_ge(staged.sem, i + (staged.base + 1))
                for b in range(2):
                    for d in range(2):
                        mm = nc.tensor.matmul(K.pairs[2][:, d * 512:d * 512 + LAT],
                                              hot[:, 2 * d + b:2 * d + b + 1].broadcast_to([64, P]), top[:],
                                              start=True, stop=True)
                    mm.then_inc(spread.sem, 1)
                    for j, s in enumerate(order):
                        pe.wait_ge(mixed.sem, i * 12 + (mixed.base + 6 * b + j + 1))
                        nc.tensor.matmul(K.pairs[0][:, 512 * (j % 2):512 * (j % 2) + LAT], kS[:, s * P:s * P + P],
                                         qS[:, b, :], start=True, stop=True).then_inc(scored.sem, 1)
                    pe.wait_ge(mixed.sem, i * 12 + (mixed.base + 6 * b + 8))
                    for j in range(4):
                        d, half = j % 2, j // 2
                        pe.wait_ge(read.sem, i * 8 + (read.base + 4 * b + j + 1))
                        for u in range(2):
                            t = 2 * half + u
                            keys = [4, 5] + (list(range(t + 1)) if d == 0 else list(range(t, 4)))
                            for n, s in enumerate(keys):
                                mm = nc.tensor.matmul(
                                    K.pairs[3][:, 512 * d + u * 129:512 * d + u * 129 + 129],
                                    prob[:, d, s, t * P:t * P + P], one(val[:, s, bass.ds(i * 2 + b, 1), :]),
                                    start=n == 0, stop=n == len(keys) - 1)
                        mm.then_inc(summed.sem, 1)
                    pe.wait_ge(normed.sem, i * 2 + (normed.base + b + 1))
                    for t in range(4):
                        mm = nc.tensor.transpose(K.pairs[1][:, t * P:t * P + P], hn[:, t, :], K.ident[:])
                    mm.then_inc(turned.sem, 1)

        @block.scalar
        def _(act):
            with act.Fori(0, 4) as i:
                for b in range(2):
                    act.wait_ge(diag_ready.sem, i * 2 + (diag_ready.base + b + 1))
                    flat = diag[:].rearrange("p d s t -> p (d s t)")
                    nc.scalar.activation(flat, flat, ACT.Exp, scale=-1.0)
                    for j, s in enumerate(order):
                        act.wait_ge(mixed.sem, i * 12 + (mixed.base + 6 * b + j + 1))
                        for d in range(2):
                            lo, hi = beyond(s, d)
                            if hi > lo:
                                op = nc.scalar.activation(wgt[:, j % 2, d, lo:hi], K.pairs[2][:, 512 * d + lo:512 * d + hi],
                                                          ACT.Exp, bias=one(keysT[:, s:s + 1, bass.ds(i * 2 + (32 * d + b), 1)]),
                                                          scale=-1.0)
                        op.then_inc(weighed.sem, 1)
                    act.wait_ge(read.sem, i * 8 + (read.base + 4 * b + 6))
                    for t in range(4):
                        nc.scalar.activation(junk, hs(t), ACT.Square, accum_out=ss[:, t:t + 1]).then_inc(K.act_c.sem, 1)
                        act.wait_ge(K.act_c.sem, i * 8 + (K.act_c.base + 4 * b + t + 1))
                    nc.scalar.activation(ss[:], ss[:], ACT.Sqrt, bias=K.eps[:], scale=1.0 / P).then_inc(rooted.sem, 1)

        @block.vector
        def _(dve):
            dve.sem_inc(mixed.sem, 2)
            dve.sem_inc(read.sem, 2)
            chain = Chain(dve, K.dve_chain)
            dve.wait_ge(K.loaded.sem, K.loaded.base + 16)
            with chain.loop(4, 2 * (3 * 4 + 1 + 3 + 1)) as i:
                for b in range(2):
                    dve.wait_ge(spread.sem, i * 2 + (spread.base + b + 1))
                    for d in range(2):
                        for s in range(4):
                            op = nc.vector.scalar_tensor_tensor(
                                diag[:, d, s, :], K.pairs[2][:, 512 * d + s * P:512 * d + s * P + P],
                                one(keysT[:, s:s + 1, bass.ds(i * 2 + (32 * d + b), 1)]), causal[:, d, :],
                                ALU.subtract, ALU.max)
                    op.then_inc(diag_ready.sem, 1)
                    for j, s in enumerate(order):
                        dve.wait_ge(scored.sem, i * 12 + (scored.base + 6 * b + j + 2))
                        dve.wait_ge(weighed.sem, i * 12 + (weighed.base + 6 * b + j + 1))
                        bank = 512 * (j % 2)
                        for d in range(2):
                            lo, hi = beyond(s, d)
                            if s < 4:
                                op = nc.vector.scalar_tensor_tensor(
                                    prob[:, d, s, s * P:s * P + P], K.pairs[0][:, bank + s * P:bank + s * P + P], 0.125,
                                    diag[:, d, s, :], ALU.mult, ALU.mult)
                            if hi > lo:
                                op = nc.vector.scalar_tensor_tensor(
                                    prob[:, d, s, lo:hi], K.pairs[0][:, bank + lo:bank + hi], 0.125,
                                    wgt[:, j % 2, d, lo:hi], ALU.mult, ALU.mult)
                        op.then_inc(mixed.sem, 1)
                    for j in range(4):
                        d, half = j % 2, j // 2
                        dve.wait_ge(summed.sem, i * 8 + (summed.base + 4 * b + j + 1))
                        ps = K.pairs[3][:, 512 * d:512 * d + 258].rearrange("p (u c) -> p u c", u=2)
                        total = ps[:, :, 128:129].rearrange("p u c -> p (u c)")
                        chain.step(nc.vector.scalar_tensor_tensor(
                            den[:, d, :], total, -1.0,
                            floorT[:, 2 * half:2 * half + 2, bass.ds(i * 2 + (32 * d + b), 1)].rearrange("p u c -> p (u c)"),
                            ALU.mult, ALU.max))
                        chain.sync()
                        chain.step(nc.vector.scalar_tensor_tensor(den[:, d, :], total, 1.0, den[:, d, :], ALU.mult, ALU.max))
                        chain.sync()
                        chain.step(nc.vector.reciprocal(den[:, d, :], den[:, d, :]))
                        chain.sync()
                        for u in range(2):
                            t = 2 * half + u
                            if d == 0:
                                op = nc.vector.tensor_scalar(hs(t), ps[:, u, 0:P], den[:, d, u:u + 1], None, ALU.mult)
                            else:
                                op = nc.vector.scalar_tensor_tensor(hs(t), ps[:, u, 0:P], den[:, d, u:u + 1],
                                                                    hs(t), ALU.mult, ALU.add)
                        op.then_inc(read.sem, 1)
                        if d == 0:
                            dve.wait_ge(read.sem, i * 8 + (read.base + 4 * b + j + 3))
                    dve.wait_ge(rooted.sem, i * 2 + (rooted.base + b + 1))
                    chain.step(nc.vector.reciprocal(ss[:], ss[:]))
                    chain.sync()
                    for t in range(4):
                        op = nc.vector.tensor_scalar(hn[:, t, :], hs(t), ss[:, t:t + 1], None, ALU.mult)
                        if t < 3:
                            chain.step(op)
                    op.then_inc(normed.sem, 1)
                    dve.wait_ge(turned.sem, i * 2 + (turned.base + b + 1))
                    head = bass.ds(i * 2 + b, 1)
                    chain.step(nc.vector.scalar_tensor_tensor(
                        one(yT[:, head, 0:LAT]), K.pairs[1][:, 0:LAT], K.vec[:, bass.ds(i * 2 + (VEC["out_g"][0] + b), 1)],
                        one(sig[:, head, :]), ALU.mult, ALU.mult))
                    chain.sync()
            chain.close()
    K.loaded.base += 16
    for c, n in ((spread, 8), (scored, 49), (summed, 32), (turned, 8), (weighed, 48), (rooted, 8), (K.act_c, 32),
                 (mixed, 50), (read, 34), (normed, 8), (diag_ready, 8), (staged, 4)):
        c.base += n


def mix1(K):
    nc = K.nc
    ada_stage(K, 1)
    norm_stage(K, K.xT, K.hT, KD, ALL, K.v("norm1_1", 0, 8), scale=1, shift=0)
    with ExitStack() as outer:
        sb = lambda name, shape: outer.enter_context(K.temp(name, shape))
        keysT, floorT, top = sb("keysT", [P, 6, 64]), sb("floorT", [P, 4, 64]), sb("top", [64, LAT])
        gate_stage(K, keysT, floorT, top)
        qT, kT = sb("qT", [P, 4, LAT]), sb("kT", [P, 4, ALL])
        conv_qk_stage(K, qT, kT)
        sig = sb("sig", [P, 8, LAT])
        project_stage(K, ["w_ml_o"], K.hT, LAT, 8, lambda b: ("act", lambda act, ps: nc.scalar.activation(
            sig[:, b, :], ps[:, 0:LAT], ACT.Sigmoid)))
        val = sb("val", [P, 6, 8, 129])
        g = K.first("w_ml_v")
        token_major_stage(K, ["w_ml_v"], [
            (g + c, t == 5, [(K.hT[:, k, t * P:t * P + P], K.slot(g + c, KD, 256)[:, k, :]) for k in range(KD)],
             256, val[:, t, 2 * c:2 * c + 2, 0:128]) for c in range(4) for t in range(6)],
            ones=val[:].rearrange("p t h c -> p (t h) c")[:, :, 128:129])
        mlstm_stage(K, qT, kT, keysT, floorT, top, val, sig, K.hT)
    residual_stage(K, "w_ml_out", K.hT, KD, LAT, 2)


def layer1(K):
    with K.activations():
        mix1(K)
    ffn(K, 1, LAT, 5, K.v("norm2_1", 0, 8), scale=4, shift=3)



TOPK = 128
TAKEN = -3e38


def index_scores_stage(K, iqT, ikT, iw, pen, rel):
    nc = K.nc
    dots, relus, added = K.pe_a, K.act_a, K.dve_a
    jobs = [(t, h) for t in range(1, 4) for h in range(4)]
    with K.temp("rl", [P, 2, LAT]) as rl, nc.Block() as block:
        @block.sync
        def _(sp):
            sp.dma_start(rel[:], K.d["rel"]).then_inc(K.loaded.sem, 16)

        @block.tensor
        def _(pe):
            for j, (t, h) in enumerate(jobs):
                if j >= 4:
                    pe.wait_ge(relus.sem, relus.base + j - 3)
                nc.tensor.matmul(K.pairs[j % 4][:, 0:P * (t + 1)], iqT[:, h, t * P:t * P + P],
                                 ikT[:, 0:P * (t + 1)], start=True, stop=True).then_inc(dots.sem, 1)

        @block.scalar
        def _(act):
            for j, (t, h) in enumerate(jobs):
                act.wait_ge(dots.sem, dots.base + j + 1)
                if j >= 2:
                    act.wait_ge(added.sem, added.base + j - 1)
                nc.scalar.activation(rl[:, j % 2, 0:P * (t + 1)], K.pairs[j % 4][:, 0:P * (t + 1)],
                                     ACT.Relu).then_inc(relus.sem, 1)

        @block.vector
        def _(dve):
            chain = Chain(dve, K.dve_chain)
            flat = iw[:].rearrange("p t h -> p (t h)")
            chain.step(nc.vector.tensor_scalar(flat, flat, 4.0 ** -0.5 * 64.0 ** -0.5, None, ALU.mult))
            chain.step(nc.vector.memset(pen[:, 0, 0:P], 0.0))
            chain.sync()
            chain.step(nc.vector.memset(pen[0:64, 0, 64:P], -BIG))
            for j, (t, h) in enumerate(jobs):
                nk = P * (t + 1)
                score = pen[:, t, :]
                dve.wait_ge(relus.sem, relus.base + j + 1)
                chain.sync()
                w = iw[:, t, h:h + 1]
                if h == 0:
                    nc.vector.tensor_scalar(score[:, 0:nk], rl[:, j % 2, 0:nk], w, None, ALU.mult).then_inc(added.sem, 1)
                else:
                    nc.vector.scalar_tensor_tensor(score[:, 0:nk], rl[:, j % 2, 0:nk], w, score[:, 0:nk],
                                                   ALU.mult, ALU.add).then_inc(added.sem, 1)
                dve.wait_ge(added.sem, added.base + j + 1)
                if h == 3:
                    chain.step(nc.vector.memset(score[0:64, nk - 64:nk], -BIG))
            dve.wait_ge(K.loaded.sem, K.loaded.base + 16)
            nc.vector.memset(rel[0:64, :, LAT - 64:LAT], -BIG)
            chain.close()
    K.loaded.base += 16
    for c in (dots, relus, added):
        c.base += len(jobs)


def select_keys(K, dve, chain, pen, best):
    nc = K.nc
    for t in range(1, 4):
        nk = P * (t + 1)
        score = pen[:, t, 0:nk]
        for _ in range(TOPK // 8):
            chain.step(nc.vector.max(best[:], score))
            chain.sync()
            chain.step(nc.vector.match_replace(score, best[:], score, TAKEN))
            chain.sync()
        chain.step(nc.vector.tensor_scalar(score, score, TAKEN / 2, -BIG, ALU.is_gt, ALU.mult))


def lru_stage(K, cx, cy, yc):
    nc = K.nc
    g = K.first("w2_lru")
    w = K.slot(g, 8, P)
    with ExitStack() as stack:
        sb = lambda name, shape: stack.enter_context(K.temp(name, shape))
        u, rec, inp, dec, th = (sb(n, [P, 4, LAT]) for n in ("u", "rec", "inp", "dec", "th"))
        ge = yc
        soft, rate = sb("soft", [P, 4]), sb("rate", [P, 2, 4])
        block = stack.enter_context(nc.Block())

        @block.sync
        def _(sp):
            K.stream(sp, ["w2_lru"])

        @block.tensor
        def _(pe):
            K.wait_weights(pe, g)
            for t in range(4):
                pe.wait_ge(K.dve_a.sem, K.dve_a.base + t + 1)
                for m in range(2):
                    mm = nc.tensor.matmul(K.pairs[t][:, 512 * m:512 * m + LAT], w[:, 4 * m + t, :], u[:, t, :],
                                          start=True, stop=True)
                mm.then_inc(K.pe_a.sem, 1)
            pe.wait_ge(K.pe_a.sem, K.pe_a.base + 4)
            pe.sem_inc(K.w_used.sem, 1)

        @block.scalar
        def _(act):
            chain = Chain(act, K.act_chain)
            chain.step(nc.scalar.activation(soft[:], K.v("lam", 0, 4), ACT.Abs))
            chain.sync()
            chain.step(nc.scalar.activation(soft[:], soft[:], ACT.Exp, scale=-1.0))
            chain.sync()
            nc.scalar.activation(soft[:], soft[:], ACT.Ln, bias=K.ones[:, 0:1]).then_inc(K.act_a.sem, 1)
            for t in range(4):
                act.wait_ge(K.pe_a.sem, K.pe_a.base + t + 1)
                nc.scalar.activation(rec[:, t, :], K.pairs[t][:, 0:LAT], ACT.Sigmoid, bias=K.v("ba", t))
                chain.step(nc.scalar.activation(inp[:, t, :], K.pairs[t][:, 512:512 + LAT], ACT.Sigmoid, bias=K.v("bx", t)))
            act.wait_ge(K.pool_a.sem, K.pool_a.base + 1)
            nc.scalar.activation(ge, ge, ACT.Sigmoid, scale=2 * 0.7978845608028654).then_inc(K.act_c.sem, 1)
            chain.sync()
            act.wait_ge(K.dve_b.sem, K.dve_b.base + 1)
            for t in range(4):
                op = nc.scalar.activation(th[:, t, :], rec[:, t, :], ACT.Tanh, scale=rate[:, 0, t:t + 1])
            for t in range(4):
                op = nc.scalar.activation(dec[:, t, :], rec[:, t, :], ACT.Exp, scale=rate[:, 1, t:t + 1])
            op.then_inc(K.act_b.sem, 1)
            act.wait_ge(K.dve_c.sem, K.dve_c.base + 1)
            nc.scalar.activation(th[:], th[:], ACT.Sqrt).then_inc(K.act_b.sem, 1)
            chain.close()

        @block.gpsimd
        def _(pool):
            chain = Chain(pool, K.pool_chain)
            chain.step(nc.gpsimd.tensor_tensor(ge, cy, cy, ALU.mult))
            chain.sync()
            chain.step(nc.gpsimd.tensor_scalar(ge, ge, 0.044715, 1.0, ALU.mult, ALU.add))
            chain.sync()
            nc.gpsimd.tensor_tensor(ge, ge, cy, ALU.mult).then_inc(K.pool_a.sem, 1)
            pool.wait_ge(K.act_c.sem, K.act_c.base + 1)
            nc.gpsimd.tensor_tensor(ge, ge, cy, ALU.mult).then_inc(K.pool_a.sem, 1)
            chain.close()

        @block.vector
        def _(dve):
            chain = Chain(dve, K.dve_chain)
            tap = lambda j, t: K.v("ccw", 4 * j + t)
            for t in range(4):
                chain.step(nc.vector.tensor_scalar(u[:, t, :], cx[:, t, :], tap(3, t), K.v("ccb", t), ALU.mult, ALU.add))
                for back in range(1, 4):
                    chain.sync()
                    op = nc.vector.scalar_tensor_tensor(u[:, t, back:], cx[:, t, 0:LAT - back], tap(3 - back, t),
                                                        u[:, t, back:], ALU.mult, ALU.add)
                    if back < 3:
                        chain.step(op)
                op.then_inc(K.dve_a.sem, 1)
            dve.wait_ge(K.act_a.sem, K.act_a.base + 1)
            chain.step(nc.vector.tensor_scalar(rate[:, 0, :], K.v("lam", 0, 4), -1.0, 0.0, ALU.mult, ALU.max))
            chain.sync()
            chain.step(nc.vector.tensor_tensor(rate[:, 0, :], rate[:, 0, :], soft[:], ALU.add))
            chain.sync()
            chain.step(nc.vector.tensor_scalar(rate[:, 1, :], rate[:, 0, :], -8.0, None, ALU.mult))
            chain.sync()
            nc.vector.tensor_scalar(rate[:, 0, :], rate[:, 0, :], 8.0, None, ALU.mult).then_inc(K.dve_b.sem, 1)
            dve.wait_ge(K.act_b.sem, K.act_b.base + 1)
            chain.step(nc.vector.tensor_tensor(rec[:], dec[:], dec[:], ALU.mult))
            chain.sync()
            nc.vector.scalar_tensor_tensor(th[:], rec[:], 1.0, th[:], ALU.add, ALU.mult).then_inc(K.dve_c.sem, 1)
            chain.step(nc.vector.tensor_tensor(inp[:], inp[:], u[:], ALU.mult))
            chain.sync()
            dve.wait_ge(K.act_b.sem, K.act_b.base + 2)
            chain.step(nc.vector.tensor_tensor(inp[:], inp[:], th[:], ALU.mult))
            chain.sync()
            for t in range(4):
                chain.step(nc.vector.tensor_tensor_scan(u[:, t, :], dec[:, t, :], inp[:, t, :], 0.0, ALU.mult, ALU.add))
            chain.sync()
            dve.wait_ge(K.pool_a.sem, K.pool_a.base + 2)
            nc.vector.tensor_tensor(yc, u[:], ge, ALU.mult)
            chain.close()
    for c, n in ((K.dve_a, 4), (K.pe_a, 4), (K.act_a, 1), (K.act_b, 2), (K.act_c, 1), (K.dve_b, 1), (K.dve_c, 1),
                 (K.pool_a, 2)):
        c.base += n


def merge_stage(K, branch_tile, merged):
    nc = K.nc
    first = K.first("w2_merge")
    multiplied, gated, summed = K.pe_a, K.act_a, K.dve_a
    bank = lambda c: K.pairs[c // 2][:, 512 * (c % 2):512 * (c % 2) + LAT]
    with ExitStack() as stack:
        sb = lambda name, shape: stack.enter_context(K.temp(name, shape))
        sg, part = sb("sg", [P, 3, LAT]), sb("part", [P, LAT])
        block = stack.enter_context(nc.Block())

        @block.sync
        def _(sp):
            K.stream(sp, ["w2_merge"])

        @block.tensor
        def _(pe):
            with pe.Fori(0, 4) as i:
                for b in range(2):
                    for c in range(2):
                        g = first + 2 * b + c
                        pe.wait_ge(K.w_ready[g % RING].sem, i * 16 + 16 * (g // RING + 1))
                        w = K.slot(g, KD, 256)
                        for half in range(2):
                            branch = 2 * c + half
                            if branch < 3:
                                pe.wait_ge(gated.sem, i * 6 + (gated.base + 3 * b + branch + 1))
                                for k in range(KD):
                                    mm = nc.tensor.matmul(bank(branch), w[:, k, half * P:half * P + P], K.hT[:, k, 0:LAT],
                                                          start=k == 0, stop=k == KD - 1)
                                mm.then_inc(multiplied.sem, 1)
                            else:
                                pe.wait_ge(summed.sem, i * 2 + (summed.base + b + 1))
                                for y, ks in enumerate(((0, 1), (2, 3), (4, 5, 6, 7))):
                                    for k in ks:
                                        mm = nc.tensor.matmul(bank(4 + y), w[:, k, P:2 * P], branch_tile(k),
                                                              start=k == ks[0], stop=k == ks[-1])
                                    mm.then_inc(multiplied.sem, 1)
                        pe.wait_ge(multiplied.sem, i * 12 + (multiplied.base + 6 * b + (2 if c == 0 else 6)))
                        pe.sem_inc(K.w_used.sem, 1)

        @block.scalar
        def _(act):
            act.sem_inc(gated.sem, 3)
            with act.Fori(0, 4) as i:
                for b in range(2):
                    act.wait_ge(summed.sem, i * 2 + (summed.base + b + 1))
                    for c in range(3):
                        act.wait_ge(multiplied.sem, i * 12 + (multiplied.base + 6 * b + c + 1))
                        nc.scalar.activation(sg[:, c, :], bank(c), ACT.Sigmoid, bias=K.vec[
                            :, bass.ds(i * 2 + (VEC["b_gate"][0] + 8 * c + b), 1)]).then_inc(gated.sem, 1)

        @block.vector
        def _(dve):
            dve.sem_inc(summed.sem, 1)
            chain = Chain(dve, K.dve_chain)
            with chain.loop(4, 8) as i:
                for b in range(2):
                    out = merged[:, bass.ds(i * 2 + b, 1), :].rearrange("p o t -> p (o t)")
                    dve.wait_ge(gated.sem, i * 6 + (gated.base + 3 * b + 6))
                    for c in range(3):
                        dve.wait_ge(multiplied.sem, i * 12 + (multiplied.base + 6 * b + c + 4))
                        to = out if c == 0 else part[:]
                        chain.step(nc.vector.tensor_tensor(to, sg[:, c, :], bank(4 + c), ALU.mult))
                        chain.sync()
                        if c > 0:
                            op = nc.vector.tensor_tensor(out, out, part[:], ALU.add)
                            if c == 1:
                                chain.step(op)
                                chain.sync()
                            else:
                                op.then_inc(summed.sem, 1)
            chain.close()
    multiplied.base += 48
    gated.base += 27
    summed.base += 9


def mix2(K):
    nc = K.nc
    norm_stage(K, K.xT, K.hT, KD, LAT, K.v("g_mix", 0, 8))
    with ExitStack() as outer:
        sb = lambda name, shape: outer.enter_context(K.temp(name, shape))
        hd = sb("hd", [P, 11, LAT])
        val, iw = sb("val", [P, 4, 512]), sb("iw", [P, 4, 4])
        first = K.first("w2_heads")
        kinds = [(K.qgain[:, 2:3], False), (K.v("ak_g"), False), (K.qgain[:, 3:4], True), (K.v("bk_g"), True),
                 (None, True), (K.v("ik_g"), True)]
        tiles = []
        for b in range(11):
            w = K.slot(first + b // 2, KD, 256)
            gain, rope = kinds[b // 2]
            tiles.append(dict(
                chunk=first + b // 2, rows=P, sums=K.ones64[:], scale=1 / 64, rope=rope, gain=gain, dst=hd[:, b, :],
                mms=[(w[:, k, b % 2 * P:b % 2 * P + P], lambda a, e, k=k: K.hT[:, k, a:e]) for k in range(KD)]))
        heads_stage(K, ["w2_heads"], tiles, LAT, "trig_seq", "rot_seq")
        cc = sb("cc", [P, 8, LAT])
        with ExitStack() as inner:
            sb_in = lambda name, shape: inner.enter_context(K.temp(name, shape))
            qpad = sb_in("qpad", [P, 12, LAT])
            pen, rel = sb_in("pen", [P, 4, LAT]), sb_in("rel", [P, 4, LAT])
            best = sb_in("best", [P, 8])
            mix = qpad[:, 8:12, :]
            g, gw = K.first("w2_v"), K.first("w2_iw")
            jobs = [(g + c, t == 3, [(K.hT[:, k, t * P:t * P + P], K.slot(g + c, KD, 256)[:, k, :]) for k in range(KD)],
                     256, val[:, t, 256 * c:256 * c + 256]) for c in range(2) for t in range(4)]
            jobs += [(gw, t == 3, [(K.hT[:, k, t * P:t * P + P], K.slot(gw, KD, 4)[:, k, :]) for k in range(KD)],
                      4, iw[:, t, :]) for t in range(4)]

            def pad(pool):
                chain = Chain(pool, K.pool_chain)
                for b in range(2):
                    chain.step(nc.gpsimd.memset(qpad[64 - 64 * b:128 - 64 * b, b::2, :], 0.0))
                    chain.sync()
                    for n, tile in enumerate((0, 4, 8)):
                        r = slice(64 * b, 64 * b + 64)
                        chain.step(nc.gpsimd.tensor_copy(qpad[r, 4 * n + b:4 * n + b + 3:2, :], hd[r, tile:tile + 2, :]))
                        chain.sync()
                chain.close()
            token_major_stage(K, ["w2_v", "w2_iw"], jobs, on_pool=pad)
            index_scores_stage(K, qpad[:, 8:12, :], hd[:, 10, :], iw, pen, rel)
            project_stage(K, ["w2_c"], K.hT, LAT, 8, lambda b: ("act", lambda act, ps: nc.scalar.activation(
                cc[:, b, :], ps[:, 0:LAT], ACT.Copy)), beside=lambda dve, chain: select_keys(K, dve, chain, pen, best))

            def steps(_):
                out = []
                for t in range(4):
                    nk = P * (t + 1)
                    for h in range(8):
                        kind, hh = h // 4, h % 4
                        out.append(dict(
                            q=qpad[:, h, t * P:t * P + P], keys=[(0, hd[:, 4 * kind + 2 + hh // 2, 0:nk])], nk=nk,
                            bias=rel[:, hh, LAT - nk:LAT] if kind == 0 else pen[:, t, 0:nk],
                            v=[val[:, c, 128 * (h // 2):128 * (h // 2) + 128] for c in range(t + 1)],
                            col=lambda at, h=h: slice(at + 64 * (h % 2), at + 64 * (h % 2) + 64),
                            out=mix[:, t, 64 * h:64 * h + 64]))
                return out
            attention_stage(K, 1, steps)
            untoken_stage(K, mix, hd, 4, 4)
        yc = sb("yc", [P, 4, LAT])
        lru_stage(K, cc[:, 0:4, :], cc[:, 4:8, :], yc[:])
        merged = sb("merged", [P, KD, LAT])
        merge_stage(K, lambda k: hd[:, k, :] if k < 4 else yc[:, k - 4, :], merged)
        residual_stage(K, "w2_out", merged, KD, LAT, None)


def layer2(K):
    with K.activations():
        mix2(K)
    ffn(K, 2, LAT, None, K.v("g_ffn", 0, 8))


def store_stage(K, tokens=LAT):
    with K.nc.Block() as block:
        @block.sync
        def _(sp):
            sp.dma_start(K.d["out"], K.xT[:, :, 0:tokens]).then_inc(K.stored.sem, 16)
            sp.wait_ge(K.stored.sem, 16)

def build(nc, arrays):
    with ExitStack() as stack:
        K = Kernel(nc, arrays, stack)
        load_stage(K)
        layer0(K)
        layer1(K)
        layer2(K)
        store_stage(K)


def lay_out(inp):
    a = {k: np.asarray(v) for k, v in inp.items()}
    out = {}

    def pack(w, cols):
        k, n = w.shape
        return np.ascontiguousarray(w.reshape(k // P, P, n // cols, cols).transpose(2, 1, 0, 3)).reshape(
            n // cols, P, -1)

    def pair(left, right):
        k, n = left.shape
        both = np.stack([left.reshape(k, n // P, P), right.reshape(k, n // P, P)], 2)
        return pack(both.reshape(k, 2 * n), 256)

    def put_ffn(layer, up, down):
        at = 0
        for part, kt in enumerate(HIDDEN_PARTS[layer]):
            hidden = slice(at * P, (at + kt) * P)
            at += kt
            out[f"w_up{layer}_{part}"] = pair(up[:, :D_FF][:, hidden], up[:, D_FF:][:, hidden])
            out[f"w_down{layer}_{part}"] = pack(down[hidden], down_blocks(kt) * P)

    zeros = lambda *shape: np.zeros(shape, np.float32)
    for layer in range(2):
        out[f"w_ada{layer}"] = pack(a["ada_w"][layer], 256)
        up = a["ffn_w_up"][layer]
        put_ffn(layer, up, a["ffn_w_down"][layer])
    w = a["att_w_in"][0]
    cq, ckv, kr, gq, gk, gv = np.split(w, np.cumsum([384, 256, 32, 512, 128])[:5], axis=1)
    out["w_att_lo"] = pack(np.concatenate([cq, ckv, zeros(D, 64), kr, zeros(D, 32)], 1), 256)
    out["w_att_gqa"] = pack(np.concatenate([gq, gk[:, :64], gk[:, :64], gk[:, 64:], gk[:, 64:]], 1), 256)
    out["w_gv"] = pack(gv, P)
    out["w_qb"] = pack(a["mla_w_qb"][0], 384)
    kvb = a["mla_w_kvb"][0].reshape(256, 8, 128)
    out["w_kvb"] = pack(np.concatenate([kvb[:, :, :64], zeros(256, 8, 32)], 2).reshape(256, 768), 768)
    out["w_va"] = pack(kvb[:, :, 64:].reshape(256, 512), 512)
    out["w_att_out"] = pack(a["att_w_out"][0], 256)

    w = a["ml_w_in"][0]
    g = w[:, 3072:3104]
    gates = zeros(D, P)
    gate_i, gate_f = zeros(P), zeros(P)
    gb = a["ml_gate_b"][0]
    for d in range(2):
        gates[:, 32 * d:32 * d + 8] = g[:, 16 * d:16 * d + 8]
        gates[:, 64 + 32 * d:72 + 32 * d] = g[:, 16 * d + 8:16 * d + 16]
        gate_i[32 * d:32 * d + 8] = gb[16 * d:16 * d + 8]
        gate_f[32 * d:32 * d + 8] = gb[16 * d + 8:16 * d + 16]
    out["w_ml_gate"] = pack(gates, P)
    out["w_ml_qk"] = pack(w[:, :1024], 256)
    out["w_ml_v"] = pack(w[:, 1024:2048], 256)
    out["w_ml_o"] = pack(w[:, 2048:3072], 256)
    out["w_ml_out"] = pack(a["ml_w_out"][0], 256)

    w = a["w_in_2"][0]
    cuts = np.cumsum([256] * 6 + [256, 64, 4, 512, 512])
    aq, ak, av, bq, bk, bv, iq, ik, iw, cx, cy, gt = np.split(w, cuts, axis=1)
    out["w2_heads"] = pack(np.concatenate([aq, ak, bq, bk, iq, ik, ik, zeros(D, P)], 1), 256)
    out["w2_c"] = pack(np.concatenate([cx, cy], 1), 256)
    out["w2_v"] = pack(np.concatenate([av, bv], 1), 256)
    out["w2_iw"] = pack(iw, 4)
    lru = zeros(P, 8, P)
    for m, name in enumerate(("lru_wa_2", "lru_wx_2")):
        for t in range(4):
            for h in range(2):
                lru[64 * h:64 * h + 64, 4 * m + t, 64 * h:64 * h + 64] = a[name][0, 2 * t + h]
    out["w2_lru"] = lru.reshape(1, P, 1024)
    both = np.concatenate([pair(gt[:, :D], gt[:, D:2 * D]), pair(gt[:, 2 * D:], a["w_branch_2"][0])], 1)
    out["w2_merge"] = both.reshape(16, P, 2048)
    out["w2_out"] = pack(a["w_out_2"][0], 256)
    put_ffn(2, a["w_ffn_in_2"][0], a["w_ffn_out_2"][0])

    vec = zeros(P, NVEC)

    def put(name, v):
        at, n = VEC[name]
        v = np.asarray(v, np.float32)
        vec[:, at:at + n] = np.concatenate([v, zeros(n * P - v.size)]).reshape(n, P).T

    for layer in range(2):
        put(f"norm1_{layer}", a["norm1_g"][layer])
        put(f"norm2_{layer}", a["norm2_g"][layer])
        put(f"ada_b{layer}", a["ada_b"][layer])
        put(f"fcw{layer}", a["ffn_conv_w"][layer].ravel())
        put(f"fcb{layer}", a["ffn_conv_b"][layer])
    put("silu_in", np.stack([a["c"][0].reshape(8, P), a["c_ctx"].reshape(8, P)], 1).ravel())
    put("qa_g", a["mla_qa_g"][0])
    put("kva_g", a["mla_kva_g"][0])
    put("mq_g", a["mla_q_g"][0])
    put("mk_g", a["mla_k_g"][0])
    twice = lambda v: np.concatenate([v, v])
    put("gq_g", twice(a["gqa_q_g"][0]))
    put("gk_g", twice(a["gqa_k_g"][0]))
    put("mcw", a["ml_conv_w"][0].ravel())
    put("mcb", a["ml_conv_b"][0])
    put("gate_i", gate_i)
    put("gate_f", gate_f)
    put("out_g", a["ml_out_g"][0].ravel())
    put("g_mix", a["g_mix_2"][0])
    put("g_ffn", a["g_ffn_2"][0])
    put("aq_g", twice(a["qk_gain_a_2"][0, 0]))
    put("ak_g", twice(a["qk_gain_a_2"][0, 1]))
    put("bq_g", twice(a["qk_gain_b_2"][0, 0]))
    put("bk_g", twice(a["qk_gain_b_2"][0, 1]))
    put("ik_g", twice(a["g_idx_k_2"][0]))
    put("ccw", a["conv_w_2"][0].ravel())
    put("ccb", a["conv_b_2"][0])
    put("ba", a["lru_ba_2"][0])
    put("bx", a["lru_bx_2"][0])
    put("lam", a["lru_lambda_2"][0])
    put("b_gate", a["b_gate_2"][0])
    out["vec"] = vec

    tokens = np.concatenate([a["x"][0], a["ctx"][0]], 0)
    out["xT"] = np.ascontiguousarray(tokens.T.reshape(KD, P, ALL).transpose(1, 0, 2))
    rel = a["rel_bias_2"][0]
    n = LAT
    ext = np.concatenate([np.repeat(rel[:, :1], 1024, 1), rel, np.repeat(rel[:, -1:], 1024, 1)], 1)
    flip = ext[:, ::-1]
    out["rel"] = np.ascontiguousarray(np.stack(
        [flip[:, 1152 - 384 - p:1152 - 384 - p + n] for p in range(P)], 0))

    out["ident"] = np.eye(P, dtype=np.float32)
    out["ones64"] = np.kron(np.eye(2), np.ones((64, 64))).astype(np.float32)

    def axial(dim):
        rows = LAT // 64
        row = np.repeat(np.arange(rows), 64).astype(np.float32)
        col = np.tile(np.arange(64), rows).astype(np.float32)
        nf = dim // 4
        inv = (np.float32(10000.0) ** (-np.arange(nf, dtype=np.float32) / nf)).astype(np.float32)
        ar, ac = row[:, None] * inv, col[:, None] * inv
        return np.concatenate([ar, ar, ac, ac], 1)

    def table(ang, rows):
        t = zeros(P, 2, LAT)
        t[:, 0] = 1.0
        for r in rows:
            t[r:r + ang.shape[1], 0] = np.cos(ang).T
            t[r:r + ang.shape[1], 1] = np.sin(ang).T
        return t

    def rotation(q, starts):
        m = zeros(P, P)
        for s in starts:
            for j in range(q):
                m[s + q + j, s + j] = -1.0
                m[s + j, s + q + j] = 1.0
        return m

    out["trig_mla"] = table(axial(32), [64])
    out["trig_gqa"] = table(axial(64), [0, 64])
    out["rot_mla"] = rotation(8, [64, 80])
    out["rot_gqa"] = rotation(16, [0, 32, 64, 96])
    pos = np.arange(LAT, dtype=np.float32)
    inv = (1.0 / (np.float32(10000.0) ** (np.arange(0, 64, 2, dtype=np.float32) / 64))).astype(np.float32)
    ang = pos[:, None] * inv[None]
    out["trig_seq"] = table(np.concatenate([ang, ang], 1), [0, 64])
    out["rot_seq"] = rotation(32, [0, 64])
    s, t = np.arange(P)[:, None], np.arange(P)[None]
    out["causal"] = np.stack([np.where(s <= t, 0, 1e4), np.where(s >= t, 0, 1e4)], 1).astype(np.float32)
    return out


def kernel(**inputs):
    import concourse.bacc as bacc
    from concourse.bass_utils import run_bass_kernel_spmd

    nc = bacc.Bacc("TRN2", target_bir_lowering=False, num_devices=1)
    arrays = lay_out(inputs)
    aps = {name: nc.dram_tensor(f"in_{name}", a.shape, F32, kind="ExternalInput").ap() for name, a in arrays.items()}
    aps["out"] = nc.dram_tensor("out_y", (P, KD, LAT), F32, kind="ExternalOutput").ap()
    build(nc, aps)
    run = run_bass_kernel_spmd(nc, [{f"in_{n}": a for n, a in arrays.items()}], core_ids=[0])
    y = run.results[0]["out_y"]
    return np.ascontiguousarray(y.transpose(2, 1, 0)).reshape(1, LAT, D)
```

```python
from contextlib import ExitStack, contextmanager

import numpy as np
import concourse.bass as bass
from concourse import mybir

F32 = mybir.dt.float32
F32R = mybir.dt.float32r
ALU = mybir.AluOpType
ACT = mybir.ActivationFunctionType
AX = mybir.AxisListType

P = 128
D, KD = 1024, 8
LAT, CTX = 512, 256
ALL = LAT + CTX
D_FF, KF = 2816, 22
HIDDEN_PARTS = {0: (8, 8, 6), 1: (11, 11), 2: (11, 11)}
EPS = 1e-6
RING = 4
SLOT = 2 * KD * P
BIG = 1e30

VEC_ORDER = [
    ("norm1_0", 8), ("norm1_1", 8), ("norm2_0", 8), ("norm2_1", 8), ("ada_b0", 48), ("ada_b1", 48),
    ("silu_in", 16), ("fcw0", 66), ("fcb0", 22), ("fcw1", 66), ("fcb1", 22),
    ("qa_g", 3), ("kva_g", 2), ("mq_g", 1), ("mk_g", 1), ("gq_g", 1), ("gk_g", 1),
    ("mcw", 24), ("mcb", 8), ("gate_i", 1), ("gate_f", 1), ("out_g", 8),
    ("g_mix", 8), ("g_ffn", 8), ("aq_g", 1), ("ak_g", 1), ("bq_g", 1), ("bk_g", 1), ("ik_g", 1),
    ("ccw", 16), ("ccb", 4), ("ba", 4), ("bx", 4), ("lam", 4), ("b_gate", 24),
]
VEC, _n = {}, 0
for _name, _w in VEC_ORDER:
    VEC[_name] = (_n, _w)
    _n += _w
NVEC = _n


Q_GAINS = [("mq_g", 96), ("gq_g", 64), ("aq_g", 64), ("bq_g", 64)]


class Count:

    def __init__(self, sem):
        self.sem, self.base = sem, 0


class Chain:

    def __init__(self, engine, count):
        self.engine, self.count, self.n, self.turn = engine, count, 0, None

    def step(self, instruction):
        instruction.then_inc(self.count.sem, 1)
        self.n += 1

    def sync(self):
        if self.turn is None:
            self.engine.wait_ge(self.count.sem, self.count.base + self.n)
        else:
            i, per = self.turn
            self.engine.wait_ge(self.count.sem, i * per + (self.count.base + self.n))

    @contextmanager
    def loop(self, turns, per):
        with self.engine.Fori(0, turns) as i:
            start = self.n
            self.turn = (i, per)
            yield i
            assert self.n - start == per, (self.n - start, per)
            self.turn = None
        self.n = start + turns * per

    def close(self):
        self.count.base += self.n


def weight_plan():
    def ffn_of(layer):
        plan = []
        for part, kt in enumerate(HIDDEN_PARTS[layer]):
            per = down_blocks(kt)
            plan += [(f"w_up{layer}_{part}", kt, 2048), (f"w_down{layer}_{part}", KD // per, kt * P * per)]
        return plan
    return [
        ("w_ada0", 24, 2048), ("w_att_lo", 3, 2048), ("w_att_gqa", 3, 2048), ("w_gv", 1, 1024),
        ("w_qb", 2, 1152), ("w_kvb", 1, 1536), ("w_va", 1, 1024), ("w_att_out", 4, 2048),
        *ffn_of(0),
        ("w_ada1", 24, 2048), ("w_ml_gate", 1, 1024), ("w_ml_qk", 4, 2048), ("w_ml_o", 4, 2048),
        ("w_ml_v", 4, 2048), ("w_ml_out", 4, 2048), *ffn_of(1),
        ("w2_heads", 6, 2048), ("w2_v", 2, 2048), ("w2_iw", 1, 32), ("w2_c", 4, 2048),
        ("w2_lru", 1, 1024), ("w2_merge", 16, 2048), ("w2_out", 4, 2048),
        *ffn_of(2),
    ]


def down_blocks(kt):
    return 2 if kt <= KD else 1


def is_split(name):
    return name not in ("w_qb", "w_kvb", "w_va", "w2_lru")


class Kernel:

    def __init__(self, nc, arrays, stack):
        self.nc, self.d, self.temps = nc, arrays, 0
        sem = lambda name: Count(stack.enter_context(nc.semaphore(name)))
        self.sb = lambda name, shape: stack.enter_context(nc.sbuf_tensor(name, shape, F32))
        self.w_ready = [sem(f"w_ready{s}") for s in range(RING)]
        self.w_used = sem("w_used")
        self.ring = self.sb("ring", [P, RING, SLOT])
        self.plan, n = {}, 0
        self.chunks = []
        for name, count, floats in weight_plan():
            self.plan[name] = (n, count, floats)
            self.chunks += [(name, c, floats) for c in range(count)]
            n += count
        self.split_number, splits = {}, 0
        for chunk, (name, _, _) in enumerate(self.chunks):
            if is_split(name):
                self.split_number[chunk] = splits
                splits += 1
        self.high_ready = sem("high_ready")
        self.w_high = self.w_low = None
        self.split_done, self.split_end, self.fresh = -1, -1, None
        self.space, self.space_at = None, 0
        self.loaded = sem("loaded")
        self.tokens_loaded = sem("tokens_loaded")
        self.pe_a = sem("pe_a")
        self.pe_b = sem("pe_b")
        self.pe_c = sem("pe_c")
        self.pe_d = sem("pe_d")
        self.act_a = sem("act_a")
        self.act_b = sem("act_b")
        self.act_c = sem("act_c")
        self.dve_a = sem("dve_a")
        self.dve_b = sem("dve_b")
        self.dve_c = sem("dve_c")
        self.dve_d = sem("dve_d")
        self.dve_e = sem("dve_e")
        self.pool_a = sem("pool_a")
        self.norm_scaled = sem("norm_scaled")
        self.norm_high = sem("norm_high")
        self.norm_shifted = sem("norm_shifted")
        self.norm_low = [sem("norm_low_even"), sem("norm_low_odd")]
        self.stored = sem("stored")
        self.dve_chain = sem("dve_chain")
        self.act_chain = sem("act_chain")
        self.pool_chain = sem("pool_chain")
        self.free = [sem(f"psum_free{s}") for s in range(4)]
        self.pairs = [stack.enter_context(nc.psum_tensor(f"pair{i}", [P, 1024], F32)) for i in range(4)]
        self.xT = self.sb("xT", [P, KD, ALL])
        self.vec = self.sb("vec", [P, NVEC])
        self.ident = self.sb("ident", [P, P])
        self.ones = self.sb("ones", [P, P])
        self.ones64 = self.sb("ones64", [P, P])
        self.c_parts = stack.enter_context(nc.sbuf_tensor("c_parts", [P, KD, 4], F32R))
        self.mod = self.sb("mod", [P, 48, 2])
        self.rinv = self.sb("rinv", [P, ALL])
        self.eps = self.sb("eps", [P, 1])
        self.qgain = self.sb("qgain", [P, 4])
        self.coef = self.sb("coef", [P, 2, KD])

    def temp(self, name, shape, dtype=F32):
        if self.space is not None and dtype == F32 and \
                self.space_at + int(np.prod(shape[1:])) <= self.space.shape[1]:
            return self.carve(shape)
        self.temps += 1
        return self.nc.sbuf_tensor(f"{name}_{self.temps}", shape, dtype)

    @contextmanager
    def arena(self, tensor):
        names = "p a b c"[:2 * len(tensor.shape) - 1]
        self.space = tensor[:].rearrange(f"{names} -> p ({names[2:]})")
        self.space_at = 0
        yield
        self.space = None

    @contextmanager
    def carve(self, shape):
        start, size = self.space_at, int(np.prod(shape[1:]))
        self.space_at += size
        ap = self.space[0:shape[0], start:start + size]
        if len(shape) == 3:
            ap = ap.rearrange("p (a b) -> p a b", a=shape[1])
        yield ap
        self.space_at = start

    @contextmanager
    def activations(self, tokens):
        with self.temp("h_high", [P, KD, tokens], F32R) as self.h_high, \
                self.temp("h_low", [P, KD, tokens], F32R) as self.h_low:
            yield

    @contextmanager
    def split_weights(self):
        with self.temp("w_high", [P, 2, SLOT], F32R) as self.w_high, \
                self.temp("w_low", [P, 2, SLOT], F32R) as self.w_low:
            yield

    def begin_split(self, names, ahead=True):
        first, (start, count, _) = self.first(names[0]), self.plan[names[-1]]
        self.fresh = first if first > self.split_done else None
        self.split_end = start + count - 1 + ahead
        self.split_done = self.split_end if self.split_end in self.split_number else start + count - 1

    def split_fresh_high(self, act):
        if self.fresh is not None:
            self.split_high(act, self.fresh)

    def split_fresh_low(self, dve, on=None):
        if self.fresh is not None:
            self.split_low(dve, self.fresh, on=on)

    def split_high(self, act, chunk, i=0):
        if isinstance(i, int):
            chunk, i = chunk + i * RING, 0
        if chunk not in self.split_number or chunk > self.split_end:
            return
        floats, n = self.chunks[chunk][2], self.split_number[chunk]
        act.wait_ge(self.w_ready[chunk % RING].sem, i * 16 + 16 * (chunk // RING + 1))
        self.nc.scalar.activation(self.w_high[:, n % 2, 0:floats], self.ring[:, chunk % RING, 0:floats],
                                  ACT.Copy).then_inc(self.high_ready.sem, 1)

    def split_low(self, dve, chunk, i=0, on=None):
        if isinstance(i, int):
            chunk, i = chunk + i * RING, 0
        if chunk not in self.split_number or chunk > self.split_end:
            return
        floats, n = self.chunks[chunk][2], self.split_number[chunk]
        dve.wait_ge(self.high_ready.sem, i * RING + (n + 1))
        (on or self.nc.vector).tensor_tensor(self.w_low[:, n % 2, 0:floats], self.ring[:, chunk % RING, 0:floats],
                                     self.w_high[:, n % 2, 0:floats].bitcast(F32),
                                     ALU.subtract).then_inc(self.w_used.sem, 1)

    def parts(self, chunk, kt, cols):
        n = self.split_number[chunk]
        return [w[:, n % 2, 0:kt * cols].rearrange("p (k c) -> p k c", k=kt) for w in (self.w_high, self.w_low)]

    def wait_parts(self, pe, chunk, i=0):
        if isinstance(i, int):
            chunk, i = chunk + i * RING, 0
        if chunk in self.split_number:
            pe.wait_ge(self.w_used.sem, i * RING + (chunk + 1))
        else:
            self.wait_weights(pe, chunk)

    def feature_products(self, chunk, block):
        w_high, w_low = self.parts(chunk, KD, 256)
        at = slice(block * P, block * P + P)
        return [(w[:, k, at], lambda a, e, h=h, k=k: h[:, k, a:e])
                for k in range(KD) for w, h in ((w_high, self.h_high), (w_high, self.h_low), (w_low, self.h_high))]

    def token_products(self, chunk, t, cols):
        w_high, w_low = self.parts(chunk, KD, cols)
        at = slice(t * P, t * P + P)
        return [(h[:, k, at], w[:, k, :])
                for k in range(KD) for h, w in ((self.h_high, w_high), (self.h_high, w_low), (self.h_low, w_high))]

    def product(self, pe, out, chunk, kt, cols, block, high, low, tokens, i=0, on_tile=None):
        if isinstance(i, int):
            chunk, i = chunk + i * RING, 0
        n = self.split_number[chunk]
        w_high, w_low = self.parts(chunk, kt, cols)
        at = slice(block * P, block * P + P)
        pe.wait_ge(self.high_ready.sem, i * RING + (n + 1))
        for j, (a, e) in enumerate(spans(tokens)):
            for k in range(kt):
                if on_tile is not None and j == 0:
                    on_tile(k)
                self.nc.tensor.matmul(out[:, a:e], w_high[:, k, at], high[:, k, a:e], start=k == 0, stop=False)
                self.nc.tensor.matmul(out[:, a:e], w_high[:, k, at], low[:, k, a:e], start=False, stop=False)
            if j == 0:
                pe.wait_ge(self.w_used.sem, i * RING + (chunk + 1))
            for k in range(kt):
                mm = self.nc.tensor.matmul(out[:, a:e], w_low[:, k, at], high[:, k, a:e], start=False, stop=k == kt - 1)
        return mm

    def v(self, name, k=0, n=1, rows=P):
        at, _ = VEC[name]
        return self.vec[0:rows, at + k:at + k + n]

    def first(self, name):
        return self.plan[name][0]

    def slot(self, chunk, k, cols):
        return self.ring[:, chunk % RING, 0:k * cols].rearrange("p (k c) -> p k c", k=k)

    def wait_weights(self, pe, chunk):
        pe.wait_ge(self.w_ready[chunk % RING].sem, 16 * (chunk // RING + 1))

    def send(self, sp, chunk):
        name, c, floats = self.chunks[chunk]
        if chunk >= RING:
            sp.wait_ge(self.w_used.sem, chunk - RING + 1)
        sp.dma_start(self.ring[:, chunk % RING, 0:floats], self.d[name][c]).then_inc(
            self.w_ready[chunk % RING].sem, 16)

    def stream(self, sp, names):
        lo = self.first(names[0]) + RING
        n0, count, _ = self.plan[names[-1]]
        hi = min(n0 + count + RING, len(self.chunks))
        at = lo
        while at < hi:
            name, c, floats = self.chunks[at]
            run = min(self.plan[name][1] - c, hi - at)
            turns = run // RING
            if turns >= 2:
                with sp.Fori(0, turns) as i:
                    for s in range(RING):
                        sp.wait_ge(self.w_used.sem, i * RING + (at + s - RING + 1))
                        sp.dma_start(self.ring[:, (at + s) % RING, 0:floats],
                                     self.d[name][bass.ds(i * RING + (c + s), 1)].rearrange("o p f -> (o p) f")
                                     ).then_inc(self.w_ready[(at + s) % RING].sem, 16)
                at += turns * RING
            else:
                self.send(sp, at)
                at += 1


def spans(tokens):
    return [(0, LAT)] if tokens == LAT else [(0, LAT), (LAT, ALL)]


def ring_turns(eng, count, body, last_differs=False, start=0):
    groups = (count - last_differs) // RING
    rest = count - groups * RING
    if groups - start > 1:
        with eng.Fori(start, groups) as i:
            for s in range(RING):
                body(i, s)
    else:
        for s in range(start * RING, groups * RING):
            body(s // RING, s % RING)
    for s in range(rest):
        body(groups, s)



def load_stage(K):
    nc = K.nc
    with K.temp("silu_c", [P, KD, 2]) as silu_c, nc.Block() as block:
        @block.sync
        def _(sp):
            sp.dma_start(K.vec[:], K.d["vec"]).then_inc(K.loaded.sem, 16)
            for c in range(RING):
                K.send(sp, c)
            for t, name in ((K.ident[:], "ident"), (K.ones64[:], "ones64"), (K.xT[:], "xT")):
                sp.dma_start(t, K.d[name]).then_inc(K.tokens_loaded.sem, 16)

        @block.vector
        def _(dve):
            nc.vector.memset(K.ones[:], 1.0)
            nc.vector.memset(K.eps[:], EPS)
            dve.wait_ge(K.loaded.sem, 16)
            for c, (name, dim) in enumerate(Q_GAINS):
                nc.vector.tensor_scalar(K.qgain[:, c:c + 1], K.v(name), float(dim) ** -0.5, None, ALU.mult)
            dve.wait_ge(K.act_a.sem, 2)
            nc.vector.tensor_tensor(K.c_parts[:, :, 2:4], silu_c[:], K.c_parts[:, :, 0:2].bitcast(F32), ALU.subtract)

        @block.scalar
        def _(act):
            act.wait_ge(K.loaded.sem, 16)
            nc.scalar.activation(silu_c[:].rearrange("p k c -> p (k c)"), K.v("silu_in", 0, 16),
                                 ACT.Silu).then_inc(K.act_a.sem, 1)
            act.wait_ge(K.act_a.sem, 1)
            nc.scalar.activation(K.c_parts[:, :, 0:2], silu_c[:], ACT.Copy).then_inc(K.act_a.sem, 1)
    K.loaded.base += 16
    K.act_a.base += 2


def ada_stage(K, layer):
    nc = K.nc
    name = f"w_ada{layer}"
    first = K.first(name)
    filled, free, turned = K.pe_a, K.free, K.pe_b
    K.begin_split([name], ahead=False)
    with K.temp("mod_rows", [4, 6 * D]) as rows, nc.Block() as block:
        @block.sync
        def _(sp):
            K.stream(sp, [name])

        @block.tensor
        def _(pe):
            def body(i, s):
                g = first + s
                w_high, w_low = K.parts(g, KD, 256)
                pe.wait_ge(free[s].sem, i + (free[s].base + 1))
                pe.wait_ge(K.high_ready.sem, i * RING + (K.split_number[g] + 1))
                for k in range(KD):
                    nc.tensor.matmul(K.pairs[s][0:4, 0:256], K.c_parts[:, k, :], w_high[:, k, :], start=k == 0, stop=False)
                pe.wait_ge(K.w_used.sem, i * RING + (g + 1))
                for k in range(KD):
                    mm = nc.tensor.matmul(K.pairs[s][0:4, 0:256], K.c_parts[:, k, :], w_low[:, k, :],
                                          start=False, stop=k == KD - 1)
                mm.then_inc(filled.sem, 1)
            ring_turns(pe, 24, body)
            for s in range(4):
                pe.wait_ge(free[s].sem, free[s].base + 24 // RING + 1)
            pe.wait_ge(K.tokens_loaded.sem, 48)
            for b in range(48):
                mm = nc.tensor.transpose(K.pairs[0][:, 4 * b:4 * b + 4], rows[:, b * P:b * P + P], K.ident[0:4, 0:4])
            mm.then_inc(turned.sem, 1)

        @block.scalar
        def _(act):
            for s in range(RING):
                act.sem_inc(free[s].sem, 1)
            K.split_fresh_high(act)

            def body(i, s):
                act.wait_ge(filled.sem, i * RING + (filled.base + s))
                K.split_high(act, first + s + 1, i)
                act.wait_ge(filled.sem, i * RING + (filled.base + s + 1))
                nc.scalar.activation(rows[:, bass.ds(i * 1024 + 256 * s, 256)], K.pairs[s][0:4, 0:256],
                                     ACT.Copy).then_inc(free[s].sem, 1)
            ring_turns(act, 24, body, last_differs=True)

        @block.vector
        def _(dve):
            K.split_fresh_low(dve)
            ring_turns(dve, 24, lambda i, s: K.split_low(dve, first + s + 1, i), last_differs=True)
            dve.wait_ge(turned.sem, turned.base + 1)
            chain = Chain(dve, K.dve_chain)
            bias = K.v(f"ada_b{layer}", 0, 48)
            columns = K.pairs[0][:, 0:192].rearrange("p (b c) -> p b c", c=4)
            chain.step(nc.vector.tensor_tensor(K.mod[:], columns[:, :, 0:2],
                                               bias.unsqueeze(2).broadcast_to([P, 48, 2]), ALU.add))
            chain.sync()
            nc.vector.tensor_tensor(K.mod[:], K.mod[:], columns[:, :, 2:4], ALU.add)
            chain.close()
    filled.base += 24
    turned.base += 1
    for s in range(4):
        free[s].base += 24 // RING + 1


def norm_stage(K, src, dst, nt, tokens, gain, scale=None, shift=None):
    nc = K.nc
    parts = spans(tokens)
    stat = K.pairs[3]
    sq_ready, stat_used, std_ready, out_ready = K.act_a, K.pe_a, K.act_b, K.dve_a
    with ExitStack() as stack:
        sq = stack.enter_context(K.temp("sq", [P, 2, tokens]))
        rinv = stack.enter_context(K.temp("rinv", [P, tokens]))
        block = stack.enter_context(nc.Block())

        @block.scalar
        def _(act):
            for k in range(nt):
                if k >= 2:
                    act.wait_ge(stat_used.sem, stat_used.base + k - 1)
                nc.scalar.activation(sq[:, k % 2, 0:tokens], src[:, k, 0:tokens], ACT.Square).then_inc(sq_ready.sem, 1)
            act.wait_ge(stat_used.sem, stat_used.base + nt)
            nc.scalar.activation(rinv[:, 0:tokens], stat[:, 0:tokens], ACT.Sqrt, bias=K.eps[:],
                                 scale=1.0 / (nt * P)).then_inc(std_ready.sem, 1)
            if shift is not None:
                for k in range(nt):
                    act.wait_ge(out_ready.sem, out_ready.base + k + 1)
                    for j, (a, b) in enumerate(parts):
                        nc.scalar.activation(dst[:, k, a:b], dst[:, k, a:b], ACT.Identity,
                                             bias=K.mod[:, shift * KD + k, j:j + 1])

        @block.tensor
        def _(pe):
            for k in range(nt):
                pe.wait_ge(sq_ready.sem, sq_ready.base + k + 1)
                for a, b in parts:
                    mm = nc.tensor.matmul(stat[:, a:b], K.ones[:], sq[:, k % 2, a:b], start=k == 0, stop=k == nt - 1)
                mm.then_inc(stat_used.sem, 1)

        @block.vector
        def _(dve):
            chain = Chain(dve, K.dve_chain)
            coef = K.coef
            for j in range(len(parts)):
                if scale is None:
                    chain.step(nc.vector.tensor_copy(coef[:, j, 0:nt], gain))
                else:
                    chain.step(nc.vector.scalar_tensor_tensor(
                        coef[:, j, 0:nt], K.mod[:, scale * KD:scale * KD + nt, j], 1.0, gain, ALU.add, ALU.mult))
            dve.wait_ge(std_ready.sem, std_ready.base + 1)
            chain.step(nc.vector.reciprocal(rinv[:, 0:tokens], rinv[:, 0:tokens]))
            chain.sync()
            for k in range(nt):
                for j, (a, b) in enumerate(parts):
                    op = nc.vector.scalar_tensor_tensor(dst[:, k, a:b], src[:, k, a:b], coef[:, j, k:k + 1],
                                                        rinv[:, a:b], ALU.mult, ALU.mult)
                op.then_inc(out_ready.sem, 1)
            chain.close()
    sq_ready.base += nt
    stat_used.base += nt
    std_ready.base += 1
    out_ready.base += nt


def stats_stage(K, tokens):
    nc = K.nc
    stat = K.pairs[3]
    sq_ready, stat_used = K.act_a, K.pe_a
    with K.temp("sq", [P, 2, tokens]) as sq, nc.Block() as block:
        @block.scalar
        def _(act):
            for k in range(KD):
                if k >= 2:
                    act.wait_ge(stat_used.sem, stat_used.base + k - 1)
                nc.scalar.activation(sq[:, k % 2, :], K.xT[:, k, 0:tokens], ACT.Square).then_inc(sq_ready.sem, 1)
            act.wait_ge(stat_used.sem, stat_used.base + KD)
            nc.scalar.activation(K.rinv[:, 0:tokens], stat[:, 0:tokens], ACT.Sqrt, bias=K.eps[:],
                                 scale=1.0 / D)

        @block.tensor
        def _(pe):
            for k in range(KD):
                pe.wait_ge(sq_ready.sem, sq_ready.base + k + 1)
                for a, b in spans(tokens):
                    mm = nc.tensor.matmul(stat[:, a:b], K.ones[:], sq[:, k % 2, a:b], start=k == 0, stop=k == KD - 1)
                mm.then_inc(stat_used.sem, 1)

    sq_ready.base += KD
    stat_used.base += KD


class Norm:

    def __init__(self, K, tokens, gain, scale, shift, y):
        self.K, self.parts, self.gain, self.scale, self.shift, self.y = K, spans(tokens), gain, scale, shift, y
        self.scaled, self.high_done, self.low_done = K.norm_scaled, K.norm_high, K.norm_low

    def wait_tile(self, pe, k):
        low = self.low_done[k % 2]
        pe.wait_ge(low.sem, low.base + k // 2 + 1)

    def act(self, act):
        K = self.K
        for k in range(KD):
            act.wait_ge(self.scaled.sem, self.scaled.base + k + 1)
            for j, (a, b) in enumerate(self.parts):
                if self.shift is None:
                    op = K.nc.scalar.activation(K.h_high[:, k, a:b], self.y[:, k % 3, a:b], ACT.Copy)
                else:
                    op = K.nc.scalar.activation(K.h_high[:, k, a:b], self.y[:, k % 3, a:b], ACT.Identity,
                                                bias=K.mod[:, self.shift * KD + k, j:j + 1])
            op.then_inc(self.high_done.sem, 1)
            if self.shift is not None and k % 2 == 1:
                act.wait_ge(self.high_done.sem, self.high_done.base + k + 1)
                for j, (a, b) in enumerate(self.parts):
                    op = K.nc.scalar.activation(self.y[:, k % 3, a:b], self.y[:, k % 3, a:b], ACT.Identity,
                                                bias=K.mod[:, self.shift * KD + k, j:j + 1])
                op.then_inc(K.norm_shifted.sem, 1)

    def low_part(self, engine, eng, k):
        K = self.K
        eng.wait_ge(self.scaled.sem, self.scaled.base + k + 1)
        eng.wait_ge(self.high_done.sem, self.high_done.base + k + 1)
        if self.shift is not None and k % 2 == 1:
            eng.wait_ge(K.norm_shifted.sem, K.norm_shifted.base + k // 2 + 1)
        for j, (a, b) in enumerate(self.parts):
            high = K.h_high[:, k, a:b].bitcast(F32)
            if self.shift is None or k % 2 == 1:
                op = engine.tensor_tensor(K.h_low[:, k, a:b], self.y[:, k % 3, a:b], high, ALU.subtract)
            else:
                op = engine.scalar_tensor_tensor(K.h_low[:, k, a:b], self.y[:, k % 3, a:b],
                                                 K.mod[:, self.shift * KD + k, j:j + 1], high, ALU.add, ALU.subtract)
        op.then_inc(self.low_done[k % 2].sem, 1)

    def dve(self, dve, chain):
        K, nc = self.K, self.K.nc
        rinv = K.rinv[:, 0:self.parts[-1][1]]
        chain.step(nc.vector.reciprocal(rinv, rinv))
        for j in range(len(self.parts)):
            if self.scale is None:
                chain.step(nc.vector.tensor_copy(K.coef[:, j, :], self.gain))
            else:
                chain.step(nc.vector.scalar_tensor_tensor(
                    K.coef[:, j, :], K.mod[:, self.scale * KD:self.scale * KD + KD, j], 1.0, self.gain,
                    ALU.add, ALU.mult))
        chain.sync()
        for k in range(KD + 2):
            if k < KD:
                if k >= 3:
                    low = self.low_done[(k - 3) % 2]
                    dve.wait_ge(low.sem, low.base + (k - 3) // 2 + 1)
                for j, (a, b) in enumerate(self.parts):
                    op = nc.vector.scalar_tensor_tensor(self.y[:, k % 3, a:b], K.xT[:, k, a:b], K.coef[:, j, k:k + 1],
                                                        K.rinv[:, a:b], ALU.mult, ALU.mult)
                op.then_inc(self.scaled.sem, 1)
            if k >= 2 and k % 2 == 0:
                self.low_part(nc.vector, dve, k - 2)

    def pool(self, pool):
        for k in range(1, KD, 2):
            self.low_part(self.K.nc.gpsimd, pool, k)

    def end(self):
        self.scaled.base += KD
        self.high_done.base += KD
        if self.shift is not None:
            self.K.norm_shifted.base += KD // 2
        for low in self.low_done:
            low.base += KD // 2


def project_stage(K, names, tokens, blocks, store, beside=None, norm=None):
    nc = K.nc
    first = K.first(names[0])
    filled, free = K.pe_a, K.free
    K.begin_split(names)
    engines = [store(b)[0] for b in range(blocks)]

    with nc.Block() as block:
        @block.sync
        def _(sp):
            K.stream(sp, names)

        @block.tensor
        def _(pe):
            for b in range(blocks):
                if b >= 4:
                    pe.wait_ge(free[b % 4].sem, free[b % 4].base + b // 4)
                K.product(pe, K.pairs[b % 4], first + b // 2, KD, 256, b % 2, K.h_high, K.h_low,
                          tokens, on_tile=(lambda k: norm.wait_tile(pe, k)) if norm and b == 0 else None
                          ).then_inc(filled.sem, 1)

        @block.scalar
        def _(act):
            K.split_fresh_high(act)
            if norm:
                norm.act(act)
            for b in range(blocks):
                if b % 2 == 0:
                    act.wait_ge(filled.sem, filled.base + b)
                    K.split_high(act, first + b // 2 + 1)
                if engines[b] == "act":
                    act.wait_ge(filled.sem, filled.base + b + 1)
                    store(b)[1](act, K.pairs[b % 4]).then_inc(free[b % 4].sem, 1)

        @block.vector
        def _(dve):
            chain = Chain(dve, K.dve_chain)
            if norm:
                norm.dve(dve, chain)
            if beside is None:
                K.split_fresh_low(dve)
            for b in range(blocks):
                if b % 2 == 0 and beside is None:
                    K.split_low(dve, first + b // 2 + 1)
                if engines[b] == "dve":
                    dve.wait_ge(filled.sem, filled.base + b + 1)
                    store(b)[1](chain, K.pairs[b % 4]).then_inc(free[b % 4].sem, 1)
            if beside is not None:
                beside(dve, chain)
            chain.close()

        @block.gpsimd
        def _(pool):
            if norm:
                norm.pool(pool)
            if beside is not None:
                K.split_fresh_low(pool, on=nc.gpsimd)
                for b in range(0, blocks, 2):
                    K.split_low(pool, first + b // 2 + 1, on=nc.gpsimd)
    if norm:
        norm.end()
    filled.base += blocks
    for s in range(4):
        free[s].base += len(range(s, blocks, 4))


def ffn_up_stage(K, layer, part, tokens, high, low, norm=None):
    nc = K.nc
    name = f"w_up{layer}_{part}"
    first, kt, at = K.first(name), HIDDEN_PARTS[layer][part], sum(HIDDEN_PARTS[layer][:part])
    parts = spans(tokens)
    K.begin_split([name])
    conv = layer < 2
    gate_done, value_done, tap_ready, silu_ready, high_done = K.pe_a, K.pe_b, K.act_a, K.act_b, K.act_c
    conv_ready, hidden_ready, low_done = K.dve_a, K.dve_b, K.dve_d
    gate_read = conv_ready if conv else silu_ready
    one = lambda ap: ap.rearrange("p o t -> p (o t)")
    with ExitStack() as stack:
        gate = stack.enter_context(K.temp("gate", [P, 2, ALL]))
        block = stack.enter_context(nc.Block())

        @block.sync
        def _(sp):
            K.stream(sp, [name])

        @block.tensor
        def _(pe):
            def first_wait(k):
                norm.wait_tile(pe, k)

            def body(i, s):
                for half, read, done in ((0, gate_read, gate_done), (1, hidden_ready, value_done)):
                    pe.wait_ge(read.sem, i * RING + (read.base + s + 1))
                    K.product(pe, K.pairs[2 * (s % 2) + half], first + s, KD, 256, half, K.h_high, K.h_low, tokens,
                              i, first_wait if norm and s == 0 and half == 0 and isinstance(i, int) else None
                              ).then_inc(done.sem, 1)
            if norm is None:
                ring_turns(pe, kt, body)
            else:
                for s in range(RING):
                    body(0, s)
                ring_turns(pe, kt, body, start=1)

        @block.scalar
        def _(act):
            if not conv:
                act.sem_inc(silu_ready.sem, 2)
            act.sem_inc(high_done.sem, 1)
            if norm:
                K.split_fresh_high(act)
                norm.act(act)

            def body(i, s):
                act.wait_ge(value_done.sem, i * RING + (value_done.base + s))
                K.split_high(act, first + s + 1, i)
                act.wait_ge(gate_done.sem, i * RING + (gate_done.base + s + 1))
                act.wait_ge(low_done.sem, i * RING + (low_done.base + s + 1))
                ps = K.pairs[2 * (s % 2)]
                g = gate[:, s % 2, 0:tokens]
                if conv:
                    middle = K.vec[:, bass.ds(i * RING + (VEC[f"fcw{layer}"][0] + KF + at + s), 1)]
                    bias = K.vec[:, bass.ds(i * RING + (VEC[f"fcb{layer}"][0] + at + s), 1)]
                    nc.scalar.activation(g, ps[:, 0:tokens], ACT.Identity, bias=bias,
                                         scale=middle).then_inc(tap_ready.sem, 1)
                    act.wait_ge(conv_ready.sem, i * RING + (conv_ready.base + s + 3))
                    nc.scalar.activation(g, g, ACT.Silu).then_inc(silu_ready.sem, 1)
                else:
                    nc.scalar.activation(g, ps[:, 0:tokens], ACT.Silu).then_inc(silu_ready.sem, 1)
                act.wait_ge(hidden_ready.sem, i * RING + (hidden_ready.base + s + 3))
                nc.scalar.activation(one(high[:, bass.ds(i * RING + s, 1), 0:tokens]), g,
                                     ACT.Copy).then_inc(high_done.sem, 1)
            ring_turns(act, kt, body, last_differs=True)

        @block.vector
        def _(dve):
            dve.sem_inc(hidden_ready.sem, 2)
            dve.sem_inc(low_done.sem, 2)
            if conv:
                dve.sem_inc(conv_ready.sem, 2)
            if norm:
                chain = Chain(dve, K.dve_chain)
                norm.dve(dve, chain)
                K.split_fresh_low(dve)
                chain.close()

            def body(i, s):
                K.split_low(dve, first + s + 1, i)
                ps = K.pairs[2 * (s % 2)]
                g = gate[:, s % 2, :]
                if conv:
                    taps = VEC[f"fcw{layer}"][0] + at
                    before = K.vec[:, bass.ds(i * RING + (taps + s), 1)]
                    after = K.vec[:, bass.ds(i * RING + (taps + 2 * KF + s), 1)]
                    dve.wait_ge(tap_ready.sem, i * RING + (tap_ready.base + s + 1))
                    for a, e in parts:
                        op = nc.vector.scalar_tensor_tensor(g[:, a + 1:e], ps[:, a:e - 1], before,
                                                            g[:, a + 1:e], ALU.mult, ALU.add)
                    op.then_inc(K.dve_c.sem, 1)
                    dve.wait_ge(K.dve_c.sem, i * RING + (K.dve_c.base + s + 1))
                    for a, e in parts:
                        op = nc.vector.scalar_tensor_tensor(g[:, a:e - 1], ps[:, a + 1:e], after,
                                                            g[:, a:e - 1], ALU.mult, ALU.add)
                    op.then_inc(conv_ready.sem, 1)
                dve.wait_ge(silu_ready.sem, i * RING + (silu_ready.base + s + (1 if conv else 3)))
                dve.wait_ge(value_done.sem, i * RING + (value_done.base + s + 1))
                nc.vector.tensor_tensor(g[:, 0:tokens], g[:, 0:tokens], K.pairs[2 * (s % 2) + 1][:, 0:tokens],
                                        ALU.mult).then_inc(hidden_ready.sem, 1)
                dve.wait_ge(hidden_ready.sem, i * RING + (hidden_ready.base + s + 3))
                dve.wait_ge(high_done.sem, i * RING + (high_done.base + s + 2))
                tile = bass.ds(i * RING + s, 1)
                nc.vector.tensor_tensor(one(low[:, tile, 0:tokens]), g[:, 0:tokens],
                                        one(high[:, tile, 0:tokens]).bitcast(F32), ALU.subtract).then_inc(low_done.sem, 1)
            ring_turns(dve, kt, body, last_differs=True)

        @block.gpsimd
        def _(pool):
            if norm:
                norm.pool(pool)
    if norm:
        norm.end()
    gate_done.base += kt
    value_done.base += kt
    hidden_ready.base += kt + 2
    low_done.base += kt + 2
    high_done.base += kt + 1
    if conv:
        tap_ready.base += kt
        conv_ready.base += kt + 2
        K.dve_c.base += kt
        silu_ready.base += kt
    else:
        silu_ready.base += kt + 2


def residual_split_stage(K, name, high, low, kt, per, tokens, gate, raw=None, ahead=True, stats=True,
                         reload=False):
    nc = K.nc
    first = K.first(name)
    parts = spans(tokens)
    pairs = 3 if stats else 4
    filled, free = K.pe_a, K.free
    high_ready, low_ready = K.act_c, K.dve_b
    sq_ready, stat_used, stat = K.act_a, K.pe_b, K.pairs[3]
    K.begin_split([name], ahead)
    with K.temp("sq", [P, 2, tokens]) as sq, nc.Block() as block:
        @block.sync
        def _(sp):
            if reload:
                sp.dma_start(K.xT[:], K.d["xT"]).then_inc(K.loaded.sem, 16)
            K.stream(sp, [name])

        @block.tensor
        def _(pe):
            def tile_ready(k):
                pe.wait_ge(low_ready.sem, low_ready.base + k + 1)

            def sum_squares(k):
                pe.wait_ge(sq_ready.sem, sq_ready.base + k + 1)
                for a, b in parts:
                    mm = nc.tensor.matmul(stat[:, a:b], K.ones[:], sq[:, k % 2, a:b], start=k == 0, stop=k == KD - 1)
                mm.then_inc(stat_used.sem, 1)

            def body(i, s):
                for b in range(s * per, s * per + per):
                    if stats:
                        b = i * RING * per + b
                        if b >= pairs:
                            pe.wait_ge(free[b % pairs].sem, free[b % pairs].base + b // pairs)
                    else:
                        pe.wait_ge(free[b % 4].sem, i * per + (free[b % 4].base + b // 4 + 1))
                    K.product(pe, K.pairs[b % pairs], first + s, kt, per * P, b % per, high, low, tokens,
                              i, tile_ready if raw is not None and b == 0 else None).then_inc(filled.sem, 1)
                    if stats and b > 0:
                        sum_squares(b - 1)
            if stats:
                for c in range(KD // per):
                    body(c // RING, c % RING)
                sum_squares(KD - 1)
            else:
                ring_turns(pe, KD // per, body)

        @block.scalar
        def _(act):
            K.split_fresh_high(act)
            for k in range(kt if raw is not None else 0):
                nc.scalar.activation(high[:, k, :], raw(k), ACT.Copy).then_inc(high_ready.sem, 1)

            def body(i, s):
                act.wait_ge(filled.sem, i * (RING * per) + (filled.base + s * per))
                K.split_high(act, first + s + 1, i)
                for k in range((i * RING + s) * per, (i * RING + s + 1) * per) if stats else ():
                    act.wait_ge(free[k % pairs].sem, free[k % pairs].base + k // pairs + 1)
                    if k >= 2:
                        act.wait_ge(stat_used.sem, stat_used.base + k - 1)
                    nc.scalar.activation(sq[:, k % 2, :], K.xT[:, k, 0:tokens], ACT.Square).then_inc(sq_ready.sem, 1)
            ring_turns(act, KD // per, body, last_differs=True)
            if stats:
                act.wait_ge(stat_used.sem, stat_used.base + KD)
                nc.scalar.activation(K.rinv[:, 0:tokens], stat[:, 0:tokens], ACT.Sqrt, bias=K.eps[:],
                                     scale=1.0 / D)

        @block.vector
        def _(dve):
            if not stats:
                for s in range(4):
                    dve.sem_inc(free[s].sem, 1)
            K.split_fresh_low(dve)
            for k in range(kt if raw is not None else 0):
                dve.wait_ge(high_ready.sem, high_ready.base + k + 1)
                nc.vector.tensor_tensor(low[:, k, :], raw(k), high[:, k, :].bitcast(F32),
                                        ALU.subtract).then_inc(low_ready.sem, 1)

            if reload:
                dve.wait_ge(K.loaded.sem, K.loaded.base + 16)

            def body(i, s):
                K.split_low(dve, first + s + 1, i)
                for b in range((i * RING + s) * per, (i * RING + s + 1) * per):
                    dve.wait_ge(filled.sem, filled.base + b + 1)
                    for j, (a, e) in enumerate(parts):
                        x = K.xT[:, b, a:e]
                        if gate is None:
                            op = nc.vector.tensor_tensor(x, K.pairs[b % pairs][:, a:e], x, ALU.add)
                        else:
                            op = nc.vector.scalar_tensor_tensor(x, K.pairs[b % pairs][:, a:e],
                                                                K.mod[:, gate * KD + b, j:j + 1], x, ALU.mult, ALU.add)
                    op.then_inc(free[b % pairs].sem, 1)
            ring_turns(dve, KD // per, body, last_differs=True)
    filled.base += KD
    if reload:
        K.loaded.base += 16
    if raw is not None:
        high_ready.base += kt
        low_ready.base += kt
    for s in range(pairs):
        free[s].base += len(range(s, KD, pairs)) + (not stats)
    if stats:
        sq_ready.base += KD
        stat_used.base += KD


def ffn(K, layer, tokens, gate, gain, scale=None, shift=None):
    with K.split_weights(), K.activations(tokens):
        most = max(HIDDEN_PARTS[layer])
        with K.temp("high", [P, most, tokens], F32R) as high, K.temp("low", [P, most, tokens], F32R) as low:
            for part, kt in enumerate(HIDDEN_PARTS[layer]):
                last = part == len(HIDDEN_PARTS[layer]) - 1
                if part == 0:
                    with K.temp("normed", [P, 3, tokens]) as y:
                        ffn_up_stage(K, layer, part, tokens, high, low, Norm(K, tokens, gain, scale, shift, y))
                else:
                    ffn_up_stage(K, layer, part, tokens, high, low)
                residual_split_stage(K, f"w_down{layer}_{part}", high, low, kt, down_blocks(kt), tokens, gate,
                                     ahead=not last, stats=last and layer < 2)


def heads_stage(K, names, tiles, tokens, tables, rot, norm=None):
    nc = K.nc
    parts = spans(tokens)
    n = len(tiles)
    raw_done, stat_done, rot_done = K.pe_a, K.pe_b, K.pe_c
    sq_ready, std_ready = K.act_a, K.act_b
    gained, normed, sin_ready = K.dve_a, K.dve_b, K.dve_c
    rotated = K.pool_a
    normal = [t["gain"] is not None for t in tiles]
    roped = [t["rope"] for t in tiles]
    upto = lambda flags, j: sum(flags[:j + 1])
    stat, rots = K.pairs[2], K.pairs[3]
    first_of = {t["chunk"]: j for j, t in reversed(list(enumerate(tiles)))}
    last_of = {t["chunk"]: j for j, t in enumerate(tiles)}
    K.begin_split(names)
    with ExitStack() as stack:
        sb = lambda name, shape: stack.enter_context(K.temp(name, shape))
        sq, std = sb("sq", [P, tokens]), sb("std", [P, tokens])
        y0, y1 = sb("y0", [P, 2, tokens]), sb("y1", [P, 3, tokens])
        ys = sb("ys", [P, LAT])
        trig = sb("trig", [P, 2, LAT])
        rotm = sb("rotm", [P, P])
        block = stack.enter_context(nc.Block())

        @block.sync
        def _(sp):
            sp.dma_start(trig[:], K.d[tables]).then_inc(K.loaded.sem, 16)
            sp.dma_start(rotm[:], K.d[rot]).then_inc(K.loaded.sem, 16)
            K.stream(sp, names)

        @block.tensor
        def _(pe):
            for j in range(n + 2):
                if j < n:
                    t = tiles[j]
                    if j == 0 or tiles[j - 1]["chunk"] != t["chunk"]:
                        K.wait_parts(pe, t["chunk"])
                    if j >= 2:
                        pe.wait_ge(gained.sem, gained.base + j - 1)
                        if normal[j - 2]:
                            pe.wait_ge(sq_ready.sem, sq_ready.base + upto(normal, j - 2))
                    for a, e in parts:
                        for m, (lhs, rhs) in enumerate(t["mms"]):
                            if norm and j == 0 and a == 0 and m % 3 == 0:
                                norm.wait_tile(pe, m // 3)
                            mm = nc.tensor.matmul(K.pairs[j % 2][0:t["rows"], a:e], lhs, rhs(a, e),
                                                  start=m == 0, stop=m == len(t["mms"]) - 1)
                    mm.then_inc(raw_done.sem, 1)
                    if last_of[t["chunk"]] == j and t["chunk"] not in K.split_number:
                        pe.wait_ge(raw_done.sem, raw_done.base + j + 1)
                        pe.sem_inc(K.w_used.sem, 1)
                if 1 <= j <= n and normal[j - 1]:
                    t, r = tiles[j - 1], tiles[j - 1]["rows"]
                    pe.wait_ge(sq_ready.sem, sq_ready.base + upto(normal, j - 1))
                    if upto(normal, j - 1) > 1:
                        pe.wait_ge(std_ready.sem, std_ready.base + upto(normal, j - 1) - 1)
                    for a, e in parts:
                        mm = nc.tensor.matmul(stat[0:r, a:e], t["sums"], sq[0:r, a:e], start=True, stop=True)
                    mm.then_inc(stat_done.sem, 1)
                if j >= 2 and roped[j - 2]:
                    t, r = tiles[j - 2], tiles[j - 2]["rows"]
                    if upto(roped, j - 2) == 1:
                        pe.wait_ge(K.loaded.sem, K.loaded.base + 32)
                    else:
                        pe.wait_ge(sin_ready.sem, sin_ready.base + upto(roped, j - 2) - 1)
                    pe.wait_ge(normed.sem, normed.base + j - 1)
                    nc.tensor.matmul(rots[0:r, 0:LAT], rotm[0:r, 0:r], y1[0:r, (j - 2) % 3, 0:LAT],
                                     start=True, stop=True).then_inc(rot_done.sem, 1)

        @block.scalar
        def _(act):
            K.split_fresh_high(act)
            if norm:
                norm.act(act)
            for j in range(n + 1):
                if j < n and first_of[tiles[j]["chunk"]] == j:
                    act.wait_ge(raw_done.sem, raw_done.base + j)
                    K.split_high(act, tiles[j]["chunk"] + 1)
                if j < n:
                    r = tiles[j]["rows"]
                    act.wait_ge(raw_done.sem, raw_done.base + j + 1)
                    if j >= 2:
                        act.wait_ge(normed.sem, normed.base + j - 1)
                    raw = K.pairs[j % 2][0:r, 0:tokens]
                    if normal[j]:
                        op = nc.scalar.activation(y0[0:r, j % 2, 0:tokens], raw, ACT.Identity, scale=tiles[j]["gain"])
                    else:
                        op = nc.scalar.activation(y0[0:r, j % 2, 0:tokens], raw, ACT.Copy)
                    op.then_inc(gained.sem, 1)
                if j < n and normal[j]:
                    if upto(normal, j) > 1:
                        act.wait_ge(stat_done.sem, stat_done.base + upto(normal, j) - 1)
                    nc.scalar.activation(sq[0:r, 0:tokens], K.pairs[j % 2][0:r, 0:tokens],
                                         ACT.Square).then_inc(sq_ready.sem, 1)
                if j >= 1 and normal[j - 1]:
                    t, r = tiles[j - 1], tiles[j - 1]["rows"]
                    act.wait_ge(stat_done.sem, stat_done.base + upto(normal, j - 1))
                    if j >= 2:
                        act.wait_ge(normed.sem, normed.base + j - 1)
                    nc.scalar.activation(std[0:r, 0:tokens], stat[0:r, 0:tokens], ACT.Sqrt,
                                         bias=K.eps[0:r], scale=t["scale"]).then_inc(std_ready.sem, 1)

        @block.vector
        def _(dve):
            chain = Chain(dve, K.dve_chain)
            K.split_fresh_low(dve)
            if norm:
                norm.dve(dve, chain)
            for j in range(n + 2):
                if j < n and first_of[tiles[j]["chunk"]] == j:
                    K.split_low(dve, tiles[j]["chunk"] + 1)
                if 1 <= j <= n:
                    t, r, b = tiles[j - 1], tiles[j - 1]["rows"], (j - 1) % 3
                    if normal[j - 1]:
                        dve.wait_ge(std_ready.sem, std_ready.base + upto(normal, j - 1))
                        chain.step(nc.vector.reciprocal(std[0:r, 0:tokens], std[0:r, 0:tokens]))
                        chain.sync()
                    dve.wait_ge(gained.sem, gained.base + j)
                    if j >= 4 and roped[j - 4]:
                        dve.wait_ge(rotated.sem, rotated.base + upto(roped, j - 4))
                    to = y1[0:r, b, 0:tokens] if t["rope"] else t["dst"]
                    if normal[j - 1]:
                        op = nc.vector.tensor_tensor(to, y0[0:r, (j - 1) % 2, 0:tokens], std[0:r, 0:tokens], ALU.mult)
                    else:
                        op = nc.vector.tensor_copy(to, y0[0:r, (j - 1) % 2, 0:tokens])
                    op.then_inc(normed.sem, 1)
                if j >= 2 and roped[j - 2]:
                    r = tiles[j - 2]["rows"]
                    dve.wait_ge(rot_done.sem, rot_done.base + upto(roped, j - 2))
                    if upto(roped, j - 2) > 1:
                        dve.wait_ge(rotated.sem, rotated.base + upto(roped, j - 2) - 1)
                    nc.vector.tensor_tensor(ys[0:r, :], rots[0:r, 0:LAT], trig[0:r, 1, :],
                                            ALU.mult).then_inc(sin_ready.sem, 1)
            chain.close()

        @block.gpsimd
        def _(pool):
            chain = Chain(pool, K.pool_chain)
            if norm:
                norm.pool(pool)
            pool.wait_ge(K.loaded.sem, K.loaded.base + 32)
            for j in range(n):
                if not roped[j]:
                    continue
                t, r, b = tiles[j], tiles[j]["rows"], j % 3
                pool.wait_ge(normed.sem, normed.base + j + 1)
                if tokens > LAT:
                    chain.step(nc.gpsimd.tensor_copy(t["dst"][:, LAT:tokens], y1[0:r, b, LAT:tokens]))
                chain.step(nc.gpsimd.tensor_tensor(t["dst"][:, 0:LAT], y1[0:r, b, 0:LAT], trig[0:r, 0, :], ALU.mult))
                chain.sync()
                pool.wait_ge(sin_ready.sem, sin_ready.base + upto(roped, j))
                nc.gpsimd.tensor_tensor(t["dst"][:, 0:LAT], t["dst"][:, 0:LAT], ys[0:r, :],
                                        ALU.add).then_inc(rotated.sem, 1)
            chain.close()
    if norm:
        norm.end()
    K.loaded.base += 32
    for c in (raw_done, gained, normed):
        c.base += n
    for c in (stat_done, sq_ready, std_ready):
        c.base += sum(normal)
    for c in (rot_done, sin_ready, rotated):
        c.base += sum(roped)


def token_major_stage(K, names, jobs, ones=None, on_pool=None, ahead=True):
    nc = K.nc
    filled, free = K.pe_a, K.free
    starts = [j == 0 or jobs[j - 1][0] != jobs[j][0] for j in range(len(jobs))]
    K.begin_split(names, ahead)
    with nc.Block() as block:
        @block.sync
        def _(sp):
            K.stream(sp, names)

        @block.tensor
        def _(pe):
            for j, (chunk, last, mms, cols, dst) in enumerate(jobs):
                if starts[j]:
                    K.wait_parts(pe, chunk)
                if j >= 4:
                    pe.wait_ge(free[j % 4].sem, free[j % 4].base + j // 4)
                for m, (lhs, rhs) in enumerate(mms):
                    mm = nc.tensor.matmul(K.pairs[j % 4][:, 0:cols], lhs, rhs, start=m == 0, stop=m == len(mms) - 1)
                mm.then_inc(filled.sem, 1)
                if last and chunk not in K.split_number:
                    pe.wait_ge(filled.sem, filled.base + j + 1)
                    pe.sem_inc(K.w_used.sem, 1)

        if on_pool is not None:
            block.gpsimd(on_pool)

        def source(j):
            ps = K.pairs[j % 4][:, 0:jobs[j][3]]
            shape = jobs[j][4].shape
            return ps.rearrange("p (h c) -> p h c", h=shape[1]) if len(shape) == 3 else ps

        @block.scalar
        def _(act):
            K.split_fresh_high(act)
            for j in range(len(jobs)):
                if starts[j]:
                    act.wait_ge(filled.sem, filled.base + j)
                    K.split_high(act, jobs[j][0] + 1)
                if j % 2 == 1:
                    continue
                act.wait_ge(filled.sem, filled.base + j + 1)
                nc.scalar.activation(jobs[j][4], source(j), ACT.Copy).then_inc(free[j % 4].sem, 1)

        @block.vector
        def _(dve):
            if ones is not None:
                nc.vector.memset(ones, 1.0)
            K.split_fresh_low(dve)
            for j in range(len(jobs)):
                if starts[j]:
                    K.split_low(dve, jobs[j][0] + 1)
                if j % 2 == 0:
                    continue
                dve.wait_ge(filled.sem, filled.base + j + 1)
                nc.vector.tensor_copy(jobs[j][4], source(j)).then_inc(free[j % 4].sem, 1)
    filled.base += len(jobs)
    for s in range(4):
        free[s].base += len(range(s, len(jobs), 4))


def attention_stage(K, turns, steps_of, stage_q=None, stage_steps=0, stage_on_dve=False):
    nc = K.nc
    scored, transposed, summed = K.pe_a, K.pe_b, K.pe_c
    maxed, copied, out_ready, biased = K.dve_a, K.dve_b, K.dve_c, K.dve_d
    exped, staged = K.act_a, K.pool_a
    probe = steps_of(0)
    n = len(probe)
    assert n % 4 == 0 or turns == 1
    with_bias = "bias" in probe[0]
    pt = K.pairs[2]
    with ExitStack() as stack:
        sb = lambda name, shape: stack.enter_context(K.temp(name, shape))
        width = max(s["nk"] for s in probe)
        prob, probT = sb("prob", [P, 2, width]), sb("probT", [P, 2, width])
        scores = sb("scores", [P, 2, width]) if with_bias else None
        stats = sb("stats", [P, 3, 4])
        block = stack.enter_context(nc.Block())

        def loop(eng, body):
            if turns == 1:
                body(0)
            else:
                with eng.Fori(0, turns) as i:
                    body(i)

        if stage_q is not None and not stage_on_dve:
            @block.gpsimd
            def _(pool):
                pool.sem_inc(scored.sem, 1)
                chain = Chain(pool, K.pool_chain)
                with chain.loop(turns, stage_steps) as i:
                    pool.wait_ge(scored.sem, i * n + (scored.base + 1))
                    stage_q(nc.gpsimd, chain, i).then_inc(staged.sem, 1)
                chain.close()
        lead = 0 if stage_q is None else 1

        @block.tensor
        def _(pe):
            def body(i):
                steps = steps_of(i)
                if stage_q is not None:
                    pe.wait_ge(staged.sem, i + (staged.base + 1))
                for m in range(n + 2):
                    if m < n:
                        s = steps[m]
                        for at, rhs in s["keys"]:
                            mm = nc.tensor.matmul(K.pairs[m % 2][:, at:at + rhs.shape[-1]], s["q"], rhs,
                                                  start=True, stop=True)
                        mm.then_inc(scored.sem, 1)
                    if m >= 2:
                        j = m - 2
                        pe.wait_ge(copied.sem, i * n + (copied.base + j + 1))
                        tiles = steps[j]["v"]
                        for c, v in enumerate(tiles):
                            mm = nc.tensor.matmul(K.pairs[3][:, 512 * (j % 2):512 * (j % 2) + P],
                                                  probT[:, j % 2, c * P:c * P + P], v,
                                                  start=c == 0, stop=c == len(tiles) - 1)
                        mm.then_inc(summed.sem, 1)
                    if 1 <= m <= n:
                        j = m - 1
                        pe.wait_ge(exped.sem, i * n + (exped.base + j + 1))
                        for c in range(steps[j]["nk"] // P):
                            mm = nc.tensor.transpose(pt[:, c * P:c * P + P], prob[:, j % 2, c * P:c * P + P], K.ident[:])
                        mm.then_inc(transposed.sem, 1)
            loop(pe, body)

        @block.scalar
        def _(act):
            def body(i):
                for m, s in enumerate(steps_of(i)):
                    act.wait_ge(maxed.sem, i * n + (maxed.base + m + 1))
                    lo = s["keys"][0][0]
                    src = scores[:, m % 2, 0:s["nk"]] if with_bias else K.pairs[m % 2][:, lo:lo + s["nk"]]
                    nc.scalar.activation(prob[:, m % 2, 0:s["nk"]], src, ACT.Exp, bias=stats[:, 0, m % 4:m % 4 + 1],
                                         accum_out=stats[:, 1, m % 4:m % 4 + 1]).then_inc(exped.sem, 1)
            loop(act, body)

        @block.vector
        def _(dve):
            chain = Chain(dve, K.dve_chain)
            if stage_on_dve:
                dve.sem_inc(scored.sem, 1)

            def body(i):
                if stage_on_dve:
                    dve.wait_ge(scored.sem, i * n + (scored.base + 1))
                    stage_q(nc.vector, chain, i).then_inc(staged.sem, 1)
                steps = steps_of(i)
                for m in range(n + 2):
                    if m < n:
                        s = steps[m]
                        dve.wait_ge(scored.sem, i * n + (scored.base + lead + m + 1))
                        lo = s["keys"][0][0]
                        src = K.pairs[m % 2][:, lo:lo + s["nk"]]
                        if with_bias:
                            to = scores[:, m % 2, 0:s["nk"]]
                            chain.step(nc.vector.tensor_tensor(to, src, s["bias"], ALU.add))
                            chain.sync()
                            src = to
                        nc.vector.tensor_reduce(stats[:, 0, m % 4:m % 4 + 1], src, AX.X, ALU.max,
                                                negate=True).then_inc(maxed.sem, 1)
                    if 1 <= m <= n:
                        j = m - 1
                        dve.wait_ge(transposed.sem, i * n + (transposed.base + j + 1))
                        nk = steps[j]["nk"]
                        nc.vector.tensor_copy(probT[:, j % 2, 0:nk], pt[:, 0:nk]).then_inc(copied.sem, 1)
                    if m >= 2:
                        j = m - 2
                        dve.wait_ge(summed.sem, i * n + (summed.base + j + 1))
                        chain.step(nc.vector.reciprocal(stats[:, 2, j % 4:j % 4 + 1], stats[:, 1, j % 4:j % 4 + 1]))
                        chain.sync()
                        nc.vector.tensor_scalar(steps[j]["out"], K.pairs[3][:, steps[j]["col"](512 * (j % 2))],
                                                stats[:, 2, j % 4:j % 4 + 1], None, ALU.mult).then_inc(out_ready.sem, 1)
            if turns == 1:
                body(0)
            else:
                with chain.loop(turns, n * (2 if with_bias else 1) + (stage_steps if stage_on_dve else 0)) as i:
                    body(i)
            chain.close()
    for c in (transposed, summed, maxed, copied, out_ready, exped):
        c.base += n * turns
    scored.base += n * turns + lead
    if stage_q is not None:
        staged.base += turns


def untoken_stage(K, src, dst, tiles_k, tiles_t):
    nc = K.nc
    filled, free = K.pe_a, K.free
    width = tiles_t * P
    with nc.Block() as block:
        @block.tensor
        def _(pe):
            for k in range(tiles_k):
                if k >= 4:
                    pe.wait_ge(free[k % 4].sem, free[k % 4].base + k // 4)
                for t in range(tiles_t):
                    mm = nc.tensor.transpose(K.pairs[k % 4][:, t * P:t * P + P], src[:, t, k * P:k * P + P], K.ident[:])
                mm.then_inc(filled.sem, 1)

        @block.scalar
        def _(act):
            for k in range(0, tiles_k, 2):
                act.wait_ge(filled.sem, filled.base + k + 1)
                nc.scalar.activation(dst[:, k, 0:width], K.pairs[k % 4][:, 0:width], ACT.Copy).then_inc(free[k % 4].sem, 1)

        @block.vector
        def _(dve):
            for k in range(1, tiles_k, 2):
                dve.wait_ge(filled.sem, filled.base + k + 1)
                nc.vector.tensor_copy(dst[:, k, 0:width], K.pairs[k % 4][:, 0:width]).then_inc(free[k % 4].sem, 1)
    filled.base += tiles_k
    for s in range(4):
        free[s].base += len(range(s, tiles_k, 4))



def mix0(K):
    nc = K.nc
    with ExitStack() as outer:
        sb = lambda name, shape: outer.enter_context(K.temp(name, shape))
        val = sb("val", [P, 6, 640])
        low = sb("low", [P, KD, ALL])
        gqT, gkT = K.xT[:, 0:4, :], K.xT[:, 4:6, :]
        with K.split_weights(), K.activations(ALL):
            ada_stage(K, 0)
            stats_stage(K, ALL)

            def store(b):
                if b % 2 == 0:
                    return "act", lambda act, ps: nc.scalar.activation(low[:, b, :], ps[:, 0:ALL], ACT.Copy)
                return "dve", lambda chain, ps: nc.vector.tensor_copy(low[:, b, :], ps[:, 0:ALL])
            with K.temp("normed", [P, 3, ALL]) as y:
                project_stage(K, ["w_att_lo"], ALL, 6, store, norm=Norm(K, ALL, K.v("norm1_0", 0, 8), 1, 0, y))
            first = K.first("w_att_gqa")
            tiles = []
            for b in range(6):
                tiles.append(dict(
                    chunk=first + b // 2, rows=P, sums=K.ones64[:], scale=1 / 64, rope=True,
                    mms=K.feature_products(first + b // 2, b % 2),
                    gain=K.qgain[:, 1:2] if b < 4 else K.v("gk_g"), dst=gqT[:, b, :] if b < 4 else gkT[:, b - 4, :]))
            with K.arena(low[:, 6:8, :]):
                heads_stage(K, ["w_att_gqa"], tiles, ALL, "trig_gqa", "rot_gqa")
            g = K.first("w_gv")
            token_major_stage(K, ["w_gv"], [
                (g, t == 5, K.token_products(g, t, P), P, val[:, t, 512:640]) for t in range(6)], ahead=False)
        inner = outer.enter_context(ExitStack())
        qT, kT = (inner.enter_context(K.temp(n, [96, 8, ALL])) for n in ("qT", "kT"))
        norm_stage(K, low, low, 3, ALL, K.v("qa_g", 0, 3))
        norm_stage(K, low[:, 3:5, :], low[:, 3:5, :], 2, ALL, K.v("kva_g", 0, 2))
        gq, gkv = K.first("w_qb"), K.first("w_kvb")
        tiles = []
        for h in range(8):
            tiles.append(dict(
                chunk=gq + h // 4, rows=96, sums=K.ones[0:96, 0:96], scale=1 / 96, rope=True, gain=K.qgain[0:96, 0:1],
                mms=[(K.slot(gq + h // 4, 3, 384)[:, k, h % 4 * 96:h % 4 * 96 + 96], lambda a, e, k=k: low[:, k, a:e]) for k in range(3)],
                dst=qT[0:96, h, :]))
        for h in range(8):
            tiles.append(dict(
                chunk=gkv, rows=96, sums=K.ones[0:96, 0:96], scale=1 / 96, rope=True, gain=K.v("mk_g", rows=96),
                mms=[(K.slot(gkv, 2, 768)[:, k, h * 96:h * 96 + 96], lambda a, e, k=k: low[:, 3 + k, a:e])
                     for k in range(2)] + [(K.ident[:, 0:96], lambda a, e: low[:, 5, a:e])],
                dst=kT[:, h, :]))
        heads_stage(K, ["w_qb", "w_kvb"], tiles, ALL, "trig_mla", "rot_mla")
        g = K.first("w_va")
        token_major_stage(K, ["w_va"], [
            (g, t == 5, [(low[:, 3 + k, t * P:t * P + P], K.slot(g, 2, 512)[:, k, :]) for k in range(2)],
             512, val[:, t, 0:512]) for t in range(6)], ahead=False)
        mixed = low[:].rearrange("p k t -> p (k t)").rearrange("p (t c) -> p t c", t=6)
        order = [0, 1, 2, 3, 4, 5]
        with K.temp("qs", [P, 4, ALL]) as qs, K.temp("ks", [P, ALL]) as ks:
            one = lambda ap: ap.rearrange("p o t -> p (o t)")

            def step(t, q, key, v, col, out):
                lat = t < 4
                return dict(q=q, col=col, nk=ALL if lat else CTX, out=out,
                            keys=[(0, key(0, LAT)), (LAT, key(LAT, ALL))] if lat else [(0, key(LAT, ALL))],
                            v=[v(c) for c in (range(6) if lat else range(4, 6))])

            def mla_steps(i):
                steps = []
                for b in range(2):
                    for t in order:
                        steps.append(step(
                            t, qs[0:96, b, t * P:t * P + P],
                            lambda a, e, b=b: one(kT[:, bass.ds(i * 2 + b, 1), a:e]),
                            lambda c: val[:, c, bass.ds(i * 128, 128)],
                            lambda at, b=b: slice(at + 64 * b, at + 64 * b + 64),
                            mixed[:, t, bass.ds(i * 128 + b * 64, 64)]))
                return steps

            def mla_stage(engine, chain, i):
                return engine.tensor_copy(qs[0:96, 0:2, :], qT[0:96, bass.ds(i * 2, 2), :])
            attention_stage(K, 4, mla_steps, mla_stage)

            def gqa_steps(i):
                steps = []
                for b in range(2):
                    for half in range(2):
                        for t in order:
                            steps.append(step(
                                t, qs[:, 2 * b + half, t * P:t * P + P],
                                lambda a, e: ks[:, a:e],
                                lambda c: val[:, c, 512:640],
                                lambda at: bass.ds(i * 64 + at, 64),
                                mixed[:, t, bass.ds(i * 256 + (512 + b * 128 + half * 64), 64)]))
                return steps

            def gqa_stage(engine, chain, i):
                chain.step(engine.tensor_copy(ks[:], one(gkT[:, bass.ds(i, 1), :])))
                for half in range(2):
                    r = slice(64 * half, 64 * half + 64)
                    chain.sync()
                    op = engine.tensor_copy(qs[r, half::2, :], gqT[r, bass.ds(i * 2, 2), :])
                    if half == 0:
                        chain.step(op)
                return op
            with nc.Block() as block:
                @block.vector
                def _(dve):
                    for half in range(2):
                        nc.vector.memset(qs[64 - 64 * half:128 - 64 * half, half::2, :], 0.0)
            attention_stage(K, 2, gqa_steps, gqa_stage, 2, stage_on_dve=True)
        inner.close()
        with K.temp("mixT", [P, KD, ALL]) as mixT, K.split_weights(), K.activations(ALL):
            untoken_stage(K, mixed, mixT, KD, 6)
            with K.arena(low):
                residual_split_stage(K, "w_att_out", K.h_high, K.h_low, KD, 2, ALL, 2, raw=lambda k: mixT[:, k, :],
                                     ahead=False, reload=True)


def layer0(K):
    mix0(K)
    ffn(K, 0, ALL, 5, K.v("norm2_0", 0, 8), scale=4, shift=3)



def gate_stage(K, keysT, floorT, top, norm):
    nc = K.nc
    g = K.first("w_ml_gate")
    w_parts = K.parts(g, KD, P)
    K.begin_split(["w_ml_gate"])
    R = 64
    with ExitStack() as stack:
        sb = lambda name, shape: stack.enter_context(K.temp(name, shape))
        gi, gx, soft, run = (sb(n, [R, ALL]) for n in ("gi", "gx", "soft", "run"))
        zero, high = sb("zero", [R, ALL]), sb("high", [R, ALL])
        block = stack.enter_context(nc.Block())

        @block.sync
        def _(sp):
            K.stream(sp, ["w_ml_gate"])

        @block.tensor
        def _(pe):
            K.wait_parts(pe, g)
            for half in range(2):
                for a, e in spans(ALL):
                    for k in range(KD):
                        if half == 0 and a == 0:
                            norm.wait_tile(pe, k)
                        for n, (w, h) in enumerate(((0, K.h_high), (0, K.h_low), (1, K.h_high))):
                            mm = nc.tensor.matmul(K.pairs[half][0:R, a:e], w_parts[w][:, k, half * R:half * R + R],
                                                  h[:, k, a:e], start=k == 0 and n == 0, stop=k == KD - 1 and n == 2)
            mm.then_inc(K.pe_a.sem, 1)
            pe.wait_ge(K.dve_b.sem, K.dve_b.base + 1)
            for t in range(6):
                mm = nc.tensor.transpose(K.pairs[2][:, t * R:t * R + R], gi[:, t * P:t * P + P], K.ident[0:R, 0:R])
            mm.then_inc(K.pe_b.sem, 1)
            pe.wait_ge(K.act_b.sem, K.act_b.base + 1)
            for t in range(4):
                mm = nc.tensor.transpose(K.pairs[3][:, t * R:t * R + R], soft[:, t * P:t * P + P], K.ident[0:R, 0:R])
            mm.then_inc(K.pe_b.sem, 1)

        @block.scalar
        def _(act):
            chain = Chain(act, K.act_chain)
            K.split_fresh_high(act)
            norm.act(act)
            K.split_high(act, g + 1)
            act.wait_ge(K.dve_a.sem, K.dve_a.base + 1)
            chain.step(nc.scalar.activation(soft[:], gx[:], ACT.Abs))
            chain.sync()
            chain.step(nc.scalar.activation(soft[:], soft[:], ACT.Exp, scale=-1.0))
            chain.sync()
            nc.scalar.activation(soft[:], soft[:], ACT.Ln, bias=K.ones[0:R, 0:1]).then_inc(K.act_a.sem, 1)
            act.wait_ge(K.dve_c.sem, K.dve_c.base + 1)
            nc.scalar.activation(soft[:, 0:LAT], gx[:, 0:LAT], ACT.Exp, scale=-1.0).then_inc(K.act_b.sem, 1)
            chain.close()

        @block.vector
        def _(dve):
            chain = Chain(dve, K.dve_chain)
            K.split_fresh_low(dve)
            norm.dve(dve, chain)
            K.split_low(dve, g + 1)
            chain.step(nc.vector.memset(zero[:], 0.0))
            dve.wait_ge(K.pe_a.sem, K.pe_a.base + 1)
            chain.step(nc.vector.tensor_scalar(gi[:], K.pairs[0][0:R, 0:ALL], K.v("gate_i", rows=R), None, ALU.add))
            nc.vector.tensor_scalar(gx[:], K.pairs[1][0:R, 0:ALL], K.v("gate_f", rows=R), None,
                                    ALU.add).then_inc(K.dve_a.sem, 1)
            dve.wait_ge(K.act_a.sem, K.act_a.base + 1)
            chain.step(nc.vector.scalar_tensor_tensor(gx[:], gx[:], 0.0, soft[:], ALU.min, ALU.subtract))
            chain.sync()

            def scan(out, data, op):
                for r, rev in ((slice(0, 32), 1), (slice(32, 64), -1)):
                    part = lambda x, a, e: x[r, a:e] if rev == 1 else x[r, a:e][:, ::-1]
                    chain.step(nc.vector.tensor_tensor_scan(part(out, LAT, ALL), part(zero, LAT, ALL),
                                                            part(data, LAT, ALL), 0.0, ALU.add, op))
                chain.sync()
                for r, rev, last in ((slice(0, 32), 1, ALL - 1), (slice(32, 64), -1, LAT)):
                    part = lambda x, a, e: x[r, a:e] if rev == 1 else x[r, a:e][:, ::-1]
                    chain.step(nc.vector.tensor_tensor_scan(part(out, 0, LAT), part(zero, 0, LAT), part(data, 0, LAT),
                                                            out[r, last:last + 1], ALU.add, op))
                chain.sync()

            scan(run, gx, ALU.add)
            nc.vector.tensor_tensor(gi[:], gi[:], run[:], ALU.subtract).then_inc(K.dve_b.sem, 1)
            dve.wait_ge(K.dve_b.sem, K.dve_b.base + 1)
            scan(high, gi, ALU.max)
            chain.step(nc.vector.tensor_copy(top[:], high[:, 0:LAT]))
            nc.vector.tensor_tensor(gx[:, 0:LAT], high[:, 0:LAT], run[:, 0:LAT], ALU.add).then_inc(K.dve_c.sem, 1)
            dve.wait_ge(K.pe_b.sem, K.pe_b.base + 1)
            nc.vector.tensor_copy(keysT[:].rearrange("p t c -> p (t c)"), K.pairs[2][:, 0:6 * R])
            dve.wait_ge(K.pe_b.sem, K.pe_b.base + 2)
            nc.vector.tensor_copy(floorT[:].rearrange("p t c -> p (t c)"), K.pairs[3][:, 0:4 * R])
            chain.close()

        @block.gpsimd
        def _(pool):
            norm.pool(pool)
    norm.end()
    for c, n in ((K.pe_a, 1), (K.pe_b, 2), (K.dve_a, 1), (K.dve_b, 1), (K.dve_c, 1), (K.act_a, 1), (K.act_b, 1)):
        c.base += n


def conv_qk_stage(K, qT, kT):
    nc = K.nc
    first = K.first("w_ml_qk")
    done, tap, silu, conved = K.pe_a, K.act_a, K.act_b, K.dve_a
    cw, cb = VEC["mcw"][0], VEC["mcb"][0]
    K.begin_split(["w_ml_qk"])
    parts_of = lambda b: [(0, LAT)] if b < 4 else spans(ALL)
    with ExitStack() as stack:
        buf = stack.enter_context(K.temp("buf", [P, 2, ALL]))
        block = stack.enter_context(nc.Block())

        @block.sync
        def _(sp):
            K.stream(sp, ["w_ml_qk"])

        @block.tensor
        def _(pe):
            for b in range(8):
                if b >= 4:
                    pe.wait_ge(conved.sem, conved.base + b - 3)
                K.product(pe, K.pairs[b % 4], first + b // 2, KD, 256, b % 2, K.h_high, K.h_low,
                          parts_of(b)[-1][1]).then_inc(done.sem, 1)

        @block.scalar
        def _(act):
            K.split_fresh_high(act)
            for b in range(8):
                if b % 2 == 0:
                    act.wait_ge(done.sem, done.base + b)
                    K.split_high(act, first + b // 2 + 1)
                n = parts_of(b)[-1][1]
                act.wait_ge(done.sem, done.base + b + 1)
                if b >= 2:
                    act.wait_ge(silu.sem, silu.base + b - 1)
                nc.scalar.activation(buf[:, b % 2, 0:n], K.pairs[b % 4][:, 0:n], ACT.Identity,
                                     bias=K.vec[:, cb + b:cb + b + 1],
                                     scale=K.vec[:, cw + 8 + b:cw + 9 + b]).then_inc(tap.sem, 1)
                act.wait_ge(conved.sem, conved.base + b + 1)
                dst = qT[:, b, :] if b < 4 else kT[:, b - 4, :]
                nc.scalar.activation(dst, buf[:, b % 2, 0:n], ACT.Silu).then_inc(silu.sem, 1)

        @block.vector
        def _(dve):
            chain = Chain(dve, K.dve_chain)
            K.split_fresh_low(dve)
            for b in range(8):
                if b % 2 == 0:
                    K.split_low(dve, first + b // 2 + 1)
                dve.wait_ge(tap.sem, tap.base + b + 1)
                ps = K.pairs[b % 4]
                for a, e in parts_of(b):
                    chain.step(nc.vector.scalar_tensor_tensor(
                        buf[:, b % 2, a + 1:e], ps[:, a:e - 1], K.vec[:, cw + b:cw + b + 1],
                        buf[:, b % 2, a + 1:e], ALU.mult, ALU.add))
                chain.sync()
                for a, e in parts_of(b):
                    op = nc.vector.scalar_tensor_tensor(
                        buf[:, b % 2, a:e - 1], ps[:, a + 1:e], K.vec[:, cw + 16 + b:cw + 17 + b],
                        buf[:, b % 2, a:e - 1], ALU.mult, ALU.add)
                op.then_inc(conved.sem, 1)
            chain.close()
    for c in (done, tap, silu, conved):
        c.base += 8


def mlstm_stage(K, qT, kT, keysT, floorT, top, val, sig, yT):
    nc = K.nc
    spread, scored, summed, turned = K.pe_a, K.pe_b, K.pe_c, K.pe_d
    weighed, rooted = K.act_a, K.act_b
    mixed, read, normed, diag_ready, out_ready = K.dve_a, K.dve_b, K.dve_c, K.dve_d, K.dve_e
    staged = K.pool_a
    order = [4, 5, 0, 1, 2, 3]
    one = lambda ap: ap.rearrange("p o t -> p (o t)")
    beyond = lambda s, d: (0, LAT) if s >= 4 else (((s + 1) * P, LAT) if d == 0 else (0, s * P))
    with ExitStack() as stack:
        sb = lambda name, shape: stack.enter_context(K.temp(name, shape))
        kS, qS, hot = sb("kS", [P, ALL]), sb("qS", [P, 2, LAT]), sb("hot", [64, 4])
        diag = sb("diag", [P, 2, 4, P])
        wgt = sb("wgt", [P, 2, 2, LAT])
        prob = sb("prob", [P, 2, 6, LAT])
        hs = lambda t: K.xT[:, t // 2, LAT + P * (t % 2):LAT + P * (t % 2) + P]
        hn, junk = sb("hn", [P, 4, P]), sb("junk", [P, P])[:]
        den, ss = sb("den", [P, 2, 2]), sb("ss", [P, 4])
        causal = sb("causal", [P, 2, P])
        block = stack.enter_context(nc.Block())

        @block.sync
        def _(sp):
            sp.dma_start(causal[:], K.d["causal"]).then_inc(K.loaded.sem, 16)

        @block.gpsimd
        def _(pool):
            pool.sem_inc(scored.sem, 1)
            chain = Chain(pool, K.pool_chain)
            for b in range(2):
                chain.step(nc.gpsimd.memset(qS[64 - 64 * b:128 - 64 * b, b, :], 0.0))
                chain.sync()
            with chain.loop(4, 4) as i:
                pool.wait_ge(scored.sem, i * 12 + (scored.base + 1))
                chain.step(nc.gpsimd.tensor_copy(kS[:], one(kT[:, bass.ds(i, 1), :])))
                for b in range(2):
                    r = slice(64 * b, 64 * b + 64)
                    chain.sync()
                    chain.step(nc.gpsimd.tensor_copy(qS[r, b, :], one(qT[r, bass.ds(i, 1), :])))
                chain.sync()
                chain.step(nc.gpsimd.tensor_copy(hot[:, 0:2], K.ident[0:64, bass.ds(i * 2, 2)]))
                chain.sync()
                nc.gpsimd.tensor_copy(hot[:, 2:4], K.ident[0:64, bass.ds(i * 2 + 32, 2)]).then_inc(staged.sem, 1)
            chain.close()

        @block.tensor
        def _(pe):
            with pe.Fori(0, 4) as i:
                pe.wait_ge(staged.sem, i + (staged.base + 1))
                for b in range(2):
                    for d in range(2):
                        mm = nc.tensor.matmul(K.pairs[2][:, d * 512:d * 512 + LAT],
                                              hot[:, 2 * d + b:2 * d + b + 1].broadcast_to([64, P]), top[:],
                                              start=True, stop=True)
                    mm.then_inc(spread.sem, 1)
                    for j, s in enumerate(order):
                        pe.wait_ge(mixed.sem, i * 12 + (mixed.base + 6 * b + j + 1))
                        nc.tensor.matmul(K.pairs[0][:, 512 * (j % 2):512 * (j % 2) + LAT], kS[:, s * P:s * P + P],
                                         qS[:, b, :], start=True, stop=True).then_inc(scored.sem, 1)
                    pe.wait_ge(mixed.sem, i * 12 + (mixed.base + 6 * b + 8))
                    for j in range(4):
                        d, half = j % 2, j // 2
                        pe.wait_ge(read.sem, i * 8 + (read.base + 4 * b + j + 1))
                        for u in range(2):
                            t = 2 * half + u
                            keys = [4, 5] + (list(range(t + 1)) if d == 0 else list(range(t, 4)))
                            for n, s in enumerate(keys):
                                mm = nc.tensor.matmul(
                                    K.pairs[3][:, 512 * d + u * 129:512 * d + u * 129 + 129],
                                    prob[:, d, s, t * P:t * P + P], one(val[:, s, bass.ds(i * 2 + b, 1), :]),
                                    start=n == 0, stop=n == len(keys) - 1)
                        mm.then_inc(summed.sem, 1)
                    pe.wait_ge(normed.sem, i * 2 + (normed.base + b + 1))
                    for t in range(4):
                        mm = nc.tensor.transpose(K.pairs[1][:, t * P:t * P + P], hn[:, t, :], K.ident[:])
                    mm.then_inc(turned.sem, 1)

        @block.scalar
        def _(act):
            with act.Fori(0, 4) as i:
                for b in range(2):
                    act.wait_ge(diag_ready.sem, i * 2 + (diag_ready.base + b + 1))
                    flat = diag[:].rearrange("p d s t -> p (d s t)")
                    nc.scalar.activation(flat, flat, ACT.Exp, scale=-1.0)
                    for j, s in enumerate(order):
                        act.wait_ge(mixed.sem, i * 12 + (mixed.base + 6 * b + j + 1))
                        for d in range(2):
                            lo, hi = beyond(s, d)
                            if hi > lo:
                                op = nc.scalar.activation(wgt[:, j % 2, d, lo:hi], K.pairs[2][:, 512 * d + lo:512 * d + hi],
                                                          ACT.Exp, bias=one(keysT[:, s:s + 1, bass.ds(i * 2 + (32 * d + b), 1)]),
                                                          scale=-1.0)
                        op.then_inc(weighed.sem, 1)
                    act.wait_ge(read.sem, i * 8 + (read.base + 4 * b + 6))
                    for t in range(4):
                        nc.scalar.activation(junk, hs(t), ACT.Square, accum_out=ss[:, t:t + 1]).then_inc(K.act_c.sem, 1)
                        act.wait_ge(K.act_c.sem, i * 8 + (K.act_c.base + 4 * b + t + 1))
                    nc.scalar.activation(ss[:], ss[:], ACT.Sqrt, bias=K.eps[:], scale=1.0 / P).then_inc(rooted.sem, 1)

        @block.vector
        def _(dve):
            dve.sem_inc(mixed.sem, 2)
            dve.sem_inc(read.sem, 2)
            chain = Chain(dve, K.dve_chain)
            dve.wait_ge(K.loaded.sem, K.loaded.base + 16)
            with chain.loop(4, 2 * (3 * 4 + 1 + 3 + 1)) as i:
                for b in range(2):
                    dve.wait_ge(spread.sem, i * 2 + (spread.base + b + 1))
                    for d in range(2):
                        for s in range(4):
                            op = nc.vector.scalar_tensor_tensor(
                                diag[:, d, s, :], K.pairs[2][:, 512 * d + s * P:512 * d + s * P + P],
                                one(keysT[:, s:s + 1, bass.ds(i * 2 + (32 * d + b), 1)]), causal[:, d, :],
                                ALU.subtract, ALU.max)
                    op.then_inc(diag_ready.sem, 1)
                    for j, s in enumerate(order):
                        dve.wait_ge(scored.sem, i * 12 + (scored.base + 6 * b + j + 2))
                        dve.wait_ge(weighed.sem, i * 12 + (weighed.base + 6 * b + j + 1))
                        bank = 512 * (j % 2)
                        for d in range(2):
                            lo, hi = beyond(s, d)
                            if s < 4:
                                op = nc.vector.scalar_tensor_tensor(
                                    prob[:, d, s, s * P:s * P + P], K.pairs[0][:, bank + s * P:bank + s * P + P], 0.125,
                                    diag[:, d, s, :], ALU.mult, ALU.mult)
                            if hi > lo:
                                op = nc.vector.scalar_tensor_tensor(
                                    prob[:, d, s, lo:hi], K.pairs[0][:, bank + lo:bank + hi], 0.125,
                                    wgt[:, j % 2, d, lo:hi], ALU.mult, ALU.mult)
                        op.then_inc(mixed.sem, 1)
                    for j in range(4):
                        d, half = j % 2, j // 2
                        dve.wait_ge(summed.sem, i * 8 + (summed.base + 4 * b + j + 1))
                        ps = K.pairs[3][:, 512 * d:512 * d + 258].rearrange("p (u c) -> p u c", u=2)
                        total = ps[:, :, 128:129].rearrange("p u c -> p (u c)")
                        chain.step(nc.vector.scalar_tensor_tensor(
                            den[:, d, :], total, -1.0,
                            floorT[:, 2 * half:2 * half + 2, bass.ds(i * 2 + (32 * d + b), 1)].rearrange("p u c -> p (u c)"),
                            ALU.mult, ALU.max))
                        chain.sync()
                        chain.step(nc.vector.scalar_tensor_tensor(den[:, d, :], total, 1.0, den[:, d, :], ALU.mult, ALU.max))
                        chain.sync()
                        chain.step(nc.vector.reciprocal(den[:, d, :], den[:, d, :]))
                        chain.sync()
                        for u in range(2):
                            t = 2 * half + u
                            if d == 0:
                                op = nc.vector.tensor_scalar(hs(t), ps[:, u, 0:P], den[:, d, u:u + 1], None, ALU.mult)
                            else:
                                op = nc.vector.scalar_tensor_tensor(hs(t), ps[:, u, 0:P], den[:, d, u:u + 1],
                                                                    hs(t), ALU.mult, ALU.add)
                        op.then_inc(read.sem, 1)
                        if d == 0:
                            dve.wait_ge(read.sem, i * 8 + (read.base + 4 * b + j + 3))
                    dve.wait_ge(rooted.sem, i * 2 + (rooted.base + b + 1))
                    chain.step(nc.vector.reciprocal(ss[:], ss[:]))
                    chain.sync()
                    for t in range(4):
                        op = nc.vector.tensor_scalar(hn[:, t, :], hs(t), ss[:, t:t + 1], None, ALU.mult)
                        if t < 3:
                            chain.step(op)
                    op.then_inc(normed.sem, 1)
                    dve.wait_ge(turned.sem, i * 2 + (turned.base + b + 1))
                    head = bass.ds(i * 2 + b, 1)
                    chain.step(nc.vector.scalar_tensor_tensor(
                        one(yT[:, head, 0:LAT]), K.pairs[1][:, 0:LAT], K.vec[:, bass.ds(i * 2 + (VEC["out_g"][0] + b), 1)],
                        one(sig[:, head, :]), ALU.mult, ALU.mult))
                    chain.sync()
            chain.close()
    K.loaded.base += 16
    for c, n in ((spread, 8), (scored, 49), (summed, 32), (turned, 8), (weighed, 48), (rooted, 8), (K.act_c, 32),
                 (mixed, 50), (read, 34), (normed, 8), (diag_ready, 8), (staged, 4)):
        c.base += n


def mix1(K):
    nc = K.nc
    with ExitStack() as outer:
        sb = lambda name, shape: outer.enter_context(K.temp(name, shape))
        keysT, floorT, top = sb("keysT", [P, 6, 64]), sb("floorT", [P, 4, 64]), sb("top", [64, LAT])
        qT, kT, sig = sb("qT", [P, 4, LAT]), sb("kT", [P, 4, ALL]), sb("sig", [P, 8, LAT])
        val = sb("val", [P, 6, 8, 129])
        with K.split_weights(), K.activations(ALL):
            with K.arena(val):
                ada_stage(K, 1)
                y = sig[:].rearrange("p k t -> p (k t)")[:, 0:3 * ALL].rearrange("p (k t) -> p k t", k=3)
                gate_stage(K, keysT, floorT, top, Norm(K, ALL, K.v("norm1_1", 0, 8), 1, 0, y))
                conv_qk_stage(K, qT, kT)
            project_stage(K, ["w_ml_o"], LAT, 8, lambda b: ("act", lambda act, ps: nc.scalar.activation(
                sig[:, b, :], ps[:, 0:LAT], ACT.Sigmoid)))
            g = K.first("w_ml_v")
            token_major_stage(K, ["w_ml_v"], [
                (g + c, t == 5, K.token_products(g + c, t, 256), 256, val[:, t, 2 * c:2 * c + 2, 0:128])
                for c in range(4) for t in range(6)],
                ones=val[:].rearrange("p t h c -> p (t h) c")[:, :, 128:129], ahead=False)
        with K.temp("yT", [P, KD, LAT]) as yT:
            mlstm_stage(K, qT, kT, keysT, floorT, top, val, sig, yT)
            with K.split_weights(), K.activations(LAT), K.arena(val):
                residual_split_stage(K, "w_ml_out", K.h_high, K.h_low, KD, 2, LAT, 2, raw=lambda k: yT[:, k, :],
                                     ahead=False)


def layer1(K):
    mix1(K)
    ffn(K, 1, LAT, 5, K.v("norm2_1", 0, 8), scale=4, shift=3)



TOPK = 128
TAKEN = -3e38


def index_scores_stage(K, iqT, ikT, iw, pen, rel):
    nc = K.nc
    dots, relus, added = K.pe_a, K.act_a, K.dve_a
    jobs = [(t, h) for t in range(1, 4) for h in range(4)]
    with K.temp("rl", [P, 2, LAT]) as rl, nc.Block() as block:
        @block.sync
        def _(sp):
            sp.dma_start(rel[:], K.d["rel"]).then_inc(K.loaded.sem, 16)

        @block.tensor
        def _(pe):
            for j, (t, h) in enumerate(jobs):
                if j >= 4:
                    pe.wait_ge(relus.sem, relus.base + j - 3)
                nc.tensor.matmul(K.pairs[j % 4][:, 0:P * (t + 1)], iqT[:, h, t * P:t * P + P],
                                 ikT[:, 0:P * (t + 1)], start=True, stop=True).then_inc(dots.sem, 1)

        @block.scalar
        def _(act):
            for j, (t, h) in enumerate(jobs):
                act.wait_ge(dots.sem, dots.base + j + 1)
                if j >= 2:
                    act.wait_ge(added.sem, added.base + j - 1)
                nc.scalar.activation(rl[:, j % 2, 0:P * (t + 1)], K.pairs[j % 4][:, 0:P * (t + 1)],
                                     ACT.Relu).then_inc(relus.sem, 1)

        @block.vector
        def _(dve):
            chain = Chain(dve, K.dve_chain)
            flat = iw[:].rearrange("p t h -> p (t h)")
            chain.step(nc.vector.tensor_scalar(flat, flat, 4.0 ** -0.5 * 64.0 ** -0.5, None, ALU.mult))
            chain.step(nc.vector.memset(pen[:, 0, 0:P], 0.0))
            chain.sync()
            chain.step(nc.vector.memset(pen[0:64, 0, 64:P], -BIG))
            for j, (t, h) in enumerate(jobs):
                nk = P * (t + 1)
                score = pen[:, t, :]
                dve.wait_ge(relus.sem, relus.base + j + 1)
                chain.sync()
                w = iw[:, t, h:h + 1]
                if h == 0:
                    nc.vector.tensor_scalar(score[:, 0:nk], rl[:, j % 2, 0:nk], w, None, ALU.mult).then_inc(added.sem, 1)
                else:
                    nc.vector.scalar_tensor_tensor(score[:, 0:nk], rl[:, j % 2, 0:nk], w, score[:, 0:nk],
                                                   ALU.mult, ALU.add).then_inc(added.sem, 1)
                dve.wait_ge(added.sem, added.base + j + 1)
                if h == 3:
                    chain.step(nc.vector.memset(score[0:64, nk - 64:nk], -BIG))
            dve.wait_ge(K.loaded.sem, K.loaded.base + 16)
            nc.vector.memset(rel[0:64, :, LAT - 64:LAT], -BIG)
            chain.close()
    K.loaded.base += 16
    for c in (dots, relus, added):
        c.base += len(jobs)


def select_keys(K, dve, chain, pen, best):
    nc = K.nc
    for t in range(1, 4):
        nk = P * (t + 1)
        score = pen[:, t, 0:nk]
        for _ in range(TOPK // 8):
            chain.step(nc.vector.max(best[:], score))
            chain.sync()
            chain.step(nc.vector.match_replace(score, best[:], score, TAKEN))
            chain.sync()
        chain.step(nc.vector.tensor_scalar(score, score, TAKEN / 2, -BIG, ALU.is_gt, ALU.mult))


def lru_stage(K, cx, cy, yc):
    nc = K.nc
    g = K.first("w2_lru")
    w = K.slot(g, 8, P)
    with ExitStack() as stack:
        sb = lambda name, shape: stack.enter_context(K.temp(name, shape))
        u, rec, inp, dec, th = (sb(n, [P, 4, LAT]) for n in ("u", "rec", "inp", "dec", "th"))
        ge = sb("ge", [P, 4, LAT])[:]
        soft, rate = sb("soft", [P, 4]), sb("rate", [P, 2, 4])
        block = stack.enter_context(nc.Block())

        @block.sync
        def _(sp):
            K.stream(sp, ["w2_lru"])

        @block.tensor
        def _(pe):
            K.wait_weights(pe, g)
            for t in range(4):
                pe.wait_ge(K.dve_a.sem, K.dve_a.base + t + 1)
                for m in range(2):
                    mm = nc.tensor.matmul(K.pairs[t][:, 512 * m:512 * m + LAT], w[:, 4 * m + t, :], u[:, t, :],
                                          start=True, stop=True)
                mm.then_inc(K.pe_a.sem, 1)
            pe.wait_ge(K.pe_a.sem, K.pe_a.base + 4)
            pe.sem_inc(K.w_used.sem, 1)

        @block.scalar
        def _(act):
            chain = Chain(act, K.act_chain)
            chain.step(nc.scalar.activation(soft[:], K.v("lam", 0, 4), ACT.Abs))
            chain.sync()
            chain.step(nc.scalar.activation(soft[:], soft[:], ACT.Exp, scale=-1.0))
            chain.sync()
            nc.scalar.activation(soft[:], soft[:], ACT.Ln, bias=K.ones[:, 0:1]).then_inc(K.act_a.sem, 1)
            for t in range(4):
                act.wait_ge(K.pe_a.sem, K.pe_a.base + t + 1)
                nc.scalar.activation(rec[:, t, :], K.pairs[t][:, 0:LAT], ACT.Sigmoid, bias=K.v("ba", t))
                chain.step(nc.scalar.activation(inp[:, t, :], K.pairs[t][:, 512:512 + LAT], ACT.Sigmoid, bias=K.v("bx", t)))
            act.wait_ge(K.pool_a.sem, K.pool_a.base + 1)
            nc.scalar.activation(ge, ge, ACT.Sigmoid, scale=2 * 0.7978845608028654).then_inc(K.act_c.sem, 1)
            chain.sync()
            act.wait_ge(K.dve_b.sem, K.dve_b.base + 1)
            for t in range(4):
                op = nc.scalar.activation(th[:, t, :], rec[:, t, :], ACT.Tanh, scale=rate[:, 0, t:t + 1])
            for t in range(4):
                op = nc.scalar.activation(dec[:, t, :], rec[:, t, :], ACT.Exp, scale=rate[:, 1, t:t + 1])
            op.then_inc(K.act_b.sem, 1)
            act.wait_ge(K.dve_c.sem, K.dve_c.base + 1)
            nc.scalar.activation(th[:], th[:], ACT.Sqrt).then_inc(K.act_b.sem, 1)
            chain.close()

        @block.gpsimd
        def _(pool):
            chain = Chain(pool, K.pool_chain)
            chain.step(nc.gpsimd.tensor_tensor(ge, cy, cy, ALU.mult))
            chain.sync()
            chain.step(nc.gpsimd.tensor_scalar(ge, ge, 0.044715, 1.0, ALU.mult, ALU.add))
            chain.sync()
            nc.gpsimd.tensor_tensor(ge, ge, cy, ALU.mult).then_inc(K.pool_a.sem, 1)
            pool.wait_ge(K.act_c.sem, K.act_c.base + 1)
            nc.gpsimd.tensor_tensor(ge, ge, cy, ALU.mult).then_inc(K.pool_a.sem, 1)
            chain.close()

        @block.vector
        def _(dve):
            chain = Chain(dve, K.dve_chain)
            tap = lambda j, t: K.v("ccw", 4 * j + t)
            for t in range(4):
                chain.step(nc.vector.tensor_scalar(u[:, t, :], cx[:, t, :], tap(3, t), K.v("ccb", t), ALU.mult, ALU.add))
                for back in range(1, 4):
                    chain.sync()
                    op = nc.vector.scalar_tensor_tensor(u[:, t, back:], cx[:, t, 0:LAT - back], tap(3 - back, t),
                                                        u[:, t, back:], ALU.mult, ALU.add)
                    if back < 3:
                        chain.step(op)
                op.then_inc(K.dve_a.sem, 1)
            dve.wait_ge(K.act_a.sem, K.act_a.base + 1)
            chain.step(nc.vector.tensor_scalar(rate[:, 0, :], K.v("lam", 0, 4), -1.0, 0.0, ALU.mult, ALU.max))
            chain.sync()
            chain.step(nc.vector.tensor_tensor(rate[:, 0, :], rate[:, 0, :], soft[:], ALU.add))
            chain.sync()
            chain.step(nc.vector.tensor_scalar(rate[:, 1, :], rate[:, 0, :], -8.0, None, ALU.mult))
            chain.sync()
            nc.vector.tensor_scalar(rate[:, 0, :], rate[:, 0, :], 8.0, None, ALU.mult).then_inc(K.dve_b.sem, 1)
            dve.wait_ge(K.act_b.sem, K.act_b.base + 1)
            chain.step(nc.vector.tensor_tensor(rec[:], dec[:], dec[:], ALU.mult))
            chain.sync()
            nc.vector.scalar_tensor_tensor(th[:], rec[:], 1.0, th[:], ALU.add, ALU.mult).then_inc(K.dve_c.sem, 1)
            chain.step(nc.vector.tensor_tensor(inp[:], inp[:], u[:], ALU.mult))
            chain.sync()
            dve.wait_ge(K.act_b.sem, K.act_b.base + 2)
            chain.step(nc.vector.tensor_tensor(inp[:], inp[:], th[:], ALU.mult))
            chain.sync()
            for t in range(4):
                chain.step(nc.vector.tensor_tensor_scan(u[:, t, :], dec[:, t, :], inp[:, t, :], 0.0, ALU.mult, ALU.add))
            chain.sync()
            dve.wait_ge(K.pool_a.sem, K.pool_a.base + 2)
            nc.vector.tensor_tensor(yc, u[:], ge, ALU.mult)
            chain.close()
    for c, n in ((K.dve_a, 4), (K.pe_a, 4), (K.act_a, 1), (K.act_b, 2), (K.act_c, 1), (K.dve_b, 1), (K.dve_c, 1),
                 (K.pool_a, 2)):
        c.base += n


def merge_stage(K, branch_tile, high, low, merged):
    nc = K.nc
    first = K.first("w2_merge")
    multiplied, gated, summed = K.pe_a, K.act_a, K.dve_a
    high_ready, low_ready = K.act_c, K.dve_b
    K.begin_split(["w2_merge"])
    bank = lambda c: K.pairs[c // 2][:, 512 * (c % 2):512 * (c % 2) + LAT]
    with ExitStack() as stack:
        sb = lambda name, shape: stack.enter_context(K.temp(name, shape))
        sg, part = sb("sg", [P, 3, LAT]), sb("part", [P, LAT])
        block = stack.enter_context(nc.Block())

        @block.sync
        def _(sp):
            K.stream(sp, ["w2_merge"])

        @block.tensor
        def _(pe):
            def gate_product(i, g, half, branch):
                return K.product(pe, bank(branch), g, KD, 256, half, K.h_high, K.h_low, LAT, i)

            with pe.Fori(0, 4) as i:
                for b in range(2):
                    for c in range(2):
                        g = first + 2 * b + c
                        w_high, w_low = K.parts(g, KD, 256)
                        for half in range(2):
                            branch = 2 * c + half
                            if branch < 3:
                                pe.wait_ge(gated.sem, i * 6 + (gated.base + 3 * b + branch + 1))
                                gate_product(i, g, half, branch).then_inc(multiplied.sem, 1)
                            else:
                                pe.wait_ge(summed.sem, i * 2 + (summed.base + b + 1))
                                pe.wait_ge(low_ready.sem, low_ready.base + KD)
                                for y, ks in enumerate(((0, 1), (2, 3), (4, 5, 6, 7))):
                                    for k in ks:
                                        for n, (w, x) in enumerate(((w_high, high), (w_high, low), (w_low, high))):
                                            mm = nc.tensor.matmul(bank(4 + y), w[:, k, P:2 * P], x[:, k, :],
                                                                  start=k == ks[0] and n == 0,
                                                                  stop=k == ks[-1] and n == 2)
                                    mm.then_inc(multiplied.sem, 1)

        @block.scalar
        def _(act):
            act.sem_inc(gated.sem, 3)
            K.split_fresh_high(act)
            for k in range(KD):
                nc.scalar.activation(high[:, k, :], branch_tile(k), ACT.Copy).then_inc(high_ready.sem, 1)
            with act.Fori(0, 4) as i:
                for b in range(2):
                    act.wait_ge(multiplied.sem, i * 12 + (multiplied.base + 6 * b))
                    K.split_high(act, first + 2 * b + 1, i)
                    act.wait_ge(summed.sem, i * 2 + (summed.base + b + 1))
                    for c in range(3):
                        act.wait_ge(multiplied.sem, i * 12 + (multiplied.base + 6 * b + c + 1))
                        nc.scalar.activation(sg[:, c, :], bank(c), ACT.Sigmoid, bias=K.vec[
                            :, bass.ds(i * 2 + (VEC["b_gate"][0] + 8 * c + b), 1)]).then_inc(gated.sem, 1)
                        if c == 1:
                            K.split_high(act, first + 2 * b + 2, i)

        @block.vector
        def _(dve):
            dve.sem_inc(summed.sem, 1)
            chain = Chain(dve, K.dve_chain)
            K.split_fresh_low(dve)
            for k in range(KD):
                dve.wait_ge(high_ready.sem, high_ready.base + k + 1)
                nc.vector.tensor_tensor(low[:, k, :], branch_tile(k), high[:, k, :].bitcast(F32),
                                        ALU.subtract).then_inc(low_ready.sem, 1)
            dve.wait_ge(low_ready.sem, low_ready.base + KD)
            with chain.loop(4, 8) as i:
                for b in range(2):
                    K.split_low(dve, first + 2 * b + 1, i)
                    K.split_low(dve, first + 2 * b + 2, i)
                    out = merged[:, bass.ds(i * 2 + b, 1), :].rearrange("p o t -> p (o t)")
                    dve.wait_ge(gated.sem, i * 6 + (gated.base + 3 * b + 6))
                    for c in range(3):
                        dve.wait_ge(multiplied.sem, i * 12 + (multiplied.base + 6 * b + c + 4))
                        to = out if c == 0 else part[:]
                        chain.step(nc.vector.tensor_tensor(to, sg[:, c, :], bank(4 + c), ALU.mult))
                        chain.sync()
                        if c > 0:
                            op = nc.vector.tensor_tensor(out, out, part[:], ALU.add)
                            if c == 1:
                                chain.step(op)
                                chain.sync()
                            else:
                                op.then_inc(summed.sem, 1)
            chain.close()
    multiplied.base += 48
    high_ready.base += KD
    low_ready.base += KD
    gated.base += 27
    summed.base += 9


def mix2(K):
    nc = K.nc
    with K.activations(LAT), ExitStack() as outer:
        sb = lambda name, shape: outer.enter_context(K.temp(name, shape))
        hd = sb("hd", [P, 11, LAT])
        iw, cc = sb("iw", [P, 4, 4]), sb("cc", [P, KD, LAT])

        def val(t, col, n):
            return K.xT[:, 2 * t + col // 256, LAT + col % 256:LAT + col % 256 + n]
        first = K.first("w2_heads")
        kinds = [(K.qgain[:, 2:3], False), (K.v("ak_g"), False), (K.qgain[:, 3:4], True), (K.v("bk_g"), True),
                 (None, True), (K.v("ik_g"), True)]
        with ExitStack() as inner:
            sb_in = lambda name, shape: inner.enter_context(K.temp(name, shape))
            qpad = sb_in("qpad", [P, 12, LAT])
            pen, rel = sb_in("pen", [P, 4, LAT]), sb_in("rel", [P, 4, LAT])
            best = sb_in("best", [P, 8])
            mix = qpad[:, 8:12, :]

            def pad(pool):
                chain = Chain(pool, K.pool_chain)
                for b in range(2):
                    chain.step(nc.gpsimd.memset(qpad[64 - 64 * b:128 - 64 * b, b::2, :], 0.0))
                    chain.sync()
                    for n, tile in enumerate((0, 4, 8)):
                        r = slice(64 * b, 64 * b + 64)
                        chain.step(nc.gpsimd.tensor_copy(qpad[r, 4 * n + b:4 * n + b + 3:2, :], hd[r, tile:tile + 2, :]))
                        chain.sync()
                chain.close()
            with K.split_weights():
                with K.arena(qpad):
                    tiles = []
                    for b in range(11):
                        gain, rope = kinds[b // 2]
                        tiles.append(dict(
                            chunk=first + b // 2, rows=P, sums=K.ones64[:], scale=1 / 64, rope=rope, gain=gain,
                            dst=hd[:, b, :], mms=K.feature_products(first + b // 2, b % 2)))
                    heads_stage(K, ["w2_heads"], tiles, LAT, "trig_seq", "rot_seq",
                                norm=Norm(K, LAT, K.v("g_mix", 0, 8), None, None, cc[:, 0:3, :]))
                g, gw = K.first("w2_v"), K.first("w2_iw")
                jobs = [(g + c, t == 3, K.token_products(g + c, t, 256), 256, val(t, 256 * c, 256))
                        for c in range(2) for t in range(4)]
                jobs += [(gw, t == 3, K.token_products(gw, t, 4), 4, iw[:, t, :]) for t in range(4)]
                token_major_stage(K, ["w2_v", "w2_iw"], jobs, on_pool=pad)
                with K.arena(cc):
                    index_scores_stage(K, qpad[:, 8:12, :], hd[:, 10, :], iw, pen, rel)
                project_stage(K, ["w2_c"], LAT, 8, lambda b: ("act", lambda act, ps: nc.scalar.activation(
                    cc[:, b, :], ps[:, 0:LAT], ACT.Copy)), beside=lambda dve, chain: select_keys(K, dve, chain, pen, best))

            def steps(_):
                out = []
                for t in range(4):
                    nk = P * (t + 1)
                    for h in range(8):
                        kind, hh = h // 4, h % 4
                        out.append(dict(
                            q=qpad[:, h, t * P:t * P + P], keys=[(0, hd[:, 4 * kind + 2 + hh // 2, 0:nk])], nk=nk,
                            bias=rel[:, hh, LAT - nk:LAT] if kind == 0 else pen[:, t, 0:nk],
                            v=[val(c, 128 * (h // 2), 128) for c in range(t + 1)],
                            col=lambda at, h=h: slice(at + 64 * (h % 2), at + 64 * (h % 2) + 64),
                            out=mix[:, t, 64 * h:64 * h + 64]))
                return out
            attention_stage(K, 1, steps)
            untoken_stage(K, mix, hd, 4, 4)
        lru_stage(K, cc[:, 0:4, :], cc[:, 4:8, :], cc[:, 0:4, :])
        with K.split_weights(), K.temp("high", [P, KD, LAT], F32R) as high, K.temp("low", [P, KD, LAT], F32R) as low:
            merge_stage(K, lambda k: hd[:, k, :] if k < 4 else cc[:, k - 4, :], high, low, cc)
            residual_split_stage(K, "w2_out", high, low, KD, 2, LAT, None, raw=lambda k: cc[:, k, :], ahead=False)


def layer2(K):
    mix2(K)
    ffn(K, 2, LAT, None, K.v("g_ffn", 0, 8))


def store_stage(K, tokens=LAT):
    with K.nc.Block() as block:
        @block.sync
        def _(sp):
            sp.dma_start(K.d["out"], K.xT[:, :, 0:tokens]).then_inc(K.stored.sem, 16)
            sp.wait_ge(K.stored.sem, 16)

def build(nc, arrays):
    with ExitStack() as stack:
        K = Kernel(nc, arrays, stack)
        load_stage(K)
        layer0(K)
        layer1(K)
        layer2(K)
        store_stage(K)


def lay_out(inp):
    a = {k: np.asarray(v) for k, v in inp.items()}
    out = {}

    def pack(w, cols):
        k, n = w.shape
        return np.ascontiguousarray(w.reshape(k // P, P, n // cols, cols).transpose(2, 1, 0, 3)).reshape(
            n // cols, P, -1)

    def pair(left, right):
        k, n = left.shape
        both = np.stack([left.reshape(k, n // P, P), right.reshape(k, n // P, P)], 2)
        return pack(both.reshape(k, 2 * n), 256)

    def put_ffn(layer, up, down):
        at = 0
        for part, kt in enumerate(HIDDEN_PARTS[layer]):
            hidden = slice(at * P, (at + kt) * P)
            at += kt
            out[f"w_up{layer}_{part}"] = pair(up[:, :D_FF][:, hidden], up[:, D_FF:][:, hidden])
            out[f"w_down{layer}_{part}"] = pack(down[hidden], down_blocks(kt) * P)

    zeros = lambda *shape: np.zeros(shape, np.float32)
    for layer in range(2):
        out[f"w_ada{layer}"] = pack(a["ada_w"][layer], 256)
        up = a["ffn_w_up"][layer]
        put_ffn(layer, up, a["ffn_w_down"][layer])
    w = a["att_w_in"][0]
    cq, ckv, kr, gq, gk, gv = np.split(w, np.cumsum([384, 256, 32, 512, 128])[:5], axis=1)
    out["w_att_lo"] = pack(np.concatenate([cq, ckv, zeros(D, 64), kr, zeros(D, 32)], 1), 256)
    out["w_att_gqa"] = pack(np.concatenate([gq, gk[:, :64], gk[:, :64], gk[:, 64:], gk[:, 64:]], 1), 256)
    out["w_gv"] = pack(gv, P)
    out["w_qb"] = pack(a["mla_w_qb"][0], 384)
    kvb = a["mla_w_kvb"][0].reshape(256, 8, 128)
    out["w_kvb"] = pack(np.concatenate([kvb[:, :, :64], zeros(256, 8, 32)], 2).reshape(256, 768), 768)
    out["w_va"] = pack(kvb[:, :, 64:].reshape(256, 512), 512)
    out["w_att_out"] = pack(a["att_w_out"][0], 256)

    w = a["ml_w_in"][0]
    g = w[:, 3072:3104]
    gates = zeros(D, P)
    gate_i, gate_f = zeros(P), zeros(P)
    gb = a["ml_gate_b"][0]
    for d in range(2):
        gates[:, 32 * d:32 * d + 8] = g[:, 16 * d:16 * d + 8]
        gates[:, 64 + 32 * d:72 + 32 * d] = g[:, 16 * d + 8:16 * d + 16]
        gate_i[32 * d:32 * d + 8] = gb[16 * d:16 * d + 8]
        gate_f[32 * d:32 * d + 8] = gb[16 * d + 8:16 * d + 16]
    out["w_ml_gate"] = pack(gates, P)
    out["w_ml_qk"] = pack(w[:, :1024], 256)
    out["w_ml_v"] = pack(w[:, 1024:2048], 256)
    out["w_ml_o"] = pack(w[:, 2048:3072], 256)
    out["w_ml_out"] = pack(a["ml_w_out"][0], 256)

    w = a["w_in_2"][0]
    cuts = np.cumsum([256] * 6 + [256, 64, 4, 512, 512])
    aq, ak, av, bq, bk, bv, iq, ik, iw, cx, cy, gt = np.split(w, cuts, axis=1)
    out["w2_heads"] = pack(np.concatenate([aq, ak, bq, bk, iq, ik, ik, zeros(D, P)], 1), 256)
    out["w2_c"] = pack(np.concatenate([cx, cy], 1), 256)
    out["w2_v"] = pack(np.concatenate([av, bv], 1), 256)
    out["w2_iw"] = pack(iw, 4)
    lru = zeros(P, 8, P)
    for m, name in enumerate(("lru_wa_2", "lru_wx_2")):
        for t in range(4):
            for h in range(2):
                lru[64 * h:64 * h + 64, 4 * m + t, 64 * h:64 * h + 64] = a[name][0, 2 * t + h]
    out["w2_lru"] = lru.reshape(1, P, 1024)
    both = np.concatenate([pair(gt[:, :D], gt[:, D:2 * D]), pair(gt[:, 2 * D:], a["w_branch_2"][0])], 1)
    out["w2_merge"] = both.reshape(16, P, 2048)
    out["w2_out"] = pack(a["w_out_2"][0], 256)
    put_ffn(2, a["w_ffn_in_2"][0], a["w_ffn_out_2"][0])

    vec = zeros(P, NVEC)

    def put(name, v):
        at, n = VEC[name]
        v = np.asarray(v, np.float32)
        vec[:, at:at + n] = np.concatenate([v, zeros(n * P - v.size)]).reshape(n, P).T

    for layer in range(2):
        put(f"norm1_{layer}", a["norm1_g"][layer])
        put(f"norm2_{layer}", a["norm2_g"][layer])
        put(f"ada_b{layer}", a["ada_b"][layer])
        put(f"fcw{layer}", a["ffn_conv_w"][layer].ravel())
        put(f"fcb{layer}", a["ffn_conv_b"][layer])
    put("silu_in", np.stack([a["c"][0].reshape(8, P), a["c_ctx"].reshape(8, P)], 1).ravel())
    put("qa_g", a["mla_qa_g"][0])
    put("kva_g", a["mla_kva_g"][0])
    put("mq_g", a["mla_q_g"][0])
    put("mk_g", a["mla_k_g"][0])
    twice = lambda v: np.concatenate([v, v])
    put("gq_g", twice(a["gqa_q_g"][0]))
    put("gk_g", twice(a["gqa_k_g"][0]))
    put("mcw", a["ml_conv_w"][0].ravel())
    put("mcb", a["ml_conv_b"][0])
    put("gate_i", gate_i)
    put("gate_f", gate_f)
    put("out_g", a["ml_out_g"][0].ravel())
    put("g_mix", a["g_mix_2"][0])
    put("g_ffn", a["g_ffn_2"][0])
    put("aq_g", twice(a["qk_gain_a_2"][0, 0]))
    put("ak_g", twice(a["qk_gain_a_2"][0, 1]))
    put("bq_g", twice(a["qk_gain_b_2"][0, 0]))
    put("bk_g", twice(a["qk_gain_b_2"][0, 1]))
    put("ik_g", twice(a["g_idx_k_2"][0]))
    put("ccw", a["conv_w_2"][0].ravel())
    put("ccb", a["conv_b_2"][0])
    put("ba", a["lru_ba_2"][0])
    put("bx", a["lru_bx_2"][0])
    put("lam", a["lru_lambda_2"][0])
    put("b_gate", a["b_gate_2"][0])
    out["vec"] = vec

    tokens = np.concatenate([a["x"][0], a["ctx"][0]], 0)
    out["xT"] = np.ascontiguousarray(tokens.T.reshape(KD, P, ALL).transpose(1, 0, 2))
    rel = a["rel_bias_2"][0]
    n = LAT
    ext = np.concatenate([np.repeat(rel[:, :1], 1024, 1), rel, np.repeat(rel[:, -1:], 1024, 1)], 1)
    flip = ext[:, ::-1]
    out["rel"] = np.ascontiguousarray(np.stack(
        [flip[:, 1152 - 384 - p:1152 - 384 - p + n] for p in range(P)], 0))

    out["ident"] = np.eye(P, dtype=np.float32)
    out["ones64"] = np.kron(np.eye(2), np.ones((64, 64))).astype(np.float32)

    def axial(dim):
        rows = LAT // 64
        row = np.repeat(np.arange(rows), 64).astype(np.float32)
        col = np.tile(np.arange(64), rows).astype(np.float32)
        nf = dim // 4
        inv = (np.float32(10000.0) ** (-np.arange(nf, dtype=np.float32) / nf)).astype(np.float32)
        ar, ac = row[:, None] * inv, col[:, None] * inv
        return np.concatenate([ar, ar, ac, ac], 1)

    def table(ang, rows):
        t = zeros(P, 2, LAT)
        t[:, 0] = 1.0
        for r in rows:
            t[r:r + ang.shape[1], 0] = np.cos(ang).T
            t[r:r + ang.shape[1], 1] = np.sin(ang).T
        return t

    def rotation(q, starts):
        m = zeros(P, P)
        for s in starts:
            for j in range(q):
                m[s + q + j, s + j] = -1.0
                m[s + j, s + q + j] = 1.0
        return m

    out["trig_mla"] = table(axial(32), [64])
    out["trig_gqa"] = table(axial(64), [0, 64])
    out["rot_mla"] = rotation(8, [64, 80])
    out["rot_gqa"] = rotation(16, [0, 32, 64, 96])
    pos = np.arange(LAT, dtype=np.float32)
    inv = (1.0 / (np.float32(10000.0) ** (np.arange(0, 64, 2, dtype=np.float32) / 64))).astype(np.float32)
    ang = pos[:, None] * inv[None]
    out["trig_seq"] = table(np.concatenate([ang, ang], 1), [0, 64])
    out["rot_seq"] = rotation(32, [0, 64])
    s, t = np.arange(P)[:, None], np.arange(P)[None]
    out["causal"] = np.stack([np.where(s <= t, 0, 1e4), np.where(s >= t, 0, 1e4)], 1).astype(np.float32)
    return out


def kernel(**inputs):
    import concourse.bacc as bacc
    from concourse.bass_utils import run_bass_kernel_spmd

    nc = bacc.Bacc("TRN2", target_bir_lowering=False, num_devices=1)
    arrays = lay_out(inputs)
    aps = {name: nc.dram_tensor(f"in_{name}", a.shape, F32, kind="ExternalInput").ap() for name, a in arrays.items()}
    aps["out"] = nc.dram_tensor("out_y", (P, KD, LAT), F32, kind="ExternalOutput").ap()
    build(nc, aps)
    run = run_bass_kernel_spmd(nc, [{f"in_{n}": a for n, a in arrays.items()}], core_ids=[0])
    y = run.results[0]["out_y"]
    return np.ascontiguousarray(y.transpose(2, 1, 0)).reshape(1, LAT, D)
```
